# Optimizing a Trainium2 kernel written in Bass

```python
import math
import jax
import jax.numpy as jnp
from jax import lax
import numpy as np

D_MODEL = 2048
BATCH = 1
SEQ = 256
DEPTH = 2
DEC_BATCH = 8
DEC_SEQ = 1
PAST_LEN = 256
PAGE_SIZE = 128

N_EVEN = (DEPTH + 1) // 2
N_ODD = DEPTH // 2
BLOCK = 128
SB_HEADS = 8
SB_HEAD_DIM = D_MODEL // 16
SB_W = SB_HEADS * SB_HEAD_DIM
SB_BIAS_INIT = -6.0
RET_HEADS = 8
RET_DK = D_MODEL // 16
RET_DV = 2 * RET_DK
RET_QK_W = RET_HEADS * RET_DK
RET_V_W = RET_HEADS * RET_DV
RET_ROPE_BASE = 10000.0
AB_IN = 3 * SB_W + 2 * RET_QK_W + 2 * RET_V_W
AB_OUT = SB_W + RET_V_W
SSM_EXPAND = 2
SSM_D_INNER = SSM_EXPAND * D_MODEL
SSM_HEAD_DIM = 64
SSM_HEADS = SSM_D_INNER // SSM_HEAD_DIM
SSM_GROUPS = 8
SSM_HPG = SSM_HEADS // SSM_GROUPS
SSM_D_STATE = 128
SSM_CONV = 4
SSM_CONV_DIM = SSM_D_INNER + 2 * SSM_GROUPS * SSM_D_STATE
SSM_IN = SSM_D_INNER + SSM_CONV_DIM + SSM_HEADS
D_FF = 11 * D_MODEL // 4
FFN_CONV = 3
LN_EPS = 1e-5
NORM_EPS = 1e-5
DN_ALPHA = (2 * DEPTH) ** 0.25
DN_BETA = (8 * DEPTH) ** -0.25

kernel_name = 'hybrid_stickbreak_retnet_mamba2_convffn_step'

def _chunk_len(length):
    return length if length <= BLOCK else math.gcd(length, BLOCK)

def _layer_norm(x, g, b):
    xf = x.astype(jnp.float32)
    mu = jnp.mean(xf, axis=-1, keepdims=True)
    var = jnp.mean(jnp.square(xf - mu), axis=-1, keepdims=True)
    return ((xf - mu) * lax.rsqrt(var + LN_EPS) * g.astype(jnp.float32) + b.astype(jnp.float32)).astype(x.dtype)

def _rms(x):
    xf = x.astype(jnp.float32)
    return xf * lax.rsqrt(jnp.mean(jnp.square(xf), axis=-1, keepdims=True) + NORM_EPS)

def _causal_dwconv(x, prev, w, b):
    width, length = w.shape[0], x.shape[1]
    xp = jnp.concatenate([prev.astype(x.dtype), x], axis=1)
    out = b + xp[:, 0:length] * w[0]
    for tap in range(1, width):
        out = out + xp[:, tap:tap + length] * w[tap]
    return out, xp[:, length:]

def _rotary(x, pos):
    half = x.shape[-1] // 2
    inv_freq = RET_ROPE_BASE ** (-jnp.linspace(0.0, 1.0, half, dtype=jnp.float32))
    ang = pos.astype(jnp.float32)[:, None] * inv_freq[None, :]
    cos = jnp.cos(ang)[None, :, None, :]
    sin = jnp.sin(ang)[None, :, None, :]
    xf = x.astype(jnp.float32)
    x1, x2 = xf[..., :half], xf[..., half:]
    return jnp.concatenate([x1 * cos - x2 * sin, x1 * sin + x2 * cos], axis=-1)

def _stick_breaking(q, k, v, q_start, bias):
    lq = q.shape[1]
    scale = q.shape[-1] ** -0.5
    bias_f = bias.astype(jnp.float32)[None, :, None, None]
    outs = []
    for i0 in range(0, lq, BLOCK):
        qb = q[:, i0:i0 + BLOCK]
        nq = qb.shape[1]
        nk = q_start + i0 + nq
        kb, vb = k[:, :nk], v[:, :nk]
        z = jnp.einsum('bqhd,bkhd->bhqk', qb, kb).astype(jnp.float32) * scale + bias_f
        qpos = q_start + i0 + jnp.arange(nq)
        kpos = jnp.arange(nk)
        mask = (kpos[None, :] < qpos[:, None])[None, None]
        log_fail = jnp.where(mask, -jax.nn.softplus(z), 0.0)
        later = lax.cumsum(log_fail, axis=3, reverse=True) - log_fail
        w = jnp.where(mask, jnp.exp(jax.nn.log_sigmoid(z) + later), 0.0)
        outs.append(jnp.einsum('bhqk,bkhd->bqhd', w.astype(vb.dtype), vb))
    return jnp.concatenate(outs, axis=1)

def _retention(q, k, v, s0, log_gamma):
    bsz, length, heads, dk = q.shape
    dv = v.shape[-1]
    c = _chunk_len(length)
    n = length // c
    qc = q.reshape(bsz, n, c, heads, dk)
    kc = k.reshape(bsz, n, c, heads, dk)
    vc = v.astype(jnp.float32).reshape(bsz, n, c, heads, dv)
    idx = jnp.arange(c, dtype=jnp.float32)
    gap = idx[:, None] - idx[None, :]
    decay = jnp.where(gap >= 0, jnp.exp(log_gamma[:, None, None] * jnp.maximum(gap, 0.0)), 0.0)
    scores = jnp.einsum('bcihd,bcjhd->bchij', qc, kc) * decay
    out = jnp.einsum('bchij,bcjhe->bcihe', scores, vc)
    to_end = jnp.exp(log_gamma[:, None] * (c - 1.0 - idx)[None, :])
    contrib = jnp.einsum('bcjhd,hj,bcjhe->bchde', kc, to_end, vc)
    chunk_decay = jnp.exp(log_gamma * c)[:, None, None]

    def step(s, ct):
        return s * chunk_decay + ct, s

    s_last, s_start = lax.scan(step, s0.astype(jnp.float32), jnp.moveaxis(contrib, 1, 0))
    s_start = jnp.moveaxis(s_start, 0, 1)
    from_start = jnp.exp(log_gamma[:, None] * (idx + 1.0)[None, :])
    out = out + jnp.einsum('bcihd,hi,bchde->bcihe', qc, from_start, s_start)
    return out.reshape(bsz, length, heads, dv), s_last

def _ssd_scan(x, dt, a, bm, cm, d_skip, h0):
    bsz, length = x.shape[:2]
    c = _chunk_len(length)
    n = length // c
    xf = x.astype(jnp.float32).reshape(bsz, n, c, *x.shape[2:])
    dtc = dt.reshape(bsz, n, c, *dt.shape[2:])
    bc = bm.astype(jnp.float32).reshape(bsz, n, c, *bm.shape[2:])
    cc = cm.astype(jnp.float32).reshape(bsz, n, c, *cm.shape[2:])
    cum = jnp.cumsum(dtc * a, axis=2)
    causal = jnp.tril(jnp.ones((c, c), dtype=bool))[None, None, :, :, None, None]
    seg = cum[:, :, :, None] - cum[:, :, None, :]
    decay = jnp.exp(jnp.where(causal, seg, -jnp.inf))
    cb = jnp.einsum('bcigs,bcjgs->bcijg', cc, bc)
    w = cb[..., None] * decay * dtc[:, :, None]
    y = jnp.einsum('bcijge,bcjgep->bcigep', w, xf)
    to_end = jnp.exp(cum[:, :, -1:] - cum) * dtc
    contrib = jnp.einsum('bcjgs,bcjge,bcjgep->bcgeps', bc, to_end, xf)
    chunk_decay = jnp.exp(cum[:, :, -1])

    def step(h, inp):
        cd, ct = inp
        return h * cd[..., None, None] + ct, h

    h_last, h_start = lax.scan(step, h0.astype(jnp.float32),
                               (jnp.moveaxis(chunk_decay, 1, 0), jnp.moveaxis(contrib, 1, 0)))
    h_start = jnp.moveaxis(h_start, 0, 1)
    y = y + jnp.einsum('bcigs,bcige,bcgeps->bcigep', cc, jnp.exp(cum), h_start)
    y = y + d_skip.astype(jnp.float32)[:, :, None] * xf
    return y.reshape(bsz, length, *x.shape[2:]), h_last

def _ab_mixer(x, pos0, past_k, past_v, ret_s0, w_in, w_out, sb_bias):
    bsz, length, _ = x.shape
    proj = x @ w_in
    cuts = [SB_W, 2 * SB_W, 3 * SB_W, 3 * SB_W + RET_QK_W, 3 * SB_W + 2 * RET_QK_W,
            3 * SB_W + 2 * RET_QK_W + RET_V_W]
    qa, ka, va, qr, kr, vr, gr = jnp.split(proj, cuts, axis=-1)
    qa = qa.reshape(bsz, length, SB_HEADS, SB_HEAD_DIM)
    ka = ka.reshape(bsz, length, SB_HEADS, SB_HEAD_DIM)
    va = va.reshape(bsz, length, SB_HEADS, SB_HEAD_DIM)
    if past_k is None:
        k_all, v_all = ka, va
    else:
        k_all = jnp.concatenate([past_k.astype(ka.dtype), ka], axis=1)
        v_all = jnp.concatenate([past_v.astype(va.dtype), va], axis=1)
    ya = _stick_breaking(qa, k_all, v_all, pos0, sb_bias)
    pos = pos0 + jnp.arange(length)
    log_gamma = jnp.log(1.0 - 2.0 ** (-5.0 - jnp.arange(RET_HEADS, dtype=jnp.float32)))
    qr = _rotary(qr.reshape(bsz, length, RET_HEADS, RET_DK), pos)
    kr = _rotary(kr.reshape(bsz, length, RET_HEADS, RET_DK), pos) * (RET_DK ** -0.5)
    yr, s_new = _retention(qr, kr, vr.reshape(bsz, length, RET_HEADS, RET_DV), ret_s0, log_gamma)
    yr = _rms(yr).reshape(bsz, length, RET_V_W) * jax.nn.silu(gr.astype(jnp.float32))
    merged = jnp.concatenate([ya.reshape(bsz, length, SB_W).astype(x.dtype), yr.astype(x.dtype)], axis=-1)
    return merged @ w_out, ka, va, s_new

def _ssd_mixer(x, h0, conv0, w_in, conv_w, conv_b, dt_bias, a_log, d_skip, norm_w, w_out):
    bsz, length, _ = x.shape
    proj = x @ w_in
    z, xbc, dt_raw = jnp.split(proj, [SSM_D_INNER, SSM_D_INNER + SSM_CONV_DIM], axis=-1)
    xbc, conv_new = _causal_dwconv(xbc, conv0, conv_w, conv_b)
    xbc = jax.nn.silu(xbc)
    xs, bm, cm = jnp.split(xbc, [SSM_D_INNER, SSM_D_INNER + SSM_GROUPS * SSM_D_STATE], axis=-1)
    dt = jax.nn.softplus(dt_raw.astype(jnp.float32) + dt_bias.astype(jnp.float32))
    a = -jnp.exp(a_log.astype(jnp.float32))
    y, h = _ssd_scan(xs.reshape(bsz, length, SSM_GROUPS, SSM_HPG, SSM_HEAD_DIM),
                     dt.reshape(bsz, length, SSM_GROUPS, SSM_HPG),
                     a.reshape(SSM_GROUPS, SSM_HPG),
                     bm.reshape(bsz, length, SSM_GROUPS, SSM_D_STATE),
                     cm.reshape(bsz, length, SSM_GROUPS, SSM_D_STATE),
                     d_skip.reshape(SSM_GROUPS, SSM_HPG),
                     h0.reshape(bsz, SSM_GROUPS, SSM_HPG, SSM_HEAD_DIM, SSM_D_STATE))
    y = y.reshape(bsz, length, SSM_D_INNER) * jax.nn.silu(z.astype(jnp.float32))
    y = _rms(y.reshape(bsz, length, SSM_GROUPS, SSM_D_INNER // SSM_GROUPS)).reshape(bsz, length, SSM_D_INNER)
    y = y * norm_w.astype(jnp.float32)
    return y.astype(x.dtype) @ w_out, h.reshape(bsz, SSM_HEADS, SSM_HEAD_DIM, SSM_D_STATE), conv_new

def _conv_ffn(x, conv0, w_up, conv_w, conv_b, w_down):
    h = x @ w_up
    h, conv_new = _causal_dwconv(h, conv0, conv_w, conv_b)
    g, u = jnp.split(h, 2, axis=-1)
    return (jax.nn.silu(g) * u) @ w_down, conv_new

def _trunk(x, pos0, cache_k, cache_v, page_table, ret0, ssm0, sconv0, fconv0,
           ln1_g, ln1_b, ln2_g, ln2_b, w_in_ab, w_out_ab, sb_bias, w_in_ssd, conv_w_ssd, conv_b_ssd,
           dt_bias, a_log, d_skip, norm_w_ssd, w_out_ssd, w_up, conv_w_ffn, conv_b_ffn, w_down):
    bsz = x.shape[0]
    new_k, new_v, ret_s, ssm_s, ssm_c, ffn_c = [], [], [], [], [], []
    for layer in range(DEPTH):
        idx = layer // 2
        if layer % 2 == 0:
            if cache_k is None:
                pk, pv = None, None
            else:
                pk = jnp.take(cache_k[idx], page_table, axis=0).reshape(bsz, pos0, SB_HEADS, SB_HEAD_DIM)
                pv = jnp.take(cache_v[idx], page_table, axis=0).reshape(bsz, pos0, SB_HEADS, SB_HEAD_DIM)
            m, k_new, v_new, s_new = _ab_mixer(x, pos0, pk, pv, ret0[idx], w_in_ab[idx], w_out_ab[idx],
                                               sb_bias[idx])
            new_k.append(k_new)
            new_v.append(v_new)
            ret_s.append(s_new)
        else:
            m, h_new, c_new = _ssd_mixer(x, ssm0[idx], sconv0[idx], w_in_ssd[idx], conv_w_ssd[idx],
                                         conv_b_ssd[idx], dt_bias[idx], a_log[idx], d_skip[idx],
                                         norm_w_ssd[idx], w_out_ssd[idx])
            ssm_s.append(h_new)
            ssm_c.append(c_new)
        x = _layer_norm(DN_ALPHA * x + m, ln1_g[layer], ln1_b[layer])
        f, fc = _conv_ffn(x, fconv0[layer], w_up[layer], conv_w_ffn[layer], conv_b_ffn[layer], w_down[layer])
        ffn_c.append(fc)
        x = _layer_norm(DN_ALPHA * x + f, ln2_g[layer], ln2_b[layer])
    return (x, jnp.stack(new_k), jnp.stack(new_v), jnp.stack(ret_s), jnp.stack(ssm_s),
            jnp.stack(ssm_c), jnp.stack(ffn_c))

def setup_inputs(seed: int = 0) -> dict:
    key = jax.random.key(seed)
    ks = iter(jax.random.split(key, 48))

    def nrm(shape, scale):
        return jax.random.normal(next(ks), shape, jnp.float32) * scale

    n_pages = PAST_LEN // PAGE_SIZE
    n_used = DEC_BATCH * n_pages
    n_phys = n_used + n_used // 4
    perm = jax.random.permutation(next(ks), n_phys)
    page_table = perm[:n_used].reshape(DEC_BATCH, n_pages).astype(jnp.int32)

    dt_init = jnp.exp(jax.random.uniform(next(ks), (N_ODD, SSM_HEADS), jnp.float32)
                      * (math.log(0.1) - math.log(0.001)) + math.log(0.001))
    dt_bias = dt_init + jnp.log(-jnp.expm1(-dt_init))
    a_log = jnp.log(jax.random.uniform(next(ks), (N_ODD, SSM_HEADS), jnp.float32, 1.0, 16.0))

    return {
        'x_prompt': nrm((BATCH, SEQ, D_MODEL), 1.0),
        'x_sample': nrm((DEC_BATCH, DEC_SEQ, D_MODEL), 1.0),
        'cache_k': nrm((N_EVEN, n_phys, PAGE_SIZE, SB_HEADS, SB_HEAD_DIM), 1.0),
        'cache_v': nrm((N_EVEN, n_phys, PAGE_SIZE, SB_HEADS, SB_HEAD_DIM), 1.0),
        'page_table': page_table,
        'state_ret': nrm((N_EVEN, DEC_BATCH, RET_HEADS, RET_DK, RET_DV), 0.5),
        'state_ssm': nrm((N_ODD, DEC_BATCH, SSM_HEADS, SSM_HEAD_DIM, SSM_D_STATE), 0.5),
        'state_ssm_conv': nrm((N_ODD, DEC_BATCH, SSM_CONV - 1, SSM_CONV_DIM), 1.0),
        'state_ffn_conv': nrm((DEPTH, DEC_BATCH, FFN_CONV - 1, 2 * D_FF), 1.0),
        'ln1_g': 1.0 + nrm((DEPTH, D_MODEL), 0.02),
        'ln1_b': nrm((DEPTH, D_MODEL), 0.02),
        'ln2_g': 1.0 + nrm((DEPTH, D_MODEL), 0.02),
        'ln2_b': nrm((DEPTH, D_MODEL), 0.02),
        'w_in_ab': nrm((N_EVEN, D_MODEL, AB_IN), D_MODEL ** -0.5),
        'w_out_ab': nrm((N_EVEN, AB_OUT, D_MODEL), AB_OUT ** -0.5 * DN_BETA),
        'sb_bias': SB_BIAS_INIT + nrm((N_EVEN, SB_HEADS), 0.1),
        'w_in_ssd': nrm((N_ODD, D_MODEL, SSM_IN), D_MODEL ** -0.5),
        'conv_w_ssd': nrm((N_ODD, SSM_CONV, SSM_CONV_DIM), SSM_CONV ** -0.5),
        'conv_b_ssd': nrm((N_ODD, SSM_CONV_DIM), 0.02),
        'dt_bias': dt_bias,
        'a_log': a_log,
        'd_skip': 1.0 + nrm((N_ODD, SSM_HEADS), 0.02),
        'norm_w_ssd': 1.0 + nrm((N_ODD, SSM_D_INNER), 0.02),
        'w_out_ssd': nrm((N_ODD, SSM_D_INNER, D_MODEL), SSM_D_INNER ** -0.5 * DN_BETA),
        'w_up': nrm((DEPTH, D_MODEL, 2 * D_FF), D_MODEL ** -0.5),
        'conv_w_ffn': nrm((DEPTH, FFN_CONV, 2 * D_FF), FFN_CONV ** -0.5),
        'conv_b_ffn': nrm((DEPTH, 2 * D_FF), 0.02),
        'w_down': nrm((DEPTH, D_FF, D_MODEL), D_FF ** -0.5 * DN_BETA),
    }

def reference(x_prompt, x_sample, cache_k, cache_v, page_table, state_ret, state_ssm, state_ssm_conv,
              state_ffn_conv, ln1_g, ln1_b, ln2_g, ln2_b, w_in_ab, w_out_ab, sb_bias, w_in_ssd, conv_w_ssd,
              conv_b_ssd, dt_bias, a_log, d_skip, norm_w_ssd, w_out_ssd, w_up, conv_w_ffn, conv_b_ffn, w_down):
    bp = x_prompt.shape[0]
    past_len = page_table.shape[1] * PAGE_SIZE
    ret0 = jnp.zeros((N_EVEN, bp, RET_HEADS, RET_DK, RET_DV), jnp.float32)
    ssm0 = jnp.zeros((N_ODD, bp, SSM_HEADS, SSM_HEAD_DIM, SSM_D_STATE), jnp.float32)
    sconv0 = jnp.zeros((N_ODD, bp, SSM_CONV - 1, SSM_CONV_DIM), x_prompt.dtype)
    fconv0 = jnp.zeros((DEPTH, bp, FFN_CONV - 1, 2 * D_FF), x_prompt.dtype)
    y_prompt, k_prompt, v_prompt, ret_prompt, ssm_prompt, ssm_conv_prompt, ffn_conv_prompt = _trunk(
        x_prompt, 0, None, None, None, ret0, ssm0, sconv0, fconv0,
        ln1_g, ln1_b, ln2_g, ln2_b, w_in_ab, w_out_ab, sb_bias, w_in_ssd, conv_w_ssd, conv_b_ssd,
        dt_bias, a_log, d_skip, norm_w_ssd, w_out_ssd, w_up, conv_w_ffn, conv_b_ffn, w_down)
    y_sample, k_sample, v_sample, ret_sample, ssm_sample, ssm_conv_sample, ffn_conv_sample = _trunk(
        x_sample, past_len, cache_k, cache_v, page_table, state_ret, state_ssm, state_ssm_conv, state_ffn_conv,
        ln1_g, ln1_b, ln2_g, ln2_b, w_in_ab, w_out_ab, sb_bias, w_in_ssd, conv_w_ssd, conv_b_ssd,
        dt_bias, a_log, d_skip, norm_w_ssd, w_out_ssd, w_up, conv_w_ffn, conv_b_ffn, w_down)
    return (y_prompt, y_sample, k_prompt, v_prompt, k_sample, v_sample, ret_prompt, ret_sample,
            ssm_prompt, ssm_sample, ssm_conv_prompt, ssm_conv_sample, ffn_conv_prompt, ffn_conv_sample)


_drawn_inputs = setup_inputs


def setup_inputs(seed=0):
    import zlib

    import numpy as np

    out = dict(_drawn_inputs(seed))
    spreads = {}
    factors = {'cache_k': 4.914,
     'cache_v': 3.949,
     'sb_bias': 8.0,
     'd_skip': 8.0,
     'norm_w_ssd': 8.0,
     'conv_b_ffn': 5.869}
    for name, (base, spread) in spreads.items():
        noise = np.random.default_rng([zlib.crc32(name.encode()), seed]).standard_normal(out[name].shape)
        drawn = base * np.exp(spread * noise) if base else spread * noise
        out[name] = jnp.asarray(drawn.astype(out[name].dtype))
    for name, factor in factors.items():
        out[name] = (out[name] * factor).astype(out[name].dtype)
    return out
```

```python
from contextlib import ExitStack
import math

import numpy as np
import concourse.bass as bass
from concourse import mybir

F32 = mybir.dt.float32
F32R = mybir.dt.float32r
I32 = mybir.dt.int32
ALU = mybir.AluOpType
ACT = mybir.ActivationFunctionType
AX = mybir.AxisListType

P = 128
D = 2048
SEQ = 256
NB = 8
T = SEQ + NB
KT = D // P
H = 8
DEPTH = 2
PAST = 256
PAGE = 128
NPG = PAST // PAGE
NPHYS = 20
FF = 11 * D // 4
FT = FF // P
SSM_IN = 2 * D
XST = SSM_IN // P
G = 8
CT = XST + 2 * G
NH = 64
HD = 64
ALPHA = float((2 * DEPTH) ** 0.25)
EPS = 1e-5
SCALE = float(128 ** -0.5)
GAMMA = [1.0 - 2.0 ** (-5.0 - h) for h in range(H)]

QA, VR, KA, VA, QR, KR = 0, 8, 24, 32, 40, 48
AB_TILES = 56
BM, CM, XS = 0, 8, 16

CK = 4
CN = 4
CW = CK * CN * P
NRAW = 8
NHI = 3
LOOK = 2


class Step:

    def __init__(self, base, reg=None):
        self.base, self.reg = base, reg

    def at(self, times, plus):
        fixed = self.base * times + plus
        return fixed if self.reg is None else self.reg * times + fixed

    def next(self):
        return Step(self.base + 1, self.reg)


class Phase:

    def __init__(self, name, iters, panels, kc, ring):
        self.name, self.iters, self.panels, self.kc, self.ring = name, iters, panels, kc, ring
        self.body = panels * kc

    def place(self, before):
        self.chunk0, self.panel0, self.acc0 = before


def plan():
    phases = [
        Phase("ab", 9, 2, 4, False), Phase("out_ab", 2, 2, 6, True),
        Phase("up0", 11, 2, 4, False), Phase("down0", 4, 1, 11, True),
        Phase("dt", 1, 1, 1, False), Phase("ssd", 10, 2, 4, False), Phase("out_ssd", 4, 1, 8, True),
        Phase("up1", 11, 2, 4, False), Phase("down1", 4, 1, 11, True),
    ]
    c = p = a = 0
    raw, hi = [], []
    for ph in phases:
        ph.place((c, p, a))
        c += ph.iters * ph.body
        p += ph.iters * ph.panels
        a += 0 if ph.name == "dt" else 3 * ph.iters * ph.panels
        for _ in range(ph.iters):
            raw += [j % NRAW for j in range(ph.body)]
            hi += [j % NHI for j in range(ph.body)]
    uses = []
    count = [0] * NRAW
    for s in raw:
        count[s] += 1
        uses.append(count[s])

    def previous(slots):
        last, out = {}, []
        for n, s in enumerate(slots):
            out.append(last.get(s, -1))
            last[s] = n
        return out

    return {ph.name: ph for ph in phases}, phases, c, uses, previous(raw), previous(hi)


PHASES, ORDER, CHUNKS, USES, RAW_PREV, HI_PREV = plan()

CONST = {}


def const_layout():
    at = 0
    for name, width in (("ident", P), ("ones", P), ("upper", P), ("rot", P), ("mask", 384), ("cap", 384),
                        ("cosq", T), ("sinq", T), ("cosk", T), ("sink", T), ("decay", H * 384),
                        ("tend", 2 * H), ("mask2", 384)):
        CONST[name] = (at, at + width)
        at += width
    return at


CONST_W = const_layout()


def constants():
    c = np.zeros((P, CONST_W), np.float32)

    def put(name, a):
        c[:, CONST[name][0]:CONST[name][1]] = a

    j = np.arange(P)
    put("ident", np.eye(P))
    put("ones", np.ones((P, P)))
    put("upper", (j[:, None] >= j[None, :]))
    rot = np.zeros((P, P))
    for m in range(64):
        rot[m + 64, m] = -1.0
        rot[m, m + 64] = 1.0
    put("rot", rot)
    key = np.concatenate([np.tile(j[:, None], (1, 256)), np.tile(j[:, None] + 128, (1, 128))], 1)
    query = np.concatenate([np.arange(256), np.arange(128, 256)])[None, :]
    put("mask", key < query)
    put("mask2", key <= query)
    put("cap", np.where(key < query, 0.0, -1e30))
    half = 64
    inv = (np.float32(10000.0) ** (-np.linspace(0.0, 1.0, half, dtype=np.float32))).astype(np.float32)
    pos = np.concatenate([np.arange(SEQ), np.full(NB, PAST)]).astype(np.float32)
    ang = (pos[None, :] * inv[:, None]).astype(np.float32)
    cos, sin = np.cos(ang, dtype=np.float32), np.sin(ang, dtype=np.float32)
    cos, sin = np.concatenate([cos, cos]), np.concatenate([sin, sin])
    put("cosq", cos)
    put("sinq", sin)
    put("cosk", cos * np.float32(SCALE))
    put("sink", sin * np.float32(SCALE))
    gap = (query - key).astype(np.float64)
    put("decay", np.concatenate([np.where(gap >= 0, g ** np.maximum(gap, 0), 0.0) for g in GAMMA], 1))
    put("tend", np.stack([g ** (255.0 - (ch * 128 + j)) for g in GAMMA for ch in range(2)], 1))
    return c


PARAM = {}


def param_layout():
    at = 0
    for name, width in (("lng", 4 * KT), ("lnb", 4 * KT), ("sbias", H), ("fcw", DEPTH * 3 * 2 * FT),
                        ("fcb", DEPTH * 2 * FT), ("scw", 4 * CT), ("scb", CT), ("dskip", XST),
                        ("normw", XST), ("dtb", 1), ("alog", 1)):
        PARAM[name] = (at, at + width)
        at += width
    return at


PARAM_W = param_layout()
OUT_SHAPES = {
    "y": (P, KT, T), "kv": (P, 2 * H, T), "retp": (P, H, 256), "rets": (NB, P, H * 256),
    "ssmp": (P, XST, P), "ssms": (NB, P, SSM_IN),
    "sconv": (P, CT, 11), "sconv_old": (P, CT, 2, NB), "fconv": (DEPTH, P, 2 * FT, 10),
    "fconv_old": (DEPTH, P, 2 * FT, NB),
}


SIGNALS = (
    "att_in", "cd_p", "cd_ready", "consts_in", "conv_base", "conv_silu", "conv_tap", "dt_a", "dt_c", "ffn_out",
    "ffn_state_in", "ffn_sum", "ffn_tile", "g_arg", "g_bc", "g_bt", "g_btc", "g_cb", "g_cbm", "g_e", "g_inv",
    "g_n", "g_out", "g_sq", "g_sqrt", "g_ss", "g_ssc", "g_st", "g_stc", "g_w", "g_x", "g_xt", "g_yd", "g_yh",
    "g_z", "gate_in", "gate_out", "kv_out", "ln_a", "ln_cen", "ln_d", "ln_mean", "ln_norm", "ln_rstd", "ln_sq",
    "ln_sqrt", "ln_sqsum", "ln_sum", "ln_var", "mask_in", "page_in0", "page_in1", "page_in2", "page_used",
    "pages_in", "rn_a", "rn_b", "rn_inv", "rn_sq", "rn_sqrt", "rn_sum", "rot_c", "rot_done", "rot_m", "rot_p",
    "rs_in0", "rs_in1", "rs_km", "rs_new", "rs_o", "rs_out0", "rs_out1", "rs_t", "rs_tc", "rs_y", "rs_yc",
    "rt_k", "rt_out", "rt_p", "rt_s", "rt_st", "rt_stc", "rt_t", "rt_v", "rt_y", "rt_yc", "sb_L", "sb_arg",
    "sb_cap", "sb_e", "sb_incl", "sb_lf", "sb_m", "sb_na", "sb_part", "sb_vs", "sb_vt", "sb_w", "sb_y",
    "sb_ycopy", "sbz", "sbz_s", "sconv_in", "sconv_out", "sm_t", "small_set", "ss_h", "ss_in0", "ss_in1",
    "ss_in2", "ss_n", "ss_o", "ss_out0", "ss_out1", "ss_out2", "ss_t", "ss_x", "ss_y", "ss_ya", "ss_yd",
    "ssd_sum", "x_back", "x_hi", "x_in", "x_lo", "x_out", "y_out", "z_in",
)


def build(nc, d):
    ctx = ExitStack()

    def sb(name, shape, dt=F32):
        return ctx.enter_context(nc.sbuf_tensor(name, shape, dt))

    def sem(name):
        return ctx.enter_context(nc.semaphore(name))

    with ctx:
        NHB = 3
        with nc.sbuf_tensor("lo", [P, NRAW, CW], F32R) as lo:
            pass
        raw = sb("raw", [P, NRAW, CW])
        with nc.sbuf_tensor("work", [P, 3 * KT * T], F32) as work:
            pass
        x_ = sb("x", [P, KT * T])
        xh = sb("xh", [P, KT, T], F32R)
        xl = sb("xl", [P, KT, T], F32R)
        pj = sb("pj", [P, AB_TILES * T])
        hi = sb("hi", [P, NHI, CW], F32R)
        cons = sb("cons", [P, 2 * P])
        par = sb("par", [P, PARAM_W])
        stage = sb("stage", [P, CN, T])
        small = sb("small", [P, 8])
        dtraw = sb("dtraw", [NH, T])
        pages_sb = sb("pages", [1, NB * NPG], I32)
        x = x_[:, :].rearrange("p (t n) -> p t n", n=T)
        pt = pj[:, :].rearrange("p (t n) -> p t n", n=T)
        ident, ones = cons[:, 0:P], cons[:, P:2 * P]
        eps_col, one_col = small[:, 0:1], small[:, 1:2]

        def par_of(name):
            return par[:, PARAM[name][0]:PARAM[name][1]]

        lng = par_of("lng").rearrange("p (l t) -> p l t", t=KT)
        lnb = par_of("lnb").rearrange("p (l t) -> p l t", t=KT)
        fcw = par_of("fcw").rearrange("p (l w t) -> p l w t", l=DEPTH, w=3)
        fcb = par_of("fcb").rearrange("p (l t) -> p l t", l=DEPTH)
        scw = par_of("scw").rearrange("p (w t) -> p w t", w=4)
        scb = par_of("scb")

        def carve(tensor, at, *shape):
            n = int(np.prod(shape))
            v = tensor[:, at:at + n]
            if len(shape) == 2:
                v = v.rearrange("p (a b) -> p a b", a=shape[0])
            elif len(shape) == 3:
                v = v.rearrange("p (a b c) -> p a b c", a=shape[0], b=shape[1])
            return v, at + n

        fst, at = carve(pj, FT * T, 2 * FT, 2, NB)
        fsum, at = carve(pj, at, 2 * FT, NB)
        fnew, at = carve(pj, at, 2 * FT, 10)
        sst, at = carve(pj, CT * T, CT, 3, NB)
        ssum, at = carve(pj, at, CT, NB)
        snew, at = carve(pj, at, CT, 11)
        ftmp = stage[:, :, :].rearrange("p a b -> p (a b)")[:, 0:2 * FT * NB].rearrange("p (a b) -> p a b", b=NB)
        stmp = stage[:, :, :].rearrange("p a b -> p (a b)")[:, 0:CT * NB].rearrange("p (a b) -> p a b", b=NB)

        acc = [ctx.enter_context(nc.psum_tensor(f"acc{n}", [P, 512], F32)) for n in range(4)]
        aux = [ctx.enter_context(nc.psum_tensor(f"aux{n}", [P, 512], F32)) for n in range(4)]
        banks = [aux, acc]

        at = 0
        upper, at = carve(work, at, P)
        rot, at = carve(work, at, P)
        mask, at = carve(work, at, 384)
        cap, at = carve(work, at, 384)
        trig, at = carve(work, at, 4, T)
        decay, at = carve(work, at, H, 384)
        tend, at = carve(work, at, H, 2)
        c0, c1 = CONST["upper"][0], CONST["tend"][1]
        assert at == c1 - c0, (at, c1 - c0)
        work_consts = work[:, 0:at]
        att0 = at
        temps = []
        for _ in range(2):
            zs, at = carve(work, at, 384)
            e_, at = carve(work, at, 384)
            lf, at = carve(work, at, 384)
            temps.append((zs, e_, lf))
        vtok = []
        ktw = []
        for _ in range(2):
            v, at = carve(work, at, 2, 256)
            vtok.append(v)
            v, at = carve(work, at, 2, P)
            ktw.append(v)
        NPB = 3
        pg0 = at = max(at, att0 + 2 * H * 256)
        page = []
        for _ in range(NPB):
            v, at = carve(work, at, H, P)
            page.append(v)
        retp, _ = carve(work, pg0, H, 256)
        assert at <= 3 * KT * T, (at, 3 * KT * T)
        at = att0
        s0buf = []
        for _ in range(2):
            v, at = carve(work, at, H, 256)
            s0buf.append(v)
        assert at <= pg0 and pg0 + 2048 <= 3 * KT * T
        at = pg0
        vts, at = carve(work, at, 2048)
        kts, _ = carve(work, c1 - c0 - H * 2 - H * 384, 1024)
        ktm, _ = carve(work, c1 - c0 - H * 2 - H * 384 + 1024, 1024)
        silg, at = carve(work, 0, 2 * H, T)
        rsum, at = carve(work, at, H, T)
        rsq, at = carve(work, at, 2, 2, T)

        at = 0
        smask = stage[:, :, :].rearrange("p a b -> p (a b)")[:, 0:384]
        cumT, at = carve(work, at, SEQ)
        dtT, at = carve(work, at, T)
        dte, at = carve(work, at, T)
        cdT, at = carve(work, at, NB)
        dA, at = carve(work, at, T)
        wendT, at = carve(work, at, SEQ)
        nctok, at = carve(work, at, 2, NH)
        dtok, at = carve(work, at, 2, NH)
        wend, at = carve(work, at, 2, NH)
        dts, at = carve(work, at, NH)
        cds, at = carve(work, at, NH)
        cdbc, at = carve(work, at, NB, NH)
        acol, at = carve(work, at, 1)
        ssm0 = at
        cbm, at = carve(work, at, 384)
        btok, at = carve(work, at, 2, P)
        xdt, at = carve(work, at, 2, 512)
        xw, at = carve(work, at, 2, 512)
        esb = []
        for _ in range(2):
            v, at = carve(work, at, 384)
            esb.append(v)
        wsb = []
        for _ in range(2):
            v, at = carve(work, at, 384)
            wsb.append(v)
        hst, at = carve(work, at, 4, P)
        zg, at = carve(work, at, 4, T)
        gsq, at = carve(work, at, 4, T)
        gsum, at = carve(work, at, G, T)
        assert at <= 3 * KT * T, at
        at = ssm0
        xds, at = carve(work, at, SSM_IN)
        hbuf = []
        for _ in range(NHB):
            v, at = carve(work, at, SSM_IN // 2)
            hbuf.append(v)
        assert at <= 3 * KT * T, at

        lsq = pt[:, 0:KT, :]
        lsum, lrt = pt[:, KT, :], pt[:, KT + 1, :]
        ln_after = [4 * PHASES[n].panel0 + 4 for n in ("up0", "dt", "up1")]
        ln_after.append(4 * (PHASES["down1"].panel0 + 4) + 4)
        conv_silu0 = {0: 0, "ssd": FT // 2, 1: FT // 2 + CT // CN}
        tap0 = {0: 0, "ssd": 2 * FT, 1: 2 * FT + 2 * CT}

        def obank(h):
            return acc[h // 2][:, (h % 2) * 256:(h % 2) * 256 + 256]

        def row_of(n, rows):
            return ident[0:rows, n:n + 1].to_broadcast([rows, P])

        landed = [sem(f"landed{s}") for s in range(NRAW)]
        hi_done = sem("hi_done")
        lo_done = sem("lo_done")
        used = sem("used")
        acc_done = sem("acc_done")
        drained = sem("drained")
        R = {n: sem(n) for n in SIGNALS}
        block = ctx.enter_context(nc.Block())

        def chunk_of(ph, i, j):
            return i.at(ph.body, ph.chunk0 + j)

        def load_chunk(eng, ph, i, j):
            n = ph.chunk0 + i.base * ph.body + j
            if RAW_PREV[n] >= 0:
                eng.wait_ge(used, i.at(ph.body, RAW_PREV[n] + 1 - i.base * ph.body))
            c, s = chunk_of(ph, i, j), j % NRAW
            src = d["w"][c] if isinstance(c, int) else d["w"][bass.ds(c, 1)].rearrange("a p f -> (a p) f")
            eng.dma_start(raw[:, s, :], src).then_inc(landed[s], 16)

        def fill(ph, i, j):
            n = ph.chunk0 + j
            per = USES[n + ph.body] - USES[n] if ph.iters > 1 else 0
            return i.at(16 * per, 16 * USES[n])

        def hi_wait(ph, i, j):
            if i.reg is None:
                c = chunk_of(ph, i, j)
                back = c - HI_PREV[c] if HI_PREV[c] >= 0 else None
            else:
                back = min(n - HI_PREV[n] for n in (ph.chunk0 + k * ph.body + j for k in range(ph.iters))
                           if HI_PREV[n] >= 0)
            if back is None:
                return None
            if ph.ring:
                back = min(back, 3)
            if i.reg is not None:
                back = min(back, ph.chunk0 + i.base * ph.body + j)
            return i.at(ph.body, ph.chunk0 + j + 1 - back)

        def split_hi(act, ph, i, j, src):
            act.wait_ge(landed[j % NRAW], fill(ph, i, j))
            w = hi_wait(ph, i, j)
            if w is not None:
                act.wait_ge(used, w)
            if ph.ring:
                kc, s = j % ph.kc, j % 4
                act.activation(xh[:, CK * s:CK * s + CK, :], src[:, CK * kc:CK * kc + CK, :], ACT.Copy)
            act.activation(hi[:, j % NHI, :], raw[:, j % NRAW, :], ACT.Copy).then_inc(hi_done, 1)

        def split_lo(dve, ph, i, j, src):
            dve.wait_ge(hi_done, i.at(ph.body, ph.chunk0 + j + 1))
            if ph.ring:
                kc, s = j % ph.kc, j % 4
                dve.tensor_tensor(xl[:, CK * s:CK * s + CK, :], src[:, CK * kc:CK * kc + CK, :],
                                  xh[:, CK * s:CK * s + CK, :].bitcast(F32), ALU.subtract)
            dve.tensor_tensor(lo[:, j % NRAW, :], raw[:, j % NRAW, :], hi[:, j % NHI, :].bitcast(F32),
                              ALU.subtract).then_inc(lo_done, 1)

        def split_loop(eng, ph, split, src, evac, first=0, end=None):
            end = ph.iters if end is None else end
            if first == 0:
                for j in range(min(LOOK, ph.body * ph.iters)):
                    split(eng, ph, Step(0), j, src)

            def body(i, last):
                since = Step(i.base - first, i.reg)
                for j in range(ph.body):
                    n = j + LOOK
                    if n < ph.body:
                        split(eng, ph, i, n, src)
                    elif not last:
                        split(eng, ph, i.next(), n - ph.body, src)
                    if j % ph.kc == ph.kc - 1:
                        evac(eng, ph, i, j // ph.kc, since.at(ph.panels, j // ph.kc))

            stop = end - 1 if end == ph.iters else end
            if stop - first > 1:
                with eng.Fori(0, stop - first) as r:
                    body(Step(first, r), False)
            elif stop > first:
                body(Step(first), False)
            if end == ph.iters:
                body(Step(end - 1), True)

        def wait_acc(eng, ph, i, pb, n):
            if n < 3:
                eng.wait_ge(acc_done, i.at(3 * ph.panels, ph.acc0 + 3 * pb + n + 1))
            else:
                eng.wait_ge(used, i.at(ph.body, ph.chunk0 + pb * ph.kc + ph.kc))

        def products(pe, ph):
            def body(i):
                for j in range(ph.body):
                    pb, kc = j // ph.kc, j % ph.kc
                    pe.wait_ge(lo_done, i.at(ph.body, ph.chunk0 + j + 1))
                    s, r = j % NHI, j % NRAW
                    for n in range(CN):
                        if kc == 0:
                            pe.wait_ge(drained, i.at(4 * ph.panels, 4 * (ph.panel0 + pb) + n + 1))
                        for k in range(CK):
                            a = (j % 4 if ph.ring else kc) * CK + k
                            w = slice((k * CN + n) * P, (k * CN + n + 1) * P)
                            out = acc[n][:, 0:T]
                            pe.matmul(out, hi[:, s, w], xh[:, a, :], start=kc == 0 and k == 0, stop=False)
                            pe.matmul(out, hi[:, s, w], xl[:, a, :], start=False, stop=False)
                            m = pe.matmul(out, lo[:, r, w], xh[:, a, :], start=False,
                                          stop=kc == ph.kc - 1 and k == CK - 1)
                        if n < 3 and kc == ph.kc - 1:
                            m.then_inc(acc_done, 1)
                    m.then_inc(used, 1)

            with pe.Fori(0, ph.iters) as r:
                body(Step(0, r))

        @block.sync
        def _(sp):
            sp.dma_start(x_[:, :], d["x"]).then_inc(R["x_in"], 16)
            for ph in ORDER:
                for j in range(ph.body):
                    load_chunk(sp, ph, Step(0), j)
                if ph.iters > 1:
                    with sp.Fori(0, ph.iters - 1) as r:
                        for j in range(ph.body):
                            load_chunk(sp, ph, Step(1, r), j)

        @block.gpsimd
        def _(pool):
            pool.dma_start(cons[:, :], d["const"][:, 0:2 * P]).then_inc(R["consts_in"], 16)
            pool.dma_start(par[:, :], d["param"]).then_inc(R["consts_in"], 16)
            pool.dma_start(pages_sb[:, :], d["pages"]).then_inc(R["pages_in"], 16)

            for n in range(4):
                pool.wait_ge(drained, 4 * (PHASES["ab"].panel0 + 14 + n) + 8)
                pool.dma_start(d["gate"][:, 4 * n:4 * n + 4, :], stage[:, :, :]).then_inc(R["gate_out"], 16)

            pool.wait_ge(used, PHASES["out_ab"].chunk0)
            pool.wait_ge(R["x_lo"], 1)
            pool.dma_start(work_consts, d["const"][:, c0:c1]).then_inc(R["att_in"], 16)
            pool.wait_ge(drained, 4 * PHASES["out_ab"].panel0 + 4)
            pool.dma_start(d["kv"], pt[:, KA:KA + 2 * H, :]).then_inc(R["kv_out"], 16)
            pool.wait_ge(R["pages_in"], 16)
            n = 0
            for cache in ("ck", "cv"):
                for b in range(NB):
                    for k in range(NPG):
                        v = pool.value_load(pages_sb[0:1, b * NPG + k:b * NPG + k + 1], min_val=0, max_val=NPHYS - 1)
                        if n >= NPB:
                            pool.wait_ge(R["page_used"], n - NPB + 1)
                        pool.dma_start(page[n % NPB], d[cache][bass.ds(v, 1)].rearrange("a p h f -> (a p) h f"))\
                            .then_inc(R[f"page_in{n % NPB}"], 16)
                        n += 1
            pool.wait_ge(R["rt_stc"], H)
            pool.dma_start(d["retp"], retp).then_inc(R["rt_out"], 16)

            def ret_store(b):
                pool.wait_ge(R["rs_new"], H * (b + 1))
                pool.dma_start(d["rets"][b].rearrange("p (h e) -> p h e", h=H), s0buf[b % 2])\
                    .then_inc(R[f"rs_out{b % 2}"], 16)

            pool.wait_ge(R["rt_yc"], H)
            for b in range(NB):
                if b >= 2:
                    pool.wait_ge(R["rs_y"], b - 1)
                    pool.wait_ge(R[f"rs_out{b % 2}"], 16 * (b // 2))
                pool.dma_start(s0buf[b % 2], d["ret0"][b].rearrange("p (h e) -> p h e", h=H))\
                    .then_inc(R[f"rs_in{b % 2}"], 16)
                if b >= 1:
                    ret_store(b - 1)
            ret_store(NB - 1)
            pool.wait_ge(R["rs_out0"], 16 * (NB // 2))
            pool.wait_ge(R["rs_out1"], 16 * (NB // 2))
            pool.wait_ge(R["rs_yc"], 1)
            pool.wait_ge(R["gate_out"], 16 * 4)
            pool.dma_start(silg, d["gate"][:, 0:2 * H, :]).then_inc(R["gate_in"], 16)
            pool.wait_ge(R["rn_b"], 1)
            pool.dma_start(x_[:, :], d["x"]).then_inc(R["x_back"], 16)

            def ffn(layer):
                pool.wait_ge(used, PHASES[f"up{layer}"].chunk0)
                if layer == 0:
                    pool.wait_ge(R["kv_out"], 16)
                else:
                    pool.wait_ge(R["sconv_out"], 32)
                pool.dma_start(fst, d["fst"][layer]).then_inc(R["ffn_state_in"], 16)
                up = PHASES[f"up{layer}"]
                pool.wait_ge(drained, 4 * (up.panel0 + up.iters * up.panels) + 4)
                pool.wait_ge(R["ffn_state_in"], 16 * (layer + 1))
                pool.dma_start(d["fconv"][layer], fnew).then_inc(R["ffn_out"], 16)
                pool.dma_start(d["fconv_old"][layer], fst[:, :, 1, :]).then_inc(R["ffn_out"], 16)

            ffn(0)
            pool.wait_ge(R["ffn_out"], 32)
            pool.wait_ge(used, PHASES["dt"].chunk0)
            pool.dma_start(sst, d["sst"]).then_inc(R["sconv_in"], 16)
            pool.wait_ge(R["ln_a"], 2 * (KT // 2))
            pool.wait_ge(R["ln_d"], 2 * (KT // 2))
            pool.dma_start(d["xsave"], x_[:, :]).then_inc(R["x_out"], 16)
            for n in range(8):
                pool.wait_ge(drained, 4 * (PHASES["ssd"].panel0 + 12 + n) + 8)
                pool.wait_ge(R["gate_in"], 16)
                pool.dma_start(d["gate"][:, 4 * n:4 * n + 4, :], stage[:, :, :]).then_inc(R["gate_out"], 16)
            pool.wait_ge(R["sconv_in"], 16)
            pool.dma_start(d["sconv"], snew).then_inc(R["sconv_out"], 16)
            pool.dma_start(d["sconv_old"], sst[:, :, 1:3, :]).then_inc(R["sconv_out"], 16)
            pool.wait_ge(used, PHASES["out_ssd"].chunk0)
            pool.wait_ge(R["x_out"], 16)
            pool.wait_ge(R["gate_out"], 16 * 12)
            pool.dma_start(smask, d["const"][:, CONST["mask2"][0]:CONST["mask2"][1]]).then_inc(R["mask_in"], 16)

            def state_load(u):
                b, half = u // 2, u % 2
                if u >= NHB:
                    pool.wait_ge(R["ss_y"], u - NHB + 1)
                    pool.wait_ge(R[f"ss_out{u % NHB}"], 16 * (u // NHB))
                pool.dma_start(hbuf[u % NHB], d["ssm0"][b][:, half * 2048:half * 2048 + 2048])\
                    .then_inc(R[f"ss_in{u % NHB}"], 16)

            units = 2 * NB
            state_load(0)
            state_load(1)
            for u in range(units):
                b, half = u // 2, u % 2
                pool.wait_ge(R[f"ss_in{u % NHB}"], 16 * (u // NHB + 1))
                pool.wait_ge(R["cd_ready"], 1)
                hv = hbuf[u % NHB].rearrange("p (h q) -> p h q", q=HD)
                f = cdbc[:, b, 32 * half:32 * half + 32].unsqueeze(2).to_broadcast([P, 32, HD])
                pool.tensor_tensor(hv, hv, f, ALU.mult).then_inc(R["ss_h"], 1)
                if u + 2 < units:
                    state_load(u + 2)
                pool.wait_ge(R["ss_n"], 4 * (u + 1))
                pool.dma_start(d["ssms"][b][:, half * 2048:half * 2048 + 2048], hbuf[u % NHB])\
                    .then_inc(R[f"ss_out{u % NHB}"], 16)
            for s in range(NHB):
                pool.wait_ge(R[f"ss_out{s}"], 16 * ((units - s + NHB - 1) // NHB))
            pool.wait_ge(R["ss_ya"], 1)
            pool.wait_ge(R["gate_out"], 16 * 12)
            for g in range(G):
                if g >= 1:
                    pool.wait_ge(R["g_z"], g)
                pool.dma_start(zg, d["gate"][:, 4 * g:4 * g + 4, :]).then_inc(R["z_in"], 16)
                pool.wait_ge(R["g_stc"], g + 1)
                pool.dma_start(d["ssmp"][:, 4 * g:4 * g + 4, :], hst).then_inc(R["g_out"], 16)
            pool.wait_ge(R["g_n"], XST)
            pool.wait_ge(R["g_out"], 16 * G)
            pool.dma_start(x_[:, :], d["xsave"]).then_inc(R["x_back"], 16)
            ffn(1)
            pool.wait_ge(R["ln_a"], 4 * (KT // 2))
            pool.wait_ge(R["ln_d"], 4 * (KT // 2))
            pool.dma_start(d["y"], x_[:, :]).then_inc(R["y_out"], 16)
            pool.wait_ge(R["y_out"], 16)
            pool.wait_ge(R["ffn_out"], 64)
            pool.wait_ge(R["rt_out"], 16)
            pool.wait_ge(R["kv_out"], 16)

        @block.scalar
        def _(act):
            a = act.activation

            def apart(eng):
                eng.wait_ge(R["consts_in"], 32)

            def copy_tiles(eng, ph, i, pb, q):
                for n in range(CN):
                    wait_acc(eng, ph, i, pb, n)
                    apart(eng)
                    t = q * CN + n
                    dst = pt[:, t, :] if isinstance(t, int) else pt[:, bass.ds(t, 1), :].rearrange("p a n -> p (a n)")
                    a(dst, acc[n][:, 0:T], ACT.Copy).then_inc(drained, 1)

            def gate_tiles(base):
                def evac(eng, ph, i, pb, q):
                    if base or q:
                        eng.wait_ge(R["gate_out"], q * 16 + base * 16)
                    for n in range(CN):
                        wait_acc(eng, ph, i, pb, n)
                        a(stage[:, n, :], acc[n][:, 0:T], ACT.Silu).then_inc(drained, 1)
                return evac

            def conv_base(w, bias, dst, silu):
                def evac(eng, ph, i, pb, q):
                    for n in range(CN):
                        wait_acc(eng, ph, i, pb, n)
                        apart(eng)
                        ch = q * CN + n
                        col = (lambda v: v[:, ch:ch + 1] if isinstance(ch, int) else v[:, bass.ds(ch, 1)])
                        a(dst(q, n), acc[n][:, 0:T], ACT.Identity, bias=col(bias), scale=col(w))\
                            .then_inc(R["conv_base"], 1)
                    eng.wait_ge(drained, i.at(4 * ph.panels, 4 * (ph.panel0 + pb) + 8))
                    a(small[:, 2:3], small[:, 1:2], ACT.Silu)
                    silu(q)
                return evac

            act.wait_ge(R["x_in"], 16)
            a(xh[:, :, :], x, ACT.Copy).then_inc(R["x_hi"], 1)
            act.wait_ge(R["consts_in"], 32)
            act.wait_ge(R["small_set"], 2)

            ab = PHASES["ab"]
            split_loop(act, ab, split_hi, None, copy_tiles, 0, 7)
            split_loop(act, ab, split_hi, None, gate_tiles(0), 7, 9)

            act.wait_ge(R["att_in"], 16)

            def sb_z(h):
                bk, (zs, e, lf) = banks[h % 2], temps[h % 2]
                act.wait_ge(R["sbz"], h + 1)
                if h >= 2:
                    act.wait_ge(R["sb_arg"], h - 1)
                a(zs, bk[0][:, 0:384], ACT.Identity, bias=par_of("sbias")[:, h:h + 1], scale=SCALE)\
                    .then_inc(R["sbz_s"], 1)
                act.wait_ge(R["sb_vt"], h + 1)
                if h >= 2:
                    act.wait_ge(R["sb_y"], h - 1)
                a(vtok[h % 2][:, 0, :], bk[2][:, 0:256], ACT.Copy).then_inc(R["sb_vs"], 1)

            def sb_softplus(h, n=384):
                e = temps[h % 2][1][:, 0:n]
                act.wait_ge(R["sb_na"], h + 1)
                a(e, e, ACT.Exp).then_inc(R["sb_e"], 1)
                act.wait_ge(R["sb_e"], h + 1)
                a(e, e, ACT.Ln, bias=one_col).then_inc(R["sb_L"], 1)

            def sb_weight(h, n=384):
                e = temps[h % 2][1][:, 0:n]
                act.wait_ge(R["sb_cap"], h + 1)
                a(e, e, ACT.Exp).then_inc(R["sb_w"], 1)

            def sb_out(h):
                act.wait_ge(R["sb_y"], h + 1)
                a(pt[:, QA + h, 0:SEQ], banks[h % 2][3][:, 0:SEQ], ACT.Copy).then_inc(R["sb_ycopy"], 1)

            for t in range(H + 2):
                if t < H:
                    sb_z(t)
                    sb_softplus(t)
                if 1 <= t <= H:
                    sb_weight(t - 1)
                if t >= 2:
                    sb_out(t - 2)
            sb_softplus(H, 2 * NB * H)
            sb_weight(H, 2 * NB * H)

            for t in range(H + 1):
                if t < H:
                    h, bk = t, banks[t % 2]
                    act.wait_ge(R["rt_t"], h + 1)
                    if h >= 2:
                        act.wait_ge(R["rt_st"], h - 1)
                    a(vtok[h % 2].rearrange("p c e -> p (c e)"), bk[2][:, :], ACT.Copy).then_inc(R["rt_v"], 1)
                    for c in range(2):
                        ins = a(ktw[h % 2][:, c, :], bk[1][:, c * P:c * P + P], ACT.Identity,
                                scale=tend[:, h, c:c + 1])
                    ins.then_inc(R["rt_k"], 1)
                if t >= 1:
                    h = t - 1
                    act.wait_ge(R["rt_y"], h + 1)
                    a(pt[:, VR + 2 * h:VR + 2 * h + 2, 0:SEQ], banks[h % 2][3][:, :].rearrange("p (u n) -> p u n", u=2),
                      ACT.Copy).then_inc(R["rt_yc"], 1)
            act.wait_ge(R["rs_t"], 1)
            act.wait_ge(R["rt_out"], 16)
            act.wait_ge(R["rt_p"], H)
            for q in range(4):
                a(vts[0:NB, q * 512:q * 512 + 512], acc[q][0:NB, :], ACT.Copy)
            for q in range(2):
                ins = a(kts[0:NB, q * 512:q * 512 + 512], aux[q][0:NB, :], ACT.Copy)
            ins.then_inc(R["rs_tc"], 1)
            act.wait_ge(R["gate_in"], 16)
            act.wait_ge(R["rt_yc"], H)
            for t in range(H + 1):
                if t < H:
                    if t >= 2:
                        act.wait_ge(R["rn_sum"], t - 1)
                    a(rsq[:, t % 2], pt[:, VR + 2 * t:VR + 2 * t + 2, :], ACT.Square).then_inc(R["rn_sq"], 1)
                if t >= 1:
                    act.wait_ge(R["rn_sum"], t)
                    a(rsum[:, t - 1, :], aux[(t - 1) % 2][:, 0:T], ACT.Sqrt, bias=eps_col, scale=1.0 / 256)\
                        .then_inc(R["rn_sqrt"], 1)

            def norm(l, split):
                act.wait_ge(R["ln_cen"], l + 1)
                a(lsq, x, ACT.Square).then_inc(R["ln_sq"], 1)
                act.wait_ge(R["ln_var"], l + 1)
                a(lrt, aux[1][:, 0:T], ACT.Sqrt, bias=eps_col, scale=1.0 / D).then_inc(R["ln_sqrt"], 1)
                act.wait_ge(R["ln_norm"], l + 1)
                for t in range(KT // 2):
                    a(x[:, t, :], x[:, t, :], ACT.Identity, bias=lnb[:, l, t:t + 1], scale=lng[:, l, t:t + 1])\
                        .then_inc(R["ln_a"], 1)
                if split:
                    act.wait_ge(R["ln_d"], (l + 1) * (KT // 2))
                    act.wait_ge(R["ln_a"], (l + 1) * (KT // 2))
                    a(xh[:, :, :], x, ACT.Copy).then_inc(R["x_hi"], 1)

            def no_evac(eng, ph, i, pb, q):
                pass

            def ffn(layer):
                up, down = PHASES[f"up{layer}"], PHASES[f"down{layer}"]

                def silu(q):
                    a(stage[:, 0:2, :], stage[:, 0:2, :], ACT.Silu).then_inc(R["conv_silu"], 1)

                base = conv_base(fcw[:, layer, 2, :], fcb[:, layer, :], lambda q, n: stage[:, n, :], silu)

                def evac(eng, ph, i, pb, q):
                    eng.wait_ge(R["ffn_tile"], q + (layer * (FT // 2) + 1))
                    base(eng, ph, i, pb, q)

                act.wait_ge(R["ffn_sum"], 3 * (layer + 1))
                split_loop(act, up, split_hi, None, evac)
                act.wait_ge(R["ffn_tile"], (layer + 1) * (FT // 2) + 1)
                split_loop(act, down, split_hi, pt, no_evac)

            act.wait_ge(R["rn_b"], 1)
            act.wait_ge(R["sb_ycopy"], H + 1)
            split_loop(act, PHASES["out_ab"], split_hi, pt, no_evac)
            norm(0, True)
            ffn(0)
            norm(1, True)

            split_loop(act, PHASES["dt"], split_hi, None, no_evac)
            act.wait_ge(used, PHASES["dt"].chunk0 + 1)
            a(dtraw[:, :], acc[0][0:NH, 0:T], ACT.Identity, bias=par_of("dtb")[0:NH, :]).then_inc(drained, 4)

            def xbc_tile(q, n):
                t = q * CN + n
                return pt[:, t, :] if isinstance(t, int) else pt[:, bass.ds(t, 1), :].rearrange("p a n -> p (a n)")

            def xbc_silu(q):
                v = pt[:, q * CN:q * CN + CN, :] if isinstance(q, int) else pt[:, bass.ds(q * CN, CN), :]
                a(v, v, ACT.Silu).then_inc(R["conv_silu"], 1)

            act.wait_ge(R["ssd_sum"], 5)
            split_loop(act, PHASES["ssd"], split_hi, None, conv_base(scw[:, 3, :], scb, xbc_tile, xbc_silu), 0, 6)
            split_loop(act, PHASES["ssd"], split_hi, None, gate_tiles(4), 6, 10)

            act.wait_ge(R["dt_c"], 1)
            a(dte[0:NH, :], dte[0:NH, :], ACT.Exp).then_inc(R["dt_a"], 1)
            act.wait_ge(R["dt_a"], 1)
            a(dte[0:NH, :], dte[0:NH, :], ACT.Ln, bias=one_col[0:NH, :]).then_inc(R["dt_a"], 1)
            a(acol[0:NH, :], par_of("alog")[0:NH, :], ACT.Exp).then_inc(R["dt_a"], 1)
            act.wait_ge(R["dt_c"], 4)
            a(wendT[0:NH, :], cumT[0:NH, :], ACT.Exp, bias=cumT[0:NH, SEQ - 1:SEQ], scale=-1.0).then_inc(R["dt_a"], 1)
            a(cdT[0:NH, :], dA[0:NH, SEQ:T], ACT.Exp).then_inc(R["dt_a"], 1)

            def head_decay(n):
                act.wait_ge(R["g_arg"], n + 1)
                a(esb[n % 2], esb[n % 2], ACT.Exp).then_inc(R["g_e"], 1)

            for g in range(G):
                act.wait_ge(R["g_bt"], g + 1)
                if g == 0:
                    act.wait_ge(R["z_in"], 16)
                a(btok, aux[1][:, 0:256].rearrange("p (c s) -> p c s", c=2), ACT.Copy).then_inc(R["g_btc"], 1)
                for k in range(8):
                    head_decay(8 * g + k)
                act.wait_ge(R["g_st"], g + 1)
                if g >= 1:
                    act.wait_ge(R["g_out"], 16 * g)
                a(hst, aux[0][:, :].rearrange("p (t s) -> p t s", t=4), ACT.Copy).then_inc(R["g_stc"], 1)
                act.wait_ge(R["g_z"], g + 1)
                a(gsq, pt[:, XS + 4 * g:XS + 4 * g + 4, :], ACT.Square).then_inc(R["g_sq"], 1)
            act.wait_ge(R["g_ssc"], G)
            a(gsum, gsum, ACT.Sqrt).then_inc(R["g_sqrt"], 1)
            act.wait_ge(R["g_n"], XST)
            act.wait_ge(R["g_out"], 16 * G)
            split_loop(act, PHASES["out_ssd"], split_hi, pt[:, XS:XS + XST, :], no_evac)
            norm(2, True)
            ffn(1)
            norm(3, False)

        @block.vector
        def _(dve):
            tt, ts, stt = dve.tensor_tensor, dve.tensor_scalar, dve.scalar_tensor_tensor

            def no_evac(eng, ph, i, pb, q):
                pass

            def residual(ph_name):
                def evac(eng, ph, i, pb, q):
                    for n in range(CN):
                        wait_acc(eng, ph, i, pb, n)
                        t = q * CN + n
                        v = x[:, t, :] if isinstance(t, int) else x[:, bass.ds(t, 1), :].rearrange("p a n -> p (a n)")
                        stt(v, v, ALPHA, acc[n][:, 0:T], ALU.mult, ALU.add).then_inc(drained, 1)
                return evac

            def taps(w, sums, new, tap0, conv0, dst, width, after):
                def evac(eng, ph, i, pb, q):
                    for n in range(CN):
                        ch = q * CN + n
                        one = (lambda v: v[:, ch:ch + 1] if isinstance(ch, int) else v[:, bass.ds(ch, 1)])
                        row = (lambda v: v[:, ch, :] if isinstance(ch, int)
                               else v[:, bass.ds(ch, 1), :].rearrange("p a n -> p (a n)"))
                        eng.wait_ge(R["conv_base"], q * CN + (conv0 + n + 1))
                        y, h = dst(q, n), acc[n]
                        tap = tap0 + n * (width - 2)
                        dve.tensor_copy(row(new), h[:, T - NB - (width - 1):T])
                        tt(y[:, SEQ:T], y[:, SEQ:T], row(sums), ALU.add)
                        for k in range(1, width):
                            if k > 1:
                                eng.wait_ge(R["conv_tap"], q * (CN * (width - 2)) + (tap + k - 1))
                            ins = stt(y[:, k:SEQ], h[:, 0:SEQ - k], one(w[:, width - 1 - k, :]), y[:, k:SEQ],
                                      ALU.mult, ALU.add)
                            ins.then_inc(R["conv_tap"] if k < width - 1 else drained, 1)
                    after(eng, ph, i, pb, q)
                return evac

            dve.memset(small[:, 7:8], 1.0).then_inc(R["ffn_tile"], 1)
            dve.memset(small[:, 0:1], EPS).then_inc(R["small_set"], 1)
            dve.memset(small[:, 1:7], 1.0).then_inc(R["small_set"], 1)
            for n in range(4):
                dve.memset(acc[n][:, :], 0.0).then_inc(drained, 1)
            dve.wait_ge(R["x_hi"], 1)
            tt(xl[:, :, :], x, xh[:, :, :].bitcast(F32), ALU.subtract).then_inc(R["x_lo"], 1)
            split_loop(dve, PHASES["ab"], split_lo, None, no_evac)

            dve.wait_ge(R["att_in"], 16)
            dve.wait_ge(drained, 4 * PHASES["out_ab"].panel0 + 4)
            for m in range(2 * H):
                tile = pt[:, QR + m, :]
                cos, sin = (trig[:, 0, :], trig[:, 1, :]) if m < H else (trig[:, 2, :], trig[:, 3, :])
                t = temps[m % 2][0][:, 0:T]
                dve.wait_ge(R["rot_p"], m + 1)
                tt(t, sin, aux[m % 4][:, 0:T], ALU.mult).then_inc(R["rot_m"], 1)
                tt(tile, tile, cos, ALU.mult).then_inc(R["rot_c"], 1)
                dve.wait_ge(R["rot_m"], m + 1)
                dve.wait_ge(R["rot_c"], m + 1)
                tt(tile, tile, t, ALU.add).then_inc(R["rot_done"], 1)
            dve.wait_ge(R["rot_done"], 2 * H)

            def sb_neg(h, n=384):
                zs, e, _ = temps[h % 2]
                dve.wait_ge(R["sbz_s"], h + 1)
                if h >= 2:
                    dve.wait_ge(R["sb_y"], h - 1)
                stt(e[:, 0:n], zs[:, 0:n], -1.0, zs[:, 0:n], ALU.mult, ALU.min).then_inc(R["sb_na"], 1)

            def sb_fail(h, n=384):
                zs, e, lf = (v[:, 0:n] for v in temps[h % 2])
                dve.wait_ge(R["sb_L"], h + 1)
                stt(lf, zs, 0.0, e, ALU.max, ALU.add).then_inc(R["sb_lf"], 1)
                if h < H:
                    dve.wait_ge(R["sb_lf"], h + 1)
                    tt(lf, lf, mask, ALU.mult).then_inc(R["sb_m"], 1)

            def sb_arg(h, n=384):
                zs, e, _ = (v[:, 0:n] for v in temps[h % 2])
                dve.wait_ge(R["sb_incl"], h + 1)
                tt(e, zs, banks[h % 2][1][:, 0:n], ALU.subtract).then_inc(R["sb_arg"], 1)
                dve.wait_ge(R["sb_arg"], h + 1)
                if h < H:
                    tt(e, e, cap, ALU.min).then_inc(R["sb_cap"], 1)
                else:
                    ts(e, e, 0.0, None, ALU.min).then_inc(R["sb_cap"], 1)

            for t in range(H + 1):
                if t < H:
                    sb_neg(t)
                if t >= 1:
                    sb_arg(t - 1)
                if t < H:
                    sb_fail(t)
            dve.wait_ge(R["page_used"], NB * NPG)
            zs = temps[0][0][:, 0:2 * NB * H]
            v3 = (lambda v: v.rearrange("p (a h) -> p a h", h=H))
            stt(v3(zs), v3(aux[0][:, 0:2 * NB * H]), SCALE,
                par_of("sbias").unsqueeze(1).to_broadcast([P, 2 * NB, H]), ALU.mult, ALU.add).then_inc(R["sbz_s"], 1)
            sb_neg(H, 2 * NB * H)
            sb_fail(H, 2 * NB * H)
            sb_arg(H, 2 * NB * H)
            dve.wait_ge(R["page_used"], 2 * NB * NPG)
            part = temps[1][0][:, 0:NB * H]
            dve.tensor_copy(part, aux[3][:, NB * H:2 * NB * H]).then_inc(R["sb_part"], 1)
            dve.wait_ge(R["sb_part"], 1)
            tt(pt[:, QA:QA + H, SEQ:T], part.rearrange("p (h b) -> p h b", b=NB),
               aux[3][:, 0:NB * H].rearrange("p (h b) -> p h b", b=NB), ALU.add).then_inc(R["sb_ycopy"], 1)

            for t in range(H + 1):
                if t < H:
                    h = t
                    dve.wait_ge(R["rt_s"], h + 1)
                    if h >= 2:
                        dve.wait_ge(R["rt_y"], h - 1)
                    tt(temps[h % 2][2], decay[:, h, :], banks[h % 2][0][:, 0:384], ALU.mult).then_inc(R["rt_p"], 1)
                if t >= 1:
                    h = t - 1
                    dve.wait_ge(R["rt_st"], h + 1)
                    if h == 0:
                        dve.wait_ge(R["page_used"], 2 * NB * NPG)
                    dve.tensor_copy(retp[:, h, :], banks[h % 2][0][:, 0:256]).then_inc(R["rt_stc"], 1)

            def key_of(b):
                if b >= 1:
                    dve.wait_ge(R["rs_o"], 4 * b)
                ts(ktm[0:NB, :], kts[0:NB, :], ident[0:NB, b:b + 1], None, ALU.mult).then_inc(R["rs_km"], 1)

            dve.wait_ge(R["rs_tc"], 1)
            key_of(0)
            for b in range(NB):
                if b + 1 < NB:
                    key_of(b + 1)
                dve.wait_ge(R[f"rs_in{b % 2}"], 16 * (b // 2 + 1))
                for h in range(H):
                    dve.wait_ge(R["rs_o"], 4 * b + h // 2 + 1)
                    s = s0buf[b % 2][:, h, :]
                    stt(s, s, float(GAMMA[h]), obank(h), ALU.mult, ALU.add).then_inc(R["rs_new"], 1)
            dve.wait_ge(R["rs_y"], NB)
            dve.tensor_copy(pt[:, VR:VR + 2 * H, SEQ:T], aux[2][:, 0:2 * H * NB].rearrange("p (t b) -> p t b", b=NB))\
                .then_inc(R["rs_yc"], 1)
            dve.wait_ge(R["rn_sqrt"], H)
            dve.reciprocal(rsum, rsum).then_inc(R["rn_inv"], 1)
            dve.wait_ge(R["rn_inv"], 1)
            for h in range(H):
                v = pt[:, VR + 2 * h:VR + 2 * h + 2, :]
                tt(v, v, rsum[:, h:h + 1, :].to_broadcast([P, 2, T]), ALU.mult).then_inc(R["rn_a"], 1)
            dve.wait_ge(R["rn_a"], H)
            v = pt[:, VR:VR + 2 * H, :]
            tt(v, v, silg, ALU.mult).then_inc(R["rn_b"], 1)

            def norm(l, split):
                dve.wait_ge(drained, ln_after[l])
                by_token = (lambda v: v.rearrange("p t n -> p n t"))
                dve.tensor_reduce(lsum, by_token(x), AX.X, ALU.add).then_inc(R["ln_sum"], 1)
                dve.wait_ge(R["ln_mean"], l + 1)
                stt(x, aux[0][:, 0:T].unsqueeze(1).to_broadcast([P, KT, T]), -1.0 / D, x, ALU.mult, ALU.add)\
                    .then_inc(R["ln_cen"], 1)
                dve.wait_ge(R["ln_sq"], l + 1)
                dve.tensor_reduce(lsum, by_token(lsq), AX.X, ALU.add).then_inc(R["ln_sqsum"], 1)
                dve.wait_ge(R["ln_sqrt"], l + 1)
                dve.reciprocal(lrt, lrt).then_inc(R["ln_rstd"], 1)
                dve.wait_ge(R["ln_rstd"], l + 1)
                tt(x, x, lrt.unsqueeze(1).to_broadcast([P, KT, T]), ALU.mult).then_inc(R["ln_norm"], 1)
                dve.wait_ge(R["ln_norm"], l + 1)
                for t in range(KT // 2, KT):
                    ts(x[:, t, :], x[:, t, :], lng[:, l, t:t + 1], lnb[:, l, t:t + 1], ALU.mult, ALU.add)\
                        .then_inc(R["ln_d"], 1)
                if split:
                    n = {0: 2, 1: 3, 2: 4}[l]
                    dve.wait_ge(R["x_hi"], n)
                    tt(xl[:, :, :], x, xh[:, :, :].bitcast(F32), ALU.subtract).then_inc(R["x_lo"], 1)

            def ffn(layer):
                up, down = PHASES[f"up{layer}"], PHASES[f"down{layer}"]
                dve.wait_ge(R["ffn_state_in"], 16 * (layer + 1))
                for k, o in ((0, fsum), (1, ftmp)):
                    w = fcw[:, layer, k, :].unsqueeze(2).to_broadcast([P, 2 * FT, NB])
                    tt(o, fst[:, :, k, :], w, ALU.mult).then_inc(R["ffn_sum"], 1)
                dve.wait_ge(R["ffn_sum"], 3 * layer + 2)
                tt(fsum, fsum, ftmp, ALU.add).then_inc(R["ffn_sum"], 1)
                dve.wait_ge(R["ffn_sum"], 3 * layer + 3)

                def product(eng, ph, i, pb, q):
                    eng.wait_ge(R["conv_silu"], q + (conv_silu0[layer] + 1))
                    v = pt[:, 2 * q:2 * q + 2, :] if isinstance(q, int) else pt[:, bass.ds(q * 2, 2), :]
                    tt(v, stage[:, 0:2, :], stage[:, 2:4, :], ALU.mult).then_inc(R["ffn_tile"], 1)

                ev = taps(fcw[:, layer], fsum, fnew, tap0[layer], 4 * conv_silu0[layer],
                          lambda q, n: stage[:, n, :], 3, product)
                split_loop(dve, up, split_lo, None, ev)
                dve.wait_ge(R["ffn_tile"], (layer + 1) * (FT // 2) + 1)
                split_loop(dve, down, split_lo, pt, residual("down"))

            dve.wait_ge(R["rn_b"], 1)
            dve.wait_ge(R["x_back"], 16)
            split_loop(dve, PHASES["out_ab"], split_lo, pt, residual("out"))
            norm(0, True)
            ffn(0)
            norm(1, True)

            split_loop(dve, PHASES["dt"], split_lo, None, no_evac)
            dve.wait_ge(R["sconv_in"], 16)
            wb = (lambda k: scw[:, k, :].unsqueeze(2).to_broadcast([P, CT, NB]))
            tt(ssum, sst[:, :, 0, :], wb(0), ALU.mult).then_inc(R["ssd_sum"], 1)
            for k in (1, 2):
                tt(stmp, sst[:, :, k, :], wb(k), ALU.mult).then_inc(R["ssd_sum"], 1)
                dve.wait_ge(R["ssd_sum"], 2 * k)
                tt(ssum, ssum, stmp, ALU.add).then_inc(R["ssd_sum"], 1)
                dve.wait_ge(R["ssd_sum"], 2 * k + 1)

            def xbc_tile(q, n):
                t = q * CN + n
                return pt[:, t, :] if isinstance(t, int) else pt[:, bass.ds(t, 1), :].rearrange("p a n -> p (a n)")

            ssd = PHASES["ssd"]
            ev = taps(scw, ssum, snew, tap0["ssd"], 4 * conv_silu0["ssd"], xbc_tile, 4,
                      lambda *a: None)
            split_loop(dve, ssd, split_lo, None, ev, 0, 6)
            split_loop(dve, ssd, split_lo, None, no_evac, 6, 10)

            dve.wait_ge(used, PHASES["out_ssd"].chunk0)
            dve.wait_ge(R["x_out"], 16)
            dve.wait_ge(drained, 4 * PHASES["out_ssd"].panel0 + 4)
            r = dtraw[:, :]
            stt(dte[0:NH, :], r, -1.0, r, ALU.mult, ALU.min).then_inc(R["dt_c"], 1)
            dve.wait_ge(R["dt_a"], 3)
            stt(dtT[0:NH, :], r, 0.0, dte[0:NH, :], ALU.max, ALU.add).then_inc(R["dt_c"], 1)
            dve.wait_ge(R["dt_c"], 2)
            ts(dA[0:NH, :], dtT[0:NH, :], acol[0:NH, :], -1.0, ALU.mult, ALU.mult).then_inc(R["dt_c"], 1)
            dve.wait_ge(R["dt_c"], 3)
            dve.tensor_tensor_scan(cumT[0:NH, :], one_col[0:NH, :].to_broadcast([NH, SEQ]), dA[0:NH, 0:SEQ], 0.0,
                                   ALU.mult, ALU.add).then_inc(R["dt_c"], 1)
            dve.wait_ge(R["dt_a"], 5)
            tt(wendT[0:NH, :], wendT[0:NH, :], dtT[0:NH, 0:SEQ], ALU.mult).then_inc(R["dt_c"], 1)
            dve.wait_ge(R["sm_t"], 1)
            flat = (lambda v: v.rearrange("p c h -> p (c h)"))
            ts(flat(nctok), aux[0][:, 0:2 * NH], -1.0, None, ALU.mult).then_inc(R["dt_c"], 1)
            dve.tensor_copy(flat(dtok), aux[0][:, 2 * NH:4 * NH])
            dve.tensor_copy(flat(wend), aux[0][:, 4 * NH:6 * NH])
            dve.tensor_copy(dts[0:NB, :], aux[1][0:NB, 0:NH])
            dve.tensor_copy(cds[0:NB, :], aux[1][0:NB, NH:2 * NH]).then_inc(R["dt_c"], 1)
            dve.wait_ge(R["cd_p"], 1)
            dve.tensor_copy(cdbc.rearrange("p b h -> p (b h)"), aux[2][:, :]).then_inc(R["cd_ready"], 1)
            dve.wait_ge(R["dt_c"], 7)
            for q in range(G):
                dve.wait_ge(R["ss_t"], q + 1)
                tt(xds[0:NB, q * 512:q * 512 + 512].rearrange("p (h e) -> p h e", e=HD),
                   dts[0:NB, 8 * q:8 * q + 8].unsqueeze(2).to_broadcast([NB, 8, HD]),
                   acc[q % 4][0:NB, :].rearrange("p (h e) -> p h e", e=HD), ALU.mult).then_inc(R["ss_x"], 1)
            for b in range(NB):
                for g in range(G):
                    u = 2 * b + g // 4
                    dve.wait_ge(R["ss_o"], G * b + g + 1)
                    dve.wait_ge(R["ss_h"], u + 1)
                    v = hbuf[u % NHB][:, (g % 4) * 512:(g % 4) * 512 + 512]
                    stt(v, acc[g % 4][:, :], pt[:, BM + g, SEQ + b:SEQ + b + 1], v, ALU.mult, ALU.add)\
                        .then_inc(R["ss_n"], 1)
            dve.wait_ge(R["ss_y"], 2 * NB)
            xs_s = pt[:, XS:XS + XST, SEQ:T]
            tt(xs_s, xs_s, par_of("dskip").unsqueeze(2).to_broadcast([P, XST, NB]), ALU.mult).then_inc(R["ss_yd"], 1)
            dve.wait_ge(R["ss_yd"], 1)
            tt(xs_s, xs_s, aux[3][:, 0:XST * NB].rearrange("p (t b) -> p t b", b=NB), ALU.add).then_inc(R["ss_ya"], 1)

            dskip, normw = par_of("dskip"), par_of("normw")
            dve.wait_ge(R["mask_in"], 16)
            dve.wait_ge(R["z_in"], 16)

            def pair_out(n):
                dve.wait_ge(R["g_yh"], 2 * n + 2)
                v = pt[:, XS + n, 0:SEQ]
                stt(v, v, dskip[:, n:n + 1], aux[2 + n % 2][:, 0:SEQ], ALU.mult, ALU.add).then_inc(R["g_yd"], 1)

            def exponent(n):
                dve.wait_ge(R["g_bc"], n // 2 + 1)
                if n >= 2:
                    dve.wait_ge(R["g_w"], n - 1)
                bk, o, e = acc[2 + (n // 2) % 2], (n % 2) * 256, esb[n % 2]
                ts(e[:, 0:256], bk[:, o:o + 256], nctok[:, 0, n:n + 1], 0.0, ALU.add, ALU.min)
                ts(e[:, 256:384], bk[:, o + 128:o + 256], nctok[:, 1, n:n + 1], 0.0, ALU.add, ALU.min)\
                    .then_inc(R["g_arg"], 1)

            for g in range(G):
                dve.wait_ge(R["g_cb"], g + 1)
                tt(cbm, smask, aux[0][:, 0:384], ALU.mult).then_inc(R["g_cbm"], 1)
                for c in range(2):
                    dve.wait_ge(R["g_xt"], 2 * g + c + 1)
                    src = acc[c][:, :].rearrange("p (h e) -> p h e", e=HD)
                    for o, f in ((xdt, dtok), (xw, wend)):
                        ins = tt(o[:, c, :].rearrange("p (h e) -> p h e", e=HD),
                                 f[:, c, 8 * g:8 * g + 8].unsqueeze(2).to_broadcast([P, 8, HD]), src, ALU.mult)
                ins.then_inc(R["g_x"], 1)
                dve.wait_ge(R["g_cbm"], g + 1)
                exponent(8 * g)
                for k in range(8):
                    n = 8 * g + k
                    if k < 7:
                        exponent(n + 1)
                    dve.wait_ge(R["g_e"], n + 1)
                    if n >= 2:
                        dve.wait_ge(R["g_yh"], n - 1)
                    tt(wsb[n % 2], esb[n % 2], cbm, ALU.mult).then_inc(R["g_w"], 1)
                    if k % 2 == 1 and k >= 3:
                        pair_out(n // 2 - 1)
                pair_out(4 * g + 3)
                dve.wait_ge(R["z_in"], 16 * (g + 1))
                dve.wait_ge(R["g_yd"], 4 * g + 4)
                v = pt[:, XS + 4 * g:XS + 4 * g + 4, :]
                tt(v, v, zg, ALU.mult).then_inc(R["g_z"], 1)
                dve.wait_ge(R["g_ss"], g + 1)
                ts(gsum[:, g, :], aux[1][:, 0:T], 1.0 / 512, EPS, ALU.mult, ALU.add).then_inc(R["g_ssc"], 1)
            dve.wait_ge(R["g_sqrt"], 1)
            dve.reciprocal(gsum, gsum).then_inc(R["g_inv"], 1)
            dve.wait_ge(R["g_inv"], 1)
            for t in range(XST):
                v = pt[:, XS + t, :]
                stt(v, v, normw[:, t:t + 1], gsum[:, t // 4, :], ALU.mult, ALU.mult).then_inc(R["g_n"], 1)
            dve.wait_ge(R["g_n"], XST)
            dve.wait_ge(R["x_back"], 32)
            split_loop(dve, PHASES["out_ssd"], split_lo, pt[:, XS:XS + XST, :], residual("out"))
            norm(2, True)
            ffn(1)
            norm(3, False)

        @block.tensor
        def _(pe):
            mm = pe.matmul

            def turn(out, src):
                k = src.shape[0]
                return pe.transpose(out, src, ident[0:k, 0:k])

            pe.wait_ge(R["consts_in"], 32)
            pe.wait_ge(R["x_lo"], 1)
            products(pe, PHASES["ab"])

            pe.wait_ge(drained, 4 * PHASES["out_ab"].panel0 + 4)
            pe.wait_ge(R["att_in"], 16)
            for m in range(2 * H):
                if m >= 4:
                    pe.wait_ge(R["rot_m"], m - 3)
                mm(aux[m % 4][:, 0:T], rot, pt[:, QR + m, :], start=True, stop=True).then_inc(R["rot_p"], 1)

            def sb_scores(h):
                bk = banks[h % 2]
                k, q, v = pt[:, KA + h, :], pt[:, QA + h, :], pt[:, VA + h, :]
                if h >= 2:
                    pe.wait_ge(R["sbz_s"], h - 1)
                    pe.wait_ge(R["sb_vs"], h - 1)
                mm(bk[0][:, 0:256], k[:, 0:P], q[:, 0:SEQ], start=True, stop=True)
                mm(bk[0][:, 256:384], k[:, P:SEQ], q[:, P:SEQ], start=True, stop=True).then_inc(R["sbz"], 1)
                turn(bk[2][:, 0:P], v[:, 0:P])
                turn(bk[2][:, P:SEQ], v[:, P:SEQ]).then_inc(R["sb_vt"], 1)

            def sb_sum(h):
                bk, lf = banks[h % 2], temps[h % 2][2]
                pe.wait_ge(R["sb_m"], h + 1)
                if h >= 2:
                    pe.wait_ge(R["sb_arg"], h - 1)
                mm(bk[1][:, 0:384], upper, lf, start=True, stop=False)
                mm(bk[1][:, P:SEQ], ones, lf[:, 256:384], start=False, stop=True).then_inc(R["sb_incl"], 1)

            def sb_out(h):
                bk, w, v = banks[h % 2], temps[h % 2][1], vtok[h % 2][:, 0, :]
                pe.wait_ge(R["sb_w"], h + 1)
                pe.wait_ge(R["sb_vs"], h + 1)
                if h >= 2:
                    pe.wait_ge(R["sb_ycopy"], h - 1)
                mm(bk[3][:, 0:SEQ], v[:, 0:P], w[:, 0:SEQ], start=True, stop=False)
                mm(bk[3][:, P:SEQ], v[:, P:SEQ], w[:, 256:384], start=False, stop=True).then_inc(R["sb_y"], 1)

            pe.wait_ge(R["rot_done"], 2 * H)
            for t in range(H + 2):
                if t < H:
                    sb_scores(t)
                if 1 <= t <= H:
                    sb_sum(t - 1)
                if t >= 2:
                    sb_out(t - 2)

            def page_at(n):
                pe.wait_ge(R[f"page_in{n % NPB}"], 16 * (n // NPB + 1))
                return page[n % NPB]

            pe.wait_ge(R["sb_ycopy"], H)
            n = 0
            for b in range(NB):
                for k in range(NPG):
                    pg = page_at(n)
                    for h in range(H):
                        c = k * NB * H + b * H + h
                        m = mm(aux[0][:, c:c + 1], pg[:, h, :], pt[:, QA + h, SEQ + b:SEQ + b + 1],
                               start=True, stop=True)
                    m.then_inc(R["page_used"], 1)
                    n += 1
            w = NB * H
            lf = temps[0][2]
            pe.wait_ge(R["sb_lf"], H + 1)
            mm(aux[1][:, 0:2 * w], upper, lf[:, 0:2 * w], start=True, stop=False)
            mm(aux[1][:, 0:w], ones, lf[:, w:2 * w], start=False, stop=True).then_inc(R["sb_incl"], 1)
            pe.wait_ge(R["sb_w"], H + 1)
            for b in range(NB):
                for k in range(NPG):
                    pg = page_at(n)
                    for h in range(H):
                        c = k * w + b * H + h
                        o = k * w + h * NB + b
                        m = mm(aux[3][:, o:o + 1], pg[:, h, :], temps[0][1][:, c:c + 1], start=True, stop=True)
                    m.then_inc(R["page_used"], 1)
                    n += 1

            def ret_scores(h):
                bk = banks[h % 2]
                k, q = pt[:, KR + h, :], pt[:, QR + h, :]
                if h >= 2:
                    pe.wait_ge(R["rt_stc"], h - 1)
                    pe.wait_ge(R["rt_k"], h - 1)
                mm(bk[0][:, 0:256], k[:, 0:P], q[:, 0:SEQ], start=True, stop=True)
                mm(bk[0][:, 256:384], k[:, P:SEQ], q[:, P:SEQ], start=True, stop=True).then_inc(R["rt_s"], 1)
                for c in range(2):
                    turn(bk[1][:, c * P:c * P + P], k[:, c * P:c * P + P])
                    for u in range(2):
                        m = turn(bk[2][:, c * 256 + u * P:c * 256 + u * P + P], pt[:, VR + 2 * h + u, c * P:c * P + P])
                m.then_inc(R["rt_t"], 1)

            def ret_out(h):
                bk, w, v, k = banks[h % 2], temps[h % 2][2], vtok[h % 2], ktw[h % 2]
                pe.wait_ge(R["rt_p"], h + 1)
                pe.wait_ge(R["rt_k"], h + 1)
                if h >= 2:
                    pe.wait_ge(R["rt_yc"], h - 1)
                for u in range(2):
                    o = u * 256
                    mm(bk[3][:, o:o + 256], v[:, 0, u * P:u * P + P], w[:, 0:SEQ], start=True, stop=False)
                    m = mm(bk[3][:, o + P:o + 256], v[:, 1, u * P:u * P + P], w[:, 256:384], start=False, stop=True)
                m.then_inc(R["rt_y"], 1)
                mm(bk[0][:, 0:256], k[:, 0, :], v[:, 0, :], start=True, stop=False)
                mm(bk[0][:, 0:256], k[:, 1, :], v[:, 1, :], start=False, stop=True).then_inc(R["rt_st"], 1)

            pe.wait_ge(R["sb_ycopy"], H + 1)
            for t in range(H + 1):
                if t < H:
                    ret_scores(t)
                if t >= 1:
                    ret_out(t - 1)
            pe.wait_ge(R["rt_yc"], H)
            pe.wait_ge(R["rt_stc"], H)
            for h in range(H):
                turn(aux[h // 4][0:NB, (h % 4) * P:(h % 4) * P + P], pt[:, KR + h, SEQ:T])
            for t in range(2 * H):
                m = turn(acc[t // 4][0:NB, (t % 4) * P:(t % 4) * P + P], pt[:, VR + t, SEQ:T])
            m.then_inc(R["rs_t"], 1)

            def ret_outer(b):
                pe.wait_ge(R["rs_km"], b + 1)
                for h in range(H):
                    if b >= 1 and h % 2 == 0:
                        pe.wait_ge(R["rs_new"], H * (b - 1) + h + 2)
                    m = mm(obank(h), ktm[0:NB, h * P:h * P + P], vts[0:NB, h * 256:h * 256 + 256],
                           start=True, stop=True)
                    if h % 2 == 1:
                        m.then_inc(R["rs_o"], 1)

            def ret_read(b):
                pe.wait_ge(R["rs_new"], H * (b + 1))
                for h in range(H):
                    for u in range(2):
                        c = (2 * h + u) * NB + b
                        m = mm(aux[2][:, c:c + 1], s0buf[b % 2][:, h, u * P:u * P + P],
                               pt[:, QR + h, SEQ + b:SEQ + b + 1], start=True, stop=True)
                m.then_inc(R["rs_y"], 1)

            ret_outer(0)
            for b in range(NB):
                if b + 1 < NB:
                    ret_outer(b + 1)
                ret_read(b)
            for h in range(H):
                pe.wait_ge(R["rn_sq"], h + 1)
                if h >= 2:
                    pe.wait_ge(R["rn_sqrt"], h - 1)
                for u in range(2):
                    m = mm(aux[h % 2][:, 0:T], ones, rsq[:, h % 2, u, :], start=u == 0, stop=u == 1)
                m.then_inc(R["rn_sum"], 1)

            def norm(l):
                pe.wait_ge(R["ln_sum"], l + 1)
                mm(aux[0][:, 0:T], ones, lsum, start=True, stop=True).then_inc(R["ln_mean"], 1)
                pe.wait_ge(R["ln_sqsum"], l + 1)
                mm(aux[1][:, 0:T], ones, lsum, start=True, stop=True).then_inc(R["ln_var"], 1)

            products(pe, PHASES["out_ab"])
            norm(0)
            pe.wait_ge(R["x_lo"], 2)
            products(pe, PHASES["up0"])
            products(pe, PHASES["down0"])
            norm(1)
            pe.wait_ge(R["x_lo"], 3)

            dt = PHASES["dt"]
            pe.wait_ge(lo_done, dt.chunk0 + 1)
            pe.wait_ge(drained, dt.panel0 * 4 + 1)
            for k in range(KT):
                w = slice(k * P, k * P + P)
                mm(acc[0][:, 0:T], hi[:, 0, w], xh[:, k, :], start=k == 0, stop=False)
                mm(acc[0][:, 0:T], hi[:, 0, w], xl[:, k, :], start=False, stop=False)
                m = mm(acc[0][:, 0:T], lo[:, 0, w], xh[:, k, :], start=False, stop=k == KT - 1)
            m.then_inc(used, 1)
            products(pe, PHASES["ssd"])

            pe.wait_ge(R["dt_c"], 5)
            for c in range(2):
                s = slice(c * P, c * P + P)
                for k, v in enumerate((cumT, dtT, wendT)):
                    turn(aux[0][:, (2 * k + c) * NH:(2 * k + c) * NH + NH], v[0:NH, s])
            turn(aux[1][0:NB, 0:NH], dtT[0:NH, SEQ:T])
            turn(aux[1][0:NB, NH:2 * NH], cdT[0:NH, :]).then_inc(R["sm_t"], 1)
            pe.wait_ge(R["dt_c"], 7)
            for b in range(NB):
                m = mm(aux[2][:, b * NH:b * NH + NH], row_of(b, NB), cds[0:NB, :], start=True, stop=True)
            m.then_inc(R["cd_p"], 1)
            for q in range(G):
                if q >= 4:
                    pe.wait_ge(R["ss_x"], q - 3)
                for t in range(4):
                    m = turn(acc[q % 4][0:NB, t * P:t * P + P], pt[:, XS + 4 * q + t, SEQ:T])
                m.then_inc(R["ss_t"], 1)
            pe.wait_ge(R["ss_x"], G)

            def spread(n):
                b, g = n // G, n % G
                if n >= 4:
                    pe.wait_ge(R["ss_n"], n - 3)
                mm(acc[g % 4][:, :], row_of(b, NB), xds[0:NB, g * 512:g * 512 + 512], start=True, stop=True)\
                    .then_inc(R["ss_o"], 1)

            def read_state(n):
                b, g = n // G, n % G
                u = 2 * b + g // 4
                pe.wait_ge(R["ss_n"], n + 1)
                for t in range(4):
                    c = (4 * g + t) * NB + b
                    o = (g % 4) * 512 + t * P
                    m = mm(aux[3][:, c:c + 1], hbuf[u % NHB][:, o:o + P], pt[:, CM + g, SEQ + b:SEQ + b + 1],
                           start=True, stop=True)
                if g % 4 == 3:
                    m.then_inc(R["ss_y"], 1)

            for n in range(NB * G + 3):
                if n < NB * G:
                    spread(n)
                if n >= 3:
                    read_state(n - 3)

            pe.wait_ge(R["ss_ya"], 1)
            for g in range(G):
                bm, cm = pt[:, BM + g, :], pt[:, CM + g, :]
                if g >= 1:
                    pe.wait_ge(R["g_stc"], g)
                mm(aux[0][:, 0:256], bm[:, 0:P], cm[:, 0:SEQ], start=True, stop=True)
                mm(aux[0][:, 256:384], bm[:, P:SEQ], cm[:, P:SEQ], start=True, stop=True).then_inc(R["g_cb"], 1)
                if g >= 1:
                    pe.wait_ge(R["g_ssc"], g)
                for c in range(2):
                    m = turn(aux[1][:, c * P:c * P + P], bm[:, c * P:c * P + P])
                m.then_inc(R["g_bt"], 1)
                for c in range(2):
                    for t in range(4):
                        m = turn(acc[c][:, t * P:t * P + P], pt[:, XS + 4 * g + t, c * P:c * P + P])
                    m.then_inc(R["g_xt"], 1)

                def decays(q):
                    n = 4 * g + q
                    if n >= 2:
                        pe.wait_ge(R["g_arg"], 2 * (n - 1))
                    for k in range(2):
                        m = mm(acc[2 + n % 2][:, k * 256:k * 256 + 256], row_of(2 * n + k, NH), cumT[0:NH, :],
                               start=True, stop=True)
                    m.then_inc(R["g_bc"], 1)

                decays(0)
                for q in range(4):
                    if q < 3:
                        decays(q + 1)
                    n = 4 * g + q
                    if n >= 2:
                        pe.wait_ge(R["g_yd"], n - 1)
                    if q == 0:
                        pe.wait_ge(R["g_x"], g + 1)
                    for k in range(2):
                        h = 2 * n + k
                        pe.wait_ge(R["g_w"], h + 1)
                        o = (2 * q + k) * HD
                        y = aux[2 + n % 2][k * HD:k * HD + HD, :]
                        mm(y[:, 0:SEQ], xdt[:, 0, o:o + HD], wsb[h % 2][:, 0:SEQ], start=True, stop=False)
                        m = mm(y[:, P:SEQ], xdt[:, 1, o:o + HD], wsb[h % 2][:, 256:384], start=False, stop=True)
                        m.then_inc(R["g_yh"], 1)
                pe.wait_ge(R["g_btc"], g + 1)
                for t in range(4):
                    o = slice(t * P, t * P + P)
                    mm(aux[0][:, o], xw[:, 0, o], btok[:, 0, :], start=True, stop=False)
                    m = mm(aux[0][:, o], xw[:, 1, o], btok[:, 1, :], start=False, stop=True)
                m.then_inc(R["g_st"], 1)
                pe.wait_ge(R["g_sq"], g + 1)
                for t in range(4):
                    m = mm(aux[1][:, 0:T], ones, gsq[:, t, :], start=t == 0, stop=t == 3)
                m.then_inc(R["g_ss"], 1)

            products(pe, PHASES["out_ssd"])
            norm(2)
            pe.wait_ge(R["x_lo"], 4)
            products(pe, PHASES["up1"])
            products(pe, PHASES["down1"])
            norm(3)





def feature_major(a, axis=-1):
    a = np.moveaxis(np.asarray(a), axis, 0)
    return np.ascontiguousarray(np.moveaxis(a.reshape((-1, P) + a.shape[1:]), 1, 0))


def chunks(w, panels_of, kc):
    k, n = w.shape
    v = w.reshape(k // (CK * P), CK, P, n // (CN * P), CN * P)
    return v.transpose(3, 0, 2, 1, 4).reshape(-1, P, CW)


def kernel(**inputs):
    import concourse.bacc as bacc
    from concourse.bass_utils import run_bass_kernel_spmd

    g = {k: np.asarray(v) for k, v in inputs.items()}
    f32 = np.float32

    xp = np.concatenate([g["x_prompt"][0], g["x_sample"][:, 0]], 0)
    w_ab = g["w_in_ab"][0]
    cut = [0, 1024, 2048, 3072, 4096, 5120, 7168, 9216]
    qa, ka, va, qr, kr, vr, gr = (w_ab[:, a:b] for a, b in zip(cut, cut[1:]))
    w_ab = np.concatenate([qa, vr, ka, va, qr, kr, gr], 1)
    w_ssd = g["w_in_ssd"][0]
    w_z, w_xs, w_b, w_c, w_dt = (w_ssd[:, a:b] for a, b in ((0, 4096), (4096, 8192), (8192, 9216),
                                                            (9216, 10240), (10240, 10304)))
    dt_w = np.zeros((D, P), f32)
    dt_w[:, 0:NH] = w_dt
    pairs = np.arange(2 * FT).reshape(2, FT // 2, 2).transpose(1, 0, 2).reshape(-1)

    def by_pairs(a):
        v = a.reshape(a.shape[:-1] + (2 * FT, P))
        return v[..., pairs, :].reshape(a.shape)

    w = [chunks(w_ab, 18, 4), chunks(g["w_out_ab"][0], 4, 6)]
    for layer in range(DEPTH):
        if layer:
            w += [dt_w.reshape(KT, P, P).transpose(1, 0, 2).reshape(1, P, CW),
                  chunks(np.concatenate([w_b, w_c, w_xs, w_z], 1), 20, 4), chunks(g["w_out_ssd"][0], 4, 8)]
        w += [chunks(by_pairs(g["w_up"][layer]), 22, 4), chunks(g["w_down"][layer], 4, 11)]
    w = np.concatenate(w, 0)

    param = np.zeros((P, PARAM_W), f32)

    def put(name, a, rows=P):
        param[0:rows, PARAM[name][0]:PARAM[name][1]] = a.reshape(rows, -1)

    ln_g = np.stack([g["ln1_g"][0], g["ln2_g"][0], g["ln1_g"][1], g["ln2_g"][1]])
    ln_b = np.stack([g["ln1_b"][0], g["ln2_b"][0], g["ln1_b"][1], g["ln2_b"][1]])
    put("lng", ln_g.reshape(4, KT, P).transpose(2, 0, 1))
    put("lnb", ln_b.reshape(4, KT, P).transpose(2, 0, 1))
    put("sbias", np.broadcast_to(g["sb_bias"][0][None], (P, H)))
    put("fcw", by_pairs(g["conv_w_ffn"]).reshape(DEPTH, 3, 2 * FT, P).transpose(3, 0, 1, 2))
    put("fcb", by_pairs(g["conv_b_ffn"]).reshape(DEPTH, 2 * FT, P).transpose(2, 0, 1))

    def bcx(a):
        return np.concatenate([a[..., SSM_IN:], a[..., :SSM_IN]], -1)

    put("scw", bcx(g["conv_w_ssd"][0]).reshape(4, CT, P).transpose(2, 0, 1))
    put("scb", bcx(g["conv_b_ssd"][0]).reshape(CT, P).T)
    put("dskip", np.repeat(g["d_skip"][0], HD).reshape(XST, P).T)
    put("normw", g["norm_w_ssd"][0].reshape(XST, P).T)
    put("dtb", g["dt_bias"][0], NH)
    put("alog", g["a_log"][0], NH)

    arrays = {
        "x": xp.T.reshape(KT, P, T).transpose(1, 0, 2).reshape(P, KT * T),
        "w": w, "const": constants(), "param": param,
        "pages": g["page_table"].reshape(1, -1),
        "ck": g["cache_k"][0].transpose(0, 3, 2, 1),
        "cv": g["cache_v"][0],
        "ret0": g["state_ret"][0].transpose(0, 2, 1, 3).reshape(NB, P, H * 256),
        "ssm0": g["state_ssm"][0].transpose(0, 3, 1, 2).reshape(NB, P, SSM_IN),
        "sst": bcx(g["state_ssm_conv"][0]).reshape(NB, 3, CT, P).transpose(3, 2, 1, 0),
        "fst": by_pairs(g["state_ffn_conv"]).reshape(DEPTH, NB, 2, 2 * FT, P).transpose(0, 4, 3, 2, 1),
    }
    arrays = {k: np.ascontiguousarray(v) for k, v in arrays.items()}

    nc = bacc.Bacc("TRN2", target_bir_lowering=False, num_devices=1)
    d = {k: nc.dram_tensor(f"in_{k}", v.shape, mybir.dt.from_np(v.dtype), kind="ExternalInput").ap()
         for k, v in arrays.items()}
    for k, shape in OUT_SHAPES.items():
        d[k] = nc.dram_tensor(f"out_{k}", shape, F32, kind="ExternalOutput").ap()
    d["gate"] = nc.dram_tensor("gate", (P, XST, T), F32, kind="Internal").ap()
    d["xsave"] = nc.dram_tensor("xsave", (P, KT * T), F32, kind="Internal").ap()
    d["y"] = d["y"].rearrange("p t n -> p (t n)")
    build(nc, d)
    r = run_bass_kernel_spmd(nc, [{f"in_{k}": v for k, v in arrays.items()}], core_ids=[0]).results[0]
    o = {k: r[f"out_{k}"].reshape(s) for k, s in OUT_SHAPES.items()}

    def tokens(a):
        return a.transpose(2, 1, 0).reshape(a.shape[2], -1)

    y = tokens(o["y"])
    k, v = tokens(o["kv"][:, 0:H]), tokens(o["kv"][:, H:])
    back = np.argsort(pairs)

    def channels(a, undo):
        return np.moveaxis(a[:, undo], (1, 0), (-2, -1)).reshape(a.shape[2:] + (-1,))

    xbc = np.concatenate([np.arange(2 * G, CT), np.arange(2 * G)])
    sc, so = channels(o["sconv"], xbc), channels(o["sconv_old"], xbc)
    fc = np.stack([channels(o["fconv"][l], back) for l in range(DEPTH)])
    fo = np.stack([channels(o["fconv_old"][l], back) for l in range(DEPTH)])
    out = (
        y[None, 0:SEQ], y[SEQ:, None],
        k[None, None, 0:SEQ].reshape(1, 1, SEQ, H, P), v[0:SEQ].reshape(1, 1, SEQ, H, P),
        k[SEQ:].reshape(1, NB, 1, H, P), v[SEQ:].reshape(1, NB, 1, H, P),
        o["retp"].transpose(1, 0, 2)[None, None],
        o["rets"].reshape(NB, P, H, 256).transpose(0, 2, 1, 3)[None],
        o["ssmp"].transpose(1, 0, 2).reshape(1, 1, NH, HD, P),
        o["ssms"].reshape(NB, P, NH, HD).transpose(0, 2, 3, 1)[None],
        sc[None, None, 0:3],
        np.stack([so[0], so[1], sc[3:]], 1)[None],
        fc[:, None, 0:2],
        np.stack([fo, fc[:, 2:]], 2),
    )
    return tuple(np.ascontiguousarray(a) for a in out)
```

```python
from contextlib import ExitStack
import math

import numpy as np
import concourse.bass as bass
from concourse import mybir

F32 = mybir.dt.float32
F32R = mybir.dt.float32r
I32 = mybir.dt.int32
ALU = mybir.AluOpType
ACT = mybir.ActivationFunctionType
AX = mybir.AxisListType

P = 128
D = 2048
SEQ = 256
NB = 8
T = SEQ + NB
KT = D // P
H = 8
DEPTH = 2
PAST = 256
PAGE = 128
NPG = PAST // PAGE
NPHYS = 20
FF = 11 * D // 4
FT = FF // P
SSM_IN = 2 * D
XST = SSM_IN // P
G = 8
CT = XST + 2 * G
NH = 64
HD = 64
ALPHA = float((2 * DEPTH) ** 0.25)
EPS = 1e-5
SCALE = float(128 ** -0.5)
GAMMA = [1.0 - 2.0 ** (-5.0 - h) for h in range(H)]

QA, VR, KA, VA, QR, KR = 0, 8, 24, 32, 40, 48
AB_TILES = 56
BM, CM, XS = 0, 8, 16

CK = 4
CN = 4
CW = CK * CN * P
NRAW = 6
NHI = 4
LOOK = 2


def raw_slot(j, body):
    return NRAW - 1 if body == 1 else (0, 1, 2, 3, 0, 1, 4, 5)[j] if body == 8 else j % NRAW


def hi_slot(j, body):
    return NHI - 1 if body == 1 else j % NHI


class Step:

    def __init__(self, base, reg=None):
        self.base, self.reg = base, reg

    def at(self, times, plus):
        fixed = self.base * times + plus
        return fixed if self.reg is None else self.reg * times + fixed

    def next(self):
        return Step(self.base + 1, self.reg)


class Phase:

    def __init__(self, name, iters, panels, kc, ring):
        self.name, self.iters, self.panels, self.kc, self.ring = name, iters, panels, kc, ring
        self.body = panels * kc

    def place(self, before):
        self.chunk0, self.panel0, self.acc0 = before


def plan():
    phases = [
        Phase("ab", 9, 2, 4, False), Phase("out_ab", 2, 2, 6, True),
        Phase("up0", 11, 2, 4, False), Phase("down0", 4, 1, 11, True),
        Phase("dt", 1, 1, 1, False), Phase("ssd", 10, 2, 4, False), Phase("out_ssd", 4, 1, 8, True),
        Phase("up1", 11, 2, 4, False), Phase("down1", 4, 1, 11, True),
    ]
    c = p = a = 0
    raw, hi = [], []
    for ph in phases:
        ph.place((c, p, a))
        c += ph.iters * ph.body
        p += ph.iters * ph.panels
        a += 0 if ph.name == "dt" else 3 * ph.iters * ph.panels
        for _ in range(ph.iters):
            raw += [raw_slot(j, ph.body) for j in range(ph.body)]
            hi += [hi_slot(j, ph.body) for j in range(ph.body)]
    uses = []
    count = [0] * NRAW
    for s in raw:
        count[s] += 1
        uses.append(count[s])

    def previous(slots):
        last, out = {}, []
        for n, s in enumerate(slots):
            out.append(last.get(s, -1))
            last[s] = n
        return out

    return {ph.name: ph for ph in phases}, phases, c, uses, previous(raw), previous(hi)


PHASES, ORDER, CHUNKS, USES, RAW_PREV, HI_PREV = plan()

CONST = {}


def const_layout():
    at = 0
    for name, width in (("ident", P), ("ones", P), ("upper", P), ("rot", P), ("mask", 384), ("cap", 384),
                        ("cosq", T), ("sinq", T), ("cosk", T), ("sink", T), ("decay", H * 384),
                        ("tend", 2 * H), ("mask2", 384), ("pick", 15)):
        CONST[name] = (at, at + width)
        at += width
    return at


CONST_W = const_layout()


def constants():
    c = np.zeros((P, CONST_W), np.float32)

    def put(name, a):
        c[:, CONST[name][0]:CONST[name][1]] = a

    j = np.arange(P)
    put("ident", np.eye(P))
    put("ones", np.ones((P, P)))
    put("upper", (j[:, None] >= j[None, :]))
    rot = np.zeros((P, P))
    for m in range(64):
        rot[m + 64, m] = -1.0
        rot[m, m + 64] = 1.0
    put("rot", rot)
    key = np.concatenate([np.tile(j[:, None], (1, 256)), np.tile(j[:, None] + 128, (1, 128))], 1)
    query = np.concatenate([np.arange(256), np.arange(128, 256)])[None, :]
    put("mask", key < query)
    put("mask2", key <= query)
    put("pick", np.tile(np.arange(15) == 7, (P, 1)))
    put("cap", np.where(key < query, 0.0, -1e30))
    half = 64
    inv = (np.float32(10000.0) ** (-np.linspace(0.0, 1.0, half, dtype=np.float32))).astype(np.float32)
    pos = np.concatenate([np.arange(SEQ), np.full(NB, PAST)]).astype(np.float32)
    ang = (pos[None, :] * inv[:, None]).astype(np.float32)
    cos, sin = np.cos(ang, dtype=np.float32), np.sin(ang, dtype=np.float32)
    cos, sin = np.concatenate([cos, cos]), np.concatenate([sin, sin])
    put("cosq", cos)
    put("sinq", sin)
    put("cosk", cos * np.float32(SCALE))
    put("sink", sin * np.float32(SCALE))
    gap = (query - key).astype(np.float64)
    put("decay", np.concatenate([np.where(gap >= 0, g ** np.maximum(gap, 0), 0.0) for g in GAMMA], 1))
    put("tend", np.stack([g ** (255.0 - (ch * 128 + j)) for g in GAMMA for ch in range(2)], 1))
    return c


PARAM = {}


def param_layout():
    at = 0
    for name, width in (("lng", 4 * KT), ("lnb", 4 * KT), ("sbias", H), ("fcw", DEPTH * 3 * 2 * FT),
                        ("fcb", DEPTH * 2 * FT), ("scw", 4 * CT), ("scb", CT), ("dskip", XST),
                        ("normw", XST), ("dtb", 1), ("alog", 1)):
        PARAM[name] = (at, at + width)
        at += width
    return at


PARAM_W = param_layout()
OUT_SHAPES = {
    "y": (P, KT, T), "kv": (P, 2 * H, T), "retp": (P, H, 256), "rets": (NB, P, H * 256),
    "ssmp": (P, XST, P), "ssms": (NB, P, SSM_IN),
    "sconv": (P, CT, 11), "sconv_old": (P, CT, 2, NB), "fconv": (DEPTH, P, 2 * FT, 10),
    "fconv_old": (DEPTH, P, 2 * FT, NB),
}


SIGNALS = (
    "att_in", "cd_p", "cd_ready", "consts_in", "conv_base", "conv_silu", "conv_tap", "dt_a", "dt_c", "ffn_out",
    "ffn_state_in", "ffn_sum", "ffn_tile", "g_arg", "g_bc", "g_bt", "g_btc", "g_cb", "g_cbm", "g_e", "g_inv",
    "g_n", "g_out", "g_sq", "g_sqrt", "g_ss", "g_ssc", "g_st", "g_stc", "g_w", "g_x", "g_xt", "g_yd", "g_yh",
    "g_z", "gate_in", "gate_out", "kv_out", "ln_a", "ln_cen", "ln_d", "ln_mean", "ln_norm", "ln_rstd", "ln_sq",
    "ln_sqrt", "ln_sqsum", "ln_sum", "ln_var", "mask_in", "page_in0", "page_in1", "page_in2", "page_used",
    "pages_in", "rn_a", "rn_b", "rn_bc", "rn_inv", "rn_sq", "rn_sqrt", "rn_sum", "rot_c", "rot_done", "rot_m",
    "rot_p", "rs_in0", "rs_in1", "rs_in2", "rs_in3", "rs_in4", "rs_km", "rs_new", "rs_o", "rs_out0", "rs_out1",
    "rs_out2", "rs_out3", "rs_out4", "rs_t", "rs_tc", "rs_y", "rs_yc", "rt_k", "rt_out", "rt_p", "rt_s",
    "rt_st", "rt_stc", "rt_t", "rt_v", "rt_y", "rt_yc", "sb_L", "sb_arg", "sb_cap", "sb_e", "sb_incl", "sb_lf",
    "sb_m", "sb_na", "sb_part", "sb_vs", "sb_vt", "sb_w", "sb_y", "sb_ycopy", "sbz", "sbz_s", "sconv_in",
    "sconv_out", "sm_t", "small_set", "ss_h", "ss_in0", "ss_in1", "ss_in2", "ss_n", "ss_o", "ss_out0",
    "ss_out1", "ss_out2", "ss_t", "ss_x", "ss_y", "ss_ya", "ss_yd", "ssd_sum", "x_back", "x_hi", "x_in",
    "x_lo", "x_out", "y_out", "z_in",
)


def build(nc, d):
    ctx = ExitStack()

    def sb(name, shape, dt=F32):
        return ctx.enter_context(nc.sbuf_tensor(name, shape, dt))

    def sem(name):
        return ctx.enter_context(nc.semaphore(name))

    with ctx:
        NHB = 3
        NRB = 5
        with nc.sbuf_tensor("lo", [P, NRAW, CW], F32R) as lo:
            pass
        raw = sb("raw", [P, NRAW, CW])
        with nc.sbuf_tensor("work", [P, 3 * KT * T], F32) as work:
            pass
        x_ = sb("x", [P, KT * T])
        xh = sb("xh", [P, KT, T], F32R)
        xl = sb("xl", [P, KT, T], F32R)
        pj = sb("pj", [P, AB_TILES * T])
        hi = sb("hi", [P, NHI, CW], F32R)
        cons = sb("cons", [P, 2 * P])
        pick = sb("pick", [P, 15])
        par = sb("par", [P, PARAM_W])
        stage = sb("stage", [P, CN, T])
        small = sb("small", [P, 8])
        dtraw = sb("dtraw", [NH, T])
        lsum = sb("lsum", [P, T])
        pages_sb = sb("pages", [1, NB * NPG], I32)
        x = x_[:, :].rearrange("p (t n) -> p t n", n=T)
        pt = pj[:, :].rearrange("p (t n) -> p t n", n=T)
        ident, ones = cons[:, 0:P], cons[:, P:2 * P]
        eps_col, one_col = small[:, 0:1], small[:, 1:2]

        def par_of(name):
            return par[:, PARAM[name][0]:PARAM[name][1]]

        lng = par_of("lng").rearrange("p (l t) -> p l t", t=KT)
        lnb = par_of("lnb").rearrange("p (l t) -> p l t", t=KT)
        fcw = par_of("fcw").rearrange("p (l w t) -> p l w t", l=DEPTH, w=3)
        fcb = par_of("fcb").rearrange("p (l t) -> p l t", l=DEPTH)
        scw = par_of("scw").rearrange("p (w t) -> p w t", w=4)
        scb = par_of("scb")

        def carve(tensor, at, *shape):
            n = int(np.prod(shape))
            v = tensor[:, at:at + n]
            if len(shape) == 2:
                v = v.rearrange("p (a b) -> p a b", a=shape[0])
            elif len(shape) == 3:
                v = v.rearrange("p (a b c) -> p a b c", a=shape[0], b=shape[1])
            return v, at + n

        fst, at = carve(pj, FT * T, 2 * FT, 2, NB)
        fsum, at = carve(pj, at, 2 * FT, NB)
        fnew, at = carve(pj, at, 2 * FT, 10)
        sst, at = carve(pj, CT * T, CT, 3, NB)
        ssum, at = carve(pj, at, CT, NB)
        snew, at = carve(pj, at, CT, 11)
        ftmp = stage[:, :, :].rearrange("p a b -> p (a b)")[:, 0:2 * FT * NB].rearrange("p (a b) -> p a b", b=NB)
        stmp = stage[:, :, :].rearrange("p a b -> p (a b)")[:, 0:CT * NB].rearrange("p (a b) -> p a b", b=NB)

        acc = [ctx.enter_context(nc.psum_tensor(f"acc{n}", [P, 512], F32)) for n in range(4)]
        aux = [ctx.enter_context(nc.psum_tensor(f"aux{n}", [P, 512], F32)) for n in range(4)]
        banks = [aux, acc]

        at = 0
        upper, at = carve(work, at, P)
        rot, at = carve(work, at, P)
        mask, at = carve(work, at, 384)
        cap, at = carve(work, at, 384)
        trig, at = carve(work, at, 4, T)
        decay, at = carve(work, at, H, 384)
        tend, at = carve(work, at, H, 2)
        c0, c1 = CONST["upper"][0], CONST["tend"][1]
        assert at == c1 - c0, (at, c1 - c0)
        work_consts = work[:, 0:at]
        att0 = at
        temps = []
        for _ in range(2):
            zs, at = carve(work, at, 384)
            e_, at = carve(work, at, 384)
            lf, at = carve(work, at, 384)
            temps.append((zs, e_, lf))
        vtok = []
        ktw = []
        for _ in range(2):
            v, at = carve(work, at, 2, 256)
            vtok.append(v)
            v, at = carve(work, at, 2, P)
            ktw.append(v)
        NPB = 3
        pg0 = at
        page = []
        for _ in range(NPB):
            v, at = carve(work, at, H, P)
            page.append(v)
        retp, _ = carve(pj, KA * T, H, 256)
        assert at <= 3 * KT * T, (at, 3 * KT * T)
        at = att0
        s0buf = []
        for _ in range(NRB):
            v, at = carve(work, at, H // 2, 256)
            s0buf.append(v)
        vts, at = carve(work, at, 2048)
        assert at <= 3 * KT * T
        kts, _ = carve(work, c1 - c0 - H * 2 - H * 384, 1024)
        ktm = [carve(work, c1 - c0 - H * 2 - H * 384 + 1024 * (1 + n), 1024)[0] for n in range(2)]
        silg = pt[:, KA:KA + 2 * H, :]
        rinv, at = carve(work, KT * T, T)
        rsq, at = carve(work, at, 2, 2, T)

        at = 0
        smask = stage[:, :, :].rearrange("p a b -> p (a b)")[:, 0:384]
        cumT, at = carve(work, at, SEQ)
        dtT, at = carve(work, at, T)
        dte, at = carve(work, at, T)
        cdT, at = carve(work, at, NB)
        dA, at = carve(work, at, T)
        wendT, at = carve(work, at, SEQ)
        nctok, at = carve(work, at, 2, NH)
        dtok, at = carve(work, at, 2, NH)
        wend, at = carve(work, at, 2, NH)
        dts, at = carve(work, at, NH)
        cds, at = carve(work, at, NH)
        cdbc, at = carve(work, at, NB, NH)
        acol, at = carve(work, at, 1)
        ssm0 = at
        stage_ = stage[:, :, :].rearrange("p a b -> p (a b)")
        cbm0, at = carve(work, at, 384)
        btok0, at = carve(work, at, 2, P)
        xdt0, at = carve(work, at, 2, 512)
        xw0, at = carve(work, at, 2, 512)
        cbm = [cbm0, carve(stage_, 384, 384)[0]]
        btok = [btok0, carve(stage_, 768, 2, P)[0]]
        xdt = [xdt0, carve(pj, CT * T, 2, 512)[0]]
        xw = [xw0, carve(pj, CT * T + 1024, 2, 512)[0]]
        NE, NW = 2, 2
        esb = []
        for _ in range(NE):
            v, at = carve(work, at, 384)
            esb.append(v)
        wsb = []
        for _ in range(NW):
            v, at = carve(work, at, 384)
            wsb.append(v)
        hst, at = carve(work, at, 4, P)
        zg, at = carve(work, at, 4, T)
        gsq, at = carve(work, at, 4, T)
        gsum, at = carve(work, at, G, T)
        assert at <= 3 * KT * T, at
        at = ssm0
        xds, at = carve(work, at, SSM_IN)
        hbuf = []
        for _ in range(NHB):
            v, at = carve(work, at, SSM_IN // 2)
            hbuf.append(v)
        assert at <= 3 * KT * T, at

        lsq = pt[:, 0:KT, :]
        lrt = pt[:, KT, :]
        conv_silu0 = {0: 0, "ssd": FT // 2, 1: FT // 2 + CT // CN}
        tap0 = {0: 0, "ssd": 2 * FT, 1: 2 * FT + 2 * CT}

        lead = [[(PHASES["up0"], 0), (PHASES["up0"], 1)], [(PHASES["dt"], 0), (PHASES["ssd"], 0), (PHASES["ssd"], 1)],
                [(PHASES["up1"], 0), (PHASES["up1"], 1)]]

        def obank(h):
            return acc[h // 2][:, (h % 2) * 256:(h % 2) * 256 + 256]

        def row_of(n, rows):
            return ident[0:rows, n:n + 1].to_broadcast([rows, P])

        landed = [sem(f"landed{s}") for s in range(NRAW)]
        hi_done = sem("hi_done")
        lo_done = sem("lo_done")
        used = sem("used")
        acc_done = sem("acc_done")
        drained = sem("drained")
        R = {n: sem(n) for n in SIGNALS}
        block = ctx.enter_context(nc.Block())

        def chunk_of(ph, i, j):
            return i.at(ph.body, ph.chunk0 + j)

        def load_chunk(eng, ph, i, j):
            n = ph.chunk0 + i.base * ph.body + j
            if RAW_PREV[n] >= 0:
                eng.wait_ge(used, i.at(ph.body, RAW_PREV[n] + 1 - i.base * ph.body))
            c, s = chunk_of(ph, i, j), raw_slot(j, ph.body)
            src = d["w"][c] if isinstance(c, int) else d["w"][bass.ds(c, 1)].rearrange("a p f -> (a p) f")
            eng.dma_start(raw[:, s, :], src).then_inc(landed[s], 16)

        def fill(ph, i, j):
            n = ph.chunk0 + j
            per = USES[n + ph.body] - USES[n] if ph.iters > 1 else 0
            return i.at(16 * per, 16 * USES[n])

        def hi_wait(ph, i, j):
            if i.reg is None:
                c = chunk_of(ph, i, j)
                back = c - HI_PREV[c] if HI_PREV[c] >= 0 else None
            else:
                back = min(n - HI_PREV[n] for n in (ph.chunk0 + k * ph.body + j for k in range(ph.iters))
                           if HI_PREV[n] >= 0)
            if back is None:
                return None
            if i.reg is not None:
                back = min(back, ph.chunk0 + i.base * ph.body + j)
            return i.at(ph.body, ph.chunk0 + j + 1 - back)

        def split_hi(act, ph, i, j, src):
            r = raw_slot(j, ph.body)
            act.wait_ge(landed[r], fill(ph, i, j))
            w = hi_wait(ph, i, j)
            if w is not None:
                act.wait_ge(used, w)
            if ph.ring:
                kc, s = j % ph.kc, j % 4
                act.activation(xh[:, CK * s:CK * s + CK, :], src[:, CK * kc:CK * kc + CK, :], ACT.Copy)
            act.activation(hi[:, hi_slot(j, ph.body), :], raw[:, r, :], ACT.Copy).then_inc(hi_done, 1)

        def split_lo(dve, ph, i, j, src):
            dve.wait_ge(hi_done, i.at(ph.body, ph.chunk0 + j + 1))
            if ph.ring:
                kc, s = j % ph.kc, j % 4
                dve.tensor_tensor(xl[:, CK * s:CK * s + CK, :], src[:, CK * kc:CK * kc + CK, :],
                                  xh[:, CK * s:CK * s + CK, :].bitcast(F32), ALU.subtract)
            r = raw_slot(j, ph.body)
            dve.tensor_tensor(lo[:, r, :], raw[:, r, :], hi[:, hi_slot(j, ph.body), :].bitcast(F32),
                              ALU.subtract).then_inc(lo_done, 1)

        def split_loop(eng, ph, split, src, evac, first=0, end=None, led=0):
            end = ph.iters if end is None else end
            if first == 0:
                for j in range(led, min(LOOK, ph.body * ph.iters)):
                    split(eng, ph, Step(0), j, src)

            def body(i, last):
                since = Step(i.base - first, i.reg)
                for j in range(ph.body):
                    n = j + LOOK
                    if n < ph.body:
                        split(eng, ph, i, n, src)
                    elif not last:
                        split(eng, ph, i.next(), n - ph.body, src)
                    if j % ph.kc == ph.kc - 1:
                        evac(eng, ph, i, j // ph.kc, since.at(ph.panels, j // ph.kc))

            stop = end - 1 if end == ph.iters else end
            if stop - first > 1:
                with eng.Fori(0, stop - first) as r:
                    body(Step(first, r), False)
            elif stop > first:
                body(Step(first), False)
            if end == ph.iters:
                body(Step(end - 1), True)

        def wait_acc(eng, ph, i, pb, n):
            if n < 3:
                eng.wait_ge(acc_done, i.at(3 * ph.panels, ph.acc0 + 3 * pb + n + 1))
            else:
                eng.wait_ge(used, i.at(ph.body, ph.chunk0 + pb * ph.kc + ph.kc))

        def products(pe, ph):
            def body(i):
                for j in range(ph.body):
                    pb, kc = j // ph.kc, j % ph.kc
                    pe.wait_ge(lo_done, i.at(ph.body, ph.chunk0 + j + 1))
                    s, r = j % NHI, raw_slot(j, ph.body)
                    for n in range(CN):
                        if kc == 0:
                            pe.wait_ge(drained, i.at(4 * ph.panels, 4 * (ph.panel0 + pb) + n + 1))
                        for k in range(CK):
                            a = (j % 4 if ph.ring else kc) * CK + k
                            w = slice((k * CN + n) * P, (k * CN + n + 1) * P)
                            out = acc[n][:, 0:T]
                            pe.matmul(out, hi[:, s, w], xh[:, a, :], start=kc == 0 and k == 0, stop=False)
                            pe.matmul(out, hi[:, s, w], xl[:, a, :], start=False, stop=False)
                            m = pe.matmul(out, lo[:, r, w], xh[:, a, :], start=False,
                                          stop=kc == ph.kc - 1 and k == CK - 1)
                        if n < 3 and kc == ph.kc - 1:
                            m.then_inc(acc_done, 1)
                    m.then_inc(used, 1)

            with pe.Fori(0, ph.iters) as r:
                body(Step(0, r))

        @block.sync
        def _(sp):
            sp.dma_start(x_[:, :], d["x"]).then_inc(R["x_in"], 16)
            for ph in ORDER:
                for j in range(ph.body):
                    load_chunk(sp, ph, Step(0), j)
                if ph.iters > 1:
                    with sp.Fori(0, ph.iters - 1) as r:
                        for j in range(ph.body):
                            load_chunk(sp, ph, Step(1, r), j)

        @block.gpsimd
        def _(pool):
            pool.dma_start(cons[:, :], d["const"][:, 0:2 * P]).then_inc(R["consts_in"], 16)
            pool.dma_start(par[:, :], d["param"]).then_inc(R["consts_in"], 16)
            pool.dma_start(pick[:, :], d["const"][:, CONST["pick"][0]:CONST["pick"][1]]).then_inc(R["consts_in"], 16)
            pool.dma_start(pages_sb[:, :], d["pages"]).then_inc(R["pages_in"], 16)

            for n in range(4):
                pool.wait_ge(drained, 4 * (PHASES["ab"].panel0 + 14 + n) + 8)
                pool.dma_start(d["gate"][:, 4 * n:4 * n + 4, :], stage[:, :, :]).then_inc(R["gate_out"], 16)

            pool.wait_ge(used, PHASES["out_ab"].chunk0)
            pool.wait_ge(R["x_lo"], 1)
            pool.dma_start(work_consts, d["const"][:, c0:c1]).then_inc(R["att_in"], 16)
            pool.wait_ge(drained, 4 * PHASES["out_ab"].panel0 + 4)
            pool.dma_start(d["kv"], pt[:, KA:KA + 2 * H, :]).then_inc(R["kv_out"], 16)
            pool.wait_ge(R["pages_in"], 16)
            n = 0
            for cache in ("ck", "cv"):
                for b in range(NB):
                    for k in range(NPG):
                        v = pool.value_load(pages_sb[0:1, b * NPG + k:b * NPG + k + 1], min_val=0, max_val=NPHYS - 1)
                        if n >= NPB:
                            pool.wait_ge(R["page_used"], n - NPB + 1)
                        pool.dma_start(page[n % NPB], d[cache][bass.ds(v, 1)].rearrange("a p h f -> (a p) h f"))\
                            .then_inc(R[f"page_in{n % NPB}"], 16)
                        n += 1
            pool.wait_ge(R["rt_stc"], H)
            pool.dma_start(d["retp"], retp).then_inc(R["rt_out"], 16)
            pool.wait_ge(R["rt_out"], 16)

            units = 2 * NB

            def ret_half(array, u):
                return array[u // 2].rearrange("p (h e) -> p h e", h=H)[:, (u % 2) * 4:(u % 2) * 4 + 4, :]

            def ret_load(u):
                if u >= NRB:
                    pool.wait_ge(R["rs_y"], u - NRB + 1)
                    pool.wait_ge(R[f"rs_out{u % NRB}"], 16 * (u // NRB))
                pool.dma_start(s0buf[u % NRB], ret_half(d["ret0"], u)).then_inc(R[f"rs_in{u % NRB}"], 16)

            pool.wait_ge(R["sb_ycopy"], H + 1)
            pool.wait_ge(R["rt_yc"], H)
            pool.wait_ge(R["page_used"], 2 * NB * NPG)
            pool.wait_ge(R["kv_out"], 16)
            pool.wait_ge(R["gate_out"], 16 * 4)
            for u in range(NRB - 1):
                ret_load(u)
            pool.dma_start(silg, d["gate"][:, 0:2 * H, :]).then_inc(R["gate_in"], 16)
            for u in range(units):
                if u + NRB - 1 < units:
                    ret_load(u + NRB - 1)
                pool.wait_ge(R["rs_new"], 4 * (u + 1))
                pool.dma_start(ret_half(d["rets"], u), s0buf[u % NRB]).then_inc(R[f"rs_out{u % NRB}"], 16)
            pool.wait_ge(R["rs_y"], units)
            pool.dma_start(x_[:, :], d["x"]).then_inc(R["x_back"], 16)
            for n in range(NRB):
                pool.wait_ge(R[f"rs_out{n}"], 16 * ((units - n + NRB - 1) // NRB))

            def ffn(layer):
                pool.wait_ge(used, PHASES[f"up{layer}"].chunk0)
                if layer == 0:
                    pool.wait_ge(R["kv_out"], 16)
                else:
                    pool.wait_ge(R["sconv_out"], 32)
                pool.dma_start(fst, d["fst"][layer]).then_inc(R["ffn_state_in"], 16)
                up = PHASES[f"up{layer}"]
                pool.wait_ge(drained, 4 * (up.panel0 + up.iters * up.panels) + 4)
                pool.wait_ge(R["ffn_state_in"], 16 * (layer + 1))
                pool.dma_start(d["fconv"][layer], fnew).then_inc(R["ffn_out"], 16)
                pool.dma_start(d["fconv_old"][layer], fst[:, :, 1, :]).then_inc(R["ffn_out"], 16)

            ffn(0)
            pool.wait_ge(R["ffn_out"], 32)
            pool.wait_ge(used, PHASES["dt"].chunk0)
            pool.dma_start(sst, d["sst"]).then_inc(R["sconv_in"], 16)
            pool.wait_ge(R["ln_a"], 2 * (KT // 2))
            pool.wait_ge(R["ln_d"], 2 * (KT // 2))
            pool.dma_start(d["xsave"], x_[:, :]).then_inc(R["x_out"], 16)
            for n in range(8):
                pool.wait_ge(drained, 4 * (PHASES["ssd"].panel0 + 12 + n) + 8)
                pool.wait_ge(R["gate_in"], 16)
                pool.dma_start(d["gate"][:, 4 * n:4 * n + 4, :], stage[:, :, :]).then_inc(R["gate_out"], 16)
            pool.wait_ge(R["sconv_in"], 16)
            pool.dma_start(d["sconv"], snew).then_inc(R["sconv_out"], 16)
            pool.dma_start(d["sconv_old"], sst[:, :, 1:3, :]).then_inc(R["sconv_out"], 16)
            pool.wait_ge(used, PHASES["out_ssd"].chunk0)
            pool.wait_ge(R["x_out"], 16)
            pool.wait_ge(R["gate_out"], 16 * 12)
            pool.dma_start(smask, d["const"][:, CONST["mask2"][0]:CONST["mask2"][1]]).then_inc(R["mask_in"], 16)

            def state_load(u):
                b, half = u // 2, u % 2
                if u >= NHB:
                    pool.wait_ge(R["ss_y"], u - NHB + 1)
                    pool.wait_ge(R[f"ss_out{u % NHB}"], 16 * (u // NHB))
                pool.dma_start(hbuf[u % NHB], d["ssm0"][b][:, half * 2048:half * 2048 + 2048])\
                    .then_inc(R[f"ss_in{u % NHB}"], 16)

            units = 2 * NB
            state_load(0)
            state_load(1)
            for u in range(units):
                b, half = u // 2, u % 2
                pool.wait_ge(R[f"ss_in{u % NHB}"], 16 * (u // NHB + 1))
                pool.wait_ge(R["cd_ready"], 1)
                hv = hbuf[u % NHB].rearrange("p (h q) -> p h q", q=HD)
                f = cdbc[:, b, 32 * half:32 * half + 32].unsqueeze(2).to_broadcast([P, 32, HD])
                pool.tensor_tensor(hv, hv, f, ALU.mult).then_inc(R["ss_h"], 1)
                if u + 2 < units:
                    state_load(u + 2)
                pool.wait_ge(R["ss_n"], 4 * (u + 1))
                pool.dma_start(d["ssms"][b][:, half * 2048:half * 2048 + 2048], hbuf[u % NHB])\
                    .then_inc(R[f"ss_out{u % NHB}"], 16)
            for s in range(NHB):
                pool.wait_ge(R[f"ss_out{s}"], 16 * ((units - s + NHB - 1) // NHB))
            pool.wait_ge(R["ss_ya"], 1)
            pool.wait_ge(R["gate_out"], 16 * 12)
            for g in range(G):
                if g >= 1:
                    pool.wait_ge(R["g_z"], g)
                pool.dma_start(zg, d["gate"][:, 4 * g:4 * g + 4, :]).then_inc(R["z_in"], 16)
                pool.wait_ge(R["g_stc"], g + 1)
                pool.dma_start(d["ssmp"][:, 4 * g:4 * g + 4, :], hst).then_inc(R["g_out"], 16)
            pool.wait_ge(R["g_n"], XST)
            pool.wait_ge(R["g_out"], 16 * G)
            pool.dma_start(x_[:, :], d["xsave"]).then_inc(R["x_back"], 16)
            ffn(1)
            pool.wait_ge(R["ln_a"], 4 * (KT // 2))
            pool.wait_ge(R["ln_d"], 4 * (KT // 2))
            pool.dma_start(d["y"], x_[:, :]).then_inc(R["y_out"], 16)
            pool.wait_ge(R["y_out"], 16)
            pool.wait_ge(R["ffn_out"], 64)
            pool.wait_ge(R["rt_out"], 16)
            pool.wait_ge(R["kv_out"], 16)

        @block.scalar
        def _(act):
            a = act.activation

            def apart(eng):
                eng.wait_ge(R["consts_in"], 48)

            def copy_tiles(eng, ph, i, pb, q):
                for n in range(CN):
                    wait_acc(eng, ph, i, pb, n)
                    apart(eng)
                    t = q * CN + n
                    dst = pt[:, t, :] if isinstance(t, int) else pt[:, bass.ds(t, 1), :].rearrange("p a n -> p (a n)")
                    a(dst, acc[n][:, 0:T], ACT.Copy).then_inc(drained, 1)

            def gate_tiles(base):
                def evac(eng, ph, i, pb, q):
                    if base or q:
                        eng.wait_ge(R["gate_out"], q * 16 + base * 16)
                    for n in range(CN):
                        wait_acc(eng, ph, i, pb, n)
                        a(stage[:, n, :], acc[n][:, 0:T], ACT.Silu).then_inc(drained, 1)
                return evac

            def conv_base(w, bias, dst, silu):
                def evac(eng, ph, i, pb, q):
                    for n in range(CN):
                        wait_acc(eng, ph, i, pb, n)
                        apart(eng)
                        ch = q * CN + n
                        col = (lambda v: v[:, ch:ch + 1] if isinstance(ch, int) else v[:, bass.ds(ch, 1)])
                        a(dst(q, n), acc[n][:, 0:T], ACT.Identity, bias=col(bias), scale=col(w))\
                            .then_inc(R["conv_base"], 1)
                    eng.wait_ge(drained, i.at(4 * ph.panels, 4 * (ph.panel0 + pb) + 8))
                    a(small[:, 2:3], small[:, 1:2], ACT.Silu)
                    silu(q)
                return evac

            act.wait_ge(R["x_in"], 16)
            a(xh[:, :, :], x, ACT.Copy).then_inc(R["x_hi"], 1)
            act.wait_ge(R["consts_in"], 48)
            act.wait_ge(R["small_set"], 2)

            ab = PHASES["ab"]
            split_loop(act, ab, split_hi, None, copy_tiles, 0, 7)
            split_loop(act, ab, split_hi, None, gate_tiles(0), 7, 9)

            act.wait_ge(R["att_in"], 16)

            def sb_z(h):
                bk, (zs, e, lf) = banks[h % 2], temps[h % 2]
                act.wait_ge(R["sbz"], h + 1)
                if h >= 2:
                    act.wait_ge(R["sb_arg"], h - 1)
                a(zs, bk[0][:, 0:384], ACT.Identity, bias=par_of("sbias")[:, h:h + 1], scale=SCALE)\
                    .then_inc(R["sbz_s"], 1)

            def sb_values(h):
                bk = banks[h % 2]
                act.wait_ge(R["sb_vt"], h + 1)
                if h >= 2:
                    act.wait_ge(R["sb_y"], h - 1)
                a(vtok[h % 2][:, 0, :], bk[2][:, 0:256], ACT.Copy).then_inc(R["sb_vs"], 1)

            def sb_softplus(h, n=384):
                e = temps[h % 2][1][:, 0:n]
                act.wait_ge(R["sb_na"], h + 1)
                a(e, e, ACT.Exp).then_inc(R["sb_e"], 1)
                act.wait_ge(R["sb_e"], h + 1)
                a(e, e, ACT.Ln, bias=one_col).then_inc(R["sb_L"], 1)

            def sb_weight(h, n=384):
                e = temps[h % 2][1][:, 0:n]
                act.wait_ge(R["sb_cap"], h + 1)
                a(e, e, ACT.Exp).then_inc(R["sb_w"], 1)

            def sb_out(h):
                act.wait_ge(R["sb_y"], h + 1)
                a(pt[:, QA + h, 0:SEQ], banks[h % 2][2][:, SEQ:2 * SEQ], ACT.Copy).then_inc(R["sb_ycopy"], 1)

            for t in range(H + 2):
                if t < H:
                    sb_z(t)
                    sb_softplus(t)
                if 1 <= t <= H:
                    sb_values(t - 1)
                    sb_weight(t - 1)
                if t >= 2:
                    sb_out(t - 2)
            sb_softplus(H, 2 * NB * H)
            sb_weight(H, 2 * NB * H)

            for t in range(H + 1):
                if t < H:
                    h, bk = t, banks[t % 2]
                    act.wait_ge(R["rt_t"], h + 1)
                    if h >= 2:
                        act.wait_ge(R["rt_st"], h - 1)
                    a(vtok[h % 2].rearrange("p c e -> p (c e)"), bk[2][:, :], ACT.Copy).then_inc(R["rt_v"], 1)
                    for c in range(2):
                        ins = a(ktw[h % 2][:, c, :], bk[1][:, c * P:c * P + P], ACT.Identity,
                                scale=tend[:, h, c:c + 1])
                    ins.then_inc(R["rt_k"], 1)
                if t >= 1:
                    h = t - 1
                    act.wait_ge(R["rt_y"], h + 1)
                    a(pt[:, VR + 2 * h:VR + 2 * h + 2, 0:SEQ], aux[3][:, :].rearrange("p (u n) -> p u n", u=2),
                      ACT.Copy).then_inc(R["rt_yc"], 1)
            act.wait_ge(R["rs_t"], 1)
            act.wait_ge(R["rt_out"], 16)
            act.wait_ge(R["rt_p"], H)
            for q in range(4):
                a(vts[0:NB, q * 512:q * 512 + 512], acc[q][0:NB, :], ACT.Copy)
            for q in range(2):
                ins = a(kts[0:NB, q * 512:q * 512 + 512], aux[q][0:NB, :], ACT.Copy)
            ins.then_inc(R["rs_tc"], 1)
            act.wait_ge(R["rs_yc"], 1)
            act.wait_ge(R["rt_yc"], H)
            rest = 16 * ((2 * NB + NRB - 1) // NRB)
            act.wait_ge(R["rs_out0"], rest)
            for h in range(H):
                if h >= 2:
                    act.wait_ge(R["rn_sum"], h - 1)
                a(rsq[:, h % 2], pt[:, VR + 2 * h:VR + 2 * h + 2, :], ACT.Square).then_inc(R["rn_sq"], 1)
            act.wait_ge(R["rn_sum"], H)
            a(rinv[0:H, :], aux[0][0:H, 0:T], ACT.Sqrt, bias=eps_col[0:H, :], scale=1.0 / 256)\
                .then_inc(R["rn_sqrt"], 1)

            def norm(l, split, ahead=()):
                for ph, j in ahead:
                    split_hi(act, ph, Step(0), j, None)
                act.wait_ge(R["ln_cen"], l + 1)
                a(lsq, x, ACT.Square).then_inc(R["ln_sq"], 1)
                act.wait_ge(R["ln_var"], l + 1)
                a(lrt, aux[1][:, 0:T], ACT.Sqrt, bias=eps_col, scale=1.0 / D).then_inc(R["ln_sqrt"], 1)
                act.wait_ge(R["ln_norm"], l + 1)
                for t in range(KT // 2):
                    a(x[:, t, :], x[:, t, :], ACT.Identity, bias=lnb[:, l, t:t + 1], scale=lng[:, l, t:t + 1])\
                        .then_inc(R["ln_a"], 1)
                if split:
                    act.wait_ge(R["ln_d"], (l + 1) * (KT // 2))
                    act.wait_ge(R["ln_a"], (l + 1) * (KT // 2))
                    a(xh[:, :, :], x, ACT.Copy).then_inc(R["x_hi"], 1)

            def no_evac(eng, ph, i, pb, q):
                pass

            def ffn(layer):
                up, down = PHASES[f"up{layer}"], PHASES[f"down{layer}"]

                def silu(q):
                    a(stage[:, 0:2, :], stage[:, 0:2, :], ACT.Silu).then_inc(R["conv_silu"], 1)

                base = conv_base(fcw[:, layer, 2, :], fcb[:, layer, :], lambda q, n: stage[:, n, :], silu)

                def evac(eng, ph, i, pb, q):
                    eng.wait_ge(R["ffn_tile"], q + (layer * (FT // 2) + 1))
                    base(eng, ph, i, pb, q)

                act.wait_ge(R["ffn_sum"], 3 * (layer + 1))
                split_loop(act, up, split_hi, None, evac, led=LOOK)
                act.wait_ge(R["ffn_tile"], (layer + 1) * (FT // 2) + 1)
                split_loop(act, down, split_hi, pt, no_evac)

            act.wait_ge(R["rn_a"], H)
            act.wait_ge(R["sb_ycopy"], H + 1)
            for n in range(NRB):
                act.wait_ge(R[f"rs_out{n}"], 16 * ((2 * NB - n + NRB - 1) // NRB))
            split_loop(act, PHASES["out_ab"], split_hi, pt, no_evac)
            norm(0, True, lead[0])
            ffn(0)
            norm(1, True, lead[1])

            act.wait_ge(used, PHASES["dt"].chunk0 + 1)
            a(dtraw[:, :], acc[0][0:NH, 0:T], ACT.Identity, bias=par_of("dtb")[0:NH, :]).then_inc(drained, 4)

            def xbc_tile(q, n):
                t = q * CN + n
                return pt[:, t, :] if isinstance(t, int) else pt[:, bass.ds(t, 1), :].rearrange("p a n -> p (a n)")

            def xbc_silu(q):
                v = pt[:, q * CN:q * CN + CN, :] if isinstance(q, int) else pt[:, bass.ds(q * CN, CN), :]
                a(v, v, ACT.Silu).then_inc(R["conv_silu"], 1)

            act.wait_ge(R["ssd_sum"], 5)
            split_loop(act, PHASES["ssd"], split_hi, None, conv_base(scw[:, 3, :], scb, xbc_tile, xbc_silu), 0, 6,
                       led=LOOK)
            split_loop(act, PHASES["ssd"], split_hi, None, gate_tiles(4), 6, 10)

            act.wait_ge(R["dt_c"], 1)
            a(dte[0:NH, :], dte[0:NH, :], ACT.Exp).then_inc(R["dt_a"], 1)
            act.wait_ge(R["dt_a"], 1)
            a(dte[0:NH, :], dte[0:NH, :], ACT.Ln, bias=one_col[0:NH, :]).then_inc(R["dt_a"], 1)
            a(acol[0:NH, :], par_of("alog")[0:NH, :], ACT.Exp).then_inc(R["dt_a"], 1)
            act.wait_ge(R["dt_c"], 4)
            a(wendT[0:NH, :], cumT[0:NH, :], ACT.Exp, bias=cumT[0:NH, SEQ - 1:SEQ], scale=-1.0).then_inc(R["dt_a"], 1)
            a(cdT[0:NH, :], dA[0:NH, SEQ:T], ACT.Exp).then_inc(R["dt_a"], 1)

            def head_decay(n):
                act.wait_ge(R["g_arg"], n + 1)
                a(esb[n % 2], esb[n % 2], ACT.Exp).then_inc(R["g_e"], 1)

            for g in range(G):
                act.wait_ge(R["g_bt"], g + 1)
                if g == 0:
                    act.wait_ge(R["z_in"], 16)
                a(btok[0], aux[1][:, 0:256].rearrange("p (c s) -> p c s", c=2), ACT.Copy).then_inc(R["g_btc"], 1)
                for k in range(8):
                    head_decay(8 * g + k)
                act.wait_ge(R["g_st"], g + 1)
                if g >= 1:
                    act.wait_ge(R["g_out"], 16 * g)
                a(hst, aux[0][:, :].rearrange("p (t s) -> p t s", t=4), ACT.Copy).then_inc(R["g_stc"], 1)
                act.wait_ge(R["g_z"], g + 1)
                a(gsq, pt[:, XS + 4 * g:XS + 4 * g + 4, :], ACT.Square).then_inc(R["g_sq"], 1)
            act.wait_ge(R["g_ssc"], G)
            a(gsum, gsum, ACT.Sqrt).then_inc(R["g_sqrt"], 1)
            act.wait_ge(R["g_n"], XST)
            act.wait_ge(R["g_out"], 16 * G)
            split_loop(act, PHASES["out_ssd"], split_hi, pt[:, XS:XS + XST, :], no_evac)
            norm(2, True, lead[2])
            ffn(1)
            norm(3, False)

        @block.vector
        def _(dve):
            tt, ts, stt = dve.tensor_tensor, dve.tensor_scalar, dve.scalar_tensor_tensor

            def no_evac(eng, ph, i, pb, q):
                pass

            def residual(l):
                def evac(eng, ph, i, pb, q):
                    for n in range(CN):
                        wait_acc(eng, ph, i, pb, n)
                        t = q * CN + n
                        v = x[:, t, :] if isinstance(t, int) else x[:, bass.ds(t, 1), :].rearrange("p a n -> p (a n)")
                        stt(v, v, ALPHA, acc[n][:, 0:T], ALU.mult, ALU.add).then_inc(drained, 1)
                    for n in range(CN):
                        eng.wait_ge(drained, i.at(4 * ph.panels, 4 * (ph.panel0 + pb) + 4 + n + 1))
                        eng.wait_ge(R["ln_sum"], q * CN + (17 * l + n + 1))
                        t = q * CN + n
                        v = x[:, t, :] if isinstance(t, int) else x[:, bass.ds(t, 1), :].rearrange("p a n -> p (a n)")
                        tt(lsum[:, :], lsum[:, :], v, ALU.add).then_inc(R["ln_sum"], 1)
                return evac

            def clear_sum(l):
                if l:
                    dve.wait_ge(R["ln_var"], l)
                dve.memset(lsum[:, :], 0.0).then_inc(R["ln_sum"], 1)

            def taps(w, sums, new, tap0, conv0, dst, width, after):
                def evac(eng, ph, i, pb, q):
                    for n in range(CN):
                        ch = q * CN + n
                        one = (lambda v: v[:, ch:ch + 1] if isinstance(ch, int) else v[:, bass.ds(ch, 1)])
                        row = (lambda v: v[:, ch, :] if isinstance(ch, int)
                               else v[:, bass.ds(ch, 1), :].rearrange("p a n -> p (a n)"))
                        eng.wait_ge(R["conv_base"], q * CN + (conv0 + n + 1))
                        y, h = dst(q, n), acc[n]
                        tap = tap0 + n * (width - 2)
                        dve.tensor_copy(row(new), h[:, T - NB - (width - 1):T])
                        tt(y[:, SEQ:T], y[:, SEQ:T], row(sums), ALU.add)
                        for k in range(1, width):
                            if k > 1:
                                eng.wait_ge(R["conv_tap"], q * (CN * (width - 2)) + (tap + k - 1))
                            ins = stt(y[:, k:SEQ], h[:, 0:SEQ - k], one(w[:, width - 1 - k, :]), y[:, k:SEQ],
                                      ALU.mult, ALU.add)
                            ins.then_inc(R["conv_tap"] if k < width - 1 else drained, 1)
                    after(eng, ph, i, pb, q)
                return evac

            dve.memset(small[:, 7:8], 1.0).then_inc(R["ffn_tile"], 1)
            dve.memset(small[:, 0:1], EPS).then_inc(R["small_set"], 1)
            dve.memset(small[:, 1:7], 1.0).then_inc(R["small_set"], 1)
            for n in range(4):
                dve.memset(acc[n][:, :], 0.0).then_inc(drained, 1)
            dve.wait_ge(R["x_hi"], 1)
            tt(xl[:, :, :], x, xh[:, :, :].bitcast(F32), ALU.subtract).then_inc(R["x_lo"], 1)
            split_loop(dve, PHASES["ab"], split_lo, None, no_evac)

            dve.wait_ge(R["att_in"], 16)
            dve.wait_ge(drained, 4 * PHASES["out_ab"].panel0 + 4)
            for m in range(2 * H):
                tile = pt[:, QR + m, :]
                cos, sin = (trig[:, 0, :], trig[:, 1, :]) if m < H else (trig[:, 2, :], trig[:, 3, :])
                t = temps[m % 2][0][:, 0:T]
                dve.wait_ge(R["rot_p"], m + 1)
                tt(t, sin, aux[m % 4][:, 0:T], ALU.mult).then_inc(R["rot_m"], 1)
                tt(tile, tile, cos, ALU.mult).then_inc(R["rot_c"], 1)
                dve.wait_ge(R["rot_m"], m + 1)
                dve.wait_ge(R["rot_c"], m + 1)
                tt(tile, tile, t, ALU.add).then_inc(R["rot_done"], 1)
            dve.wait_ge(R["rot_done"], 2 * H)

            def sb_neg(h, n=384):
                zs, e, _ = temps[h % 2]
                dve.wait_ge(R["sbz_s"], h + 1)
                if h >= 2:
                    dve.wait_ge(R["sb_y"], h - 1)
                stt(e[:, 0:n], zs[:, 0:n], -1.0, zs[:, 0:n], ALU.mult, ALU.min).then_inc(R["sb_na"], 1)

            def sb_fail(h, n=384):
                zs, e, lf = (v[:, 0:n] for v in temps[h % 2])
                dve.wait_ge(R["sb_L"], h + 1)
                stt(lf, zs, 0.0, e, ALU.max, ALU.add).then_inc(R["sb_lf"], 1)
                if h < H:
                    dve.wait_ge(R["sb_lf"], h + 1)
                    tt(lf, lf, mask, ALU.mult).then_inc(R["sb_m"], 1)

            def sb_arg(h, n=384):
                zs, e, _ = (v[:, 0:n] for v in temps[h % 2])
                dve.wait_ge(R["sb_incl"], h + 1)
                tt(e, zs, banks[h % 2 if h < H else 1][1][:, 0:n], ALU.subtract).then_inc(R["sb_arg"], 1)
                dve.wait_ge(R["sb_arg"], h + 1)
                if h < H:
                    tt(e, e, cap, ALU.min).then_inc(R["sb_cap"], 1)
                else:
                    ts(e, e, 0.0, None, ALU.min).then_inc(R["sb_cap"], 1)

            for t in range(H + 1):
                if t < H:
                    sb_neg(t)
                if t >= 1:
                    sb_arg(t - 1)
                if t < H:
                    sb_fail(t)
            dve.wait_ge(R["page_used"], NB * NPG)
            zs = temps[0][0][:, 0:2 * NB * H]
            v3 = (lambda v: v.rearrange("p (a h) -> p a h", h=H))
            stt(v3(zs), v3(aux[3][:, 0:2 * NB * H]), SCALE,
                par_of("sbias").unsqueeze(1).to_broadcast([P, 2 * NB, H]), ALU.mult, ALU.add).then_inc(R["sbz_s"], 1)
            sb_neg(H, 2 * NB * H)
            sb_fail(H, 2 * NB * H)
            sb_arg(H, 2 * NB * H)
            for t in range(H + 1):
                if t < H:
                    h = t
                    dve.wait_ge(R["rt_s"], h + 1)
                    if h >= 2:
                        dve.wait_ge(R["rt_y"], h - 1)
                    tt(temps[h % 2][2], decay[:, h, :], banks[h % 2][0][:, 0:384], ALU.mult).then_inc(R["rt_p"], 1)
                if t >= 1:
                    h = t - 1
                    dve.wait_ge(R["rt_st"], h + 1)
                    if h == 0:
                        dve.wait_ge(R["kv_out"], 16)
                    dve.tensor_copy(retp[:, h, :], banks[h % 2][0][:, 0:256]).then_inc(R["rt_stc"], 1)

            dve.wait_ge(R["page_used"], 2 * NB * NPG)
            part = temps[1][0][:, 0:NB * H]
            dve.tensor_copy(part, acc[3][:, NB * H:2 * NB * H]).then_inc(R["sb_part"], 1)
            dve.wait_ge(R["sb_part"], 1)
            tt(pt[:, QA:QA + H, SEQ:T], part.rearrange("p (h b) -> p h b", b=NB),
               acc[3][:, 0:NB * H].rearrange("p (h b) -> p h b", b=NB), ALU.add).then_inc(R["sb_ycopy"], 1)

            def key_of(b):
                if b >= 2:
                    dve.wait_ge(R["rs_o"], 4 * (b - 1))
                ts(ktm[b % 2][0:NB, :], kts[0:NB, :], ident[0:NB, b:b + 1], None, ALU.mult).then_inc(R["rs_km"], 1)

            dve.wait_ge(R["rs_tc"], 1)
            key_of(0)
            key_of(1)
            for u in range(2 * NB):
                dve.wait_ge(R[f"rs_in{u % NRB}"], 16 * (u // NRB + 1))
                for k in range(4):
                    h = 4 * (u % 2) + k
                    dve.wait_ge(R["rs_o"], 2 * u + k // 2 + 1)
                    v = s0buf[u % NRB][:, k, :]
                    stt(v, v, float(GAMMA[h]), obank(h), ALU.mult, ALU.add).then_inc(R["rs_new"], 1)
                if u % 2 and u // 2 + 2 < NB:
                    key_of(u // 2 + 2)
            dve.wait_ge(R["rs_y"], 2 * NB)
            dve.tensor_copy(pt[:, VR:VR + 2 * H, SEQ:T], aux[2][:, 0:2 * H * NB].rearrange("p (t b) -> p t b", b=NB))\
                .then_inc(R["rs_yc"], 1)
            dve.wait_ge(R["gate_in"], 16)
            dve.wait_ge(R["rn_sq"], H)
            v = pt[:, VR:VR + 2 * H, :]
            tt(v, v, silg, ALU.mult).then_inc(R["rn_b"], 1)
            dve.wait_ge(R["rn_sqrt"], 1)
            dve.reciprocal(rinv[0:H, :], rinv[0:H, :]).then_inc(R["rn_inv"], 1)
            dve.wait_ge(R["rn_b"], 1)
            for h in range(H):
                dve.wait_ge(R["rn_bc"], h + 1)
                v = pt[:, VR + 2 * h:VR + 2 * h + 2, :]
                tt(v, v, acc[h % 4][:, 0:T].unsqueeze(1).to_broadcast([P, 2, T]), ALU.mult).then_inc(R["rn_a"], 1)

            def norm(l, split, ahead=()):
                ahead = list(ahead)
                by_token = (lambda v: v.rearrange("p t n -> p n t"))
                dve.wait_ge(R["ln_mean"], l + 1)
                stt(x, aux[0][:, 0:T].unsqueeze(1).to_broadcast([P, KT, T]), -1.0 / D, x, ALU.mult, ALU.add)\
                    .then_inc(R["ln_cen"], 1)
                if ahead:
                    ph, j = ahead.pop(0)
                    split_lo(dve, ph, Step(0), j, None)
                dve.wait_ge(R["ln_sq"], l + 1)
                dve.tensor_reduce(lsum[:, :], by_token(lsq), AX.X, ALU.add).then_inc(R["ln_sqsum"], 1)
                dve.wait_ge(R["ln_sqrt"], l + 1)
                dve.reciprocal(lrt, lrt).then_inc(R["ln_rstd"], 1)
                dve.wait_ge(R["ln_rstd"], l + 1)
                tt(x, x, lrt.unsqueeze(1).to_broadcast([P, KT, T]), ALU.mult).then_inc(R["ln_norm"], 1)
                dve.wait_ge(R["ln_norm"], l + 1)
                for t in range(KT // 2, KT):
                    ts(x[:, t, :], x[:, t, :], lng[:, l, t:t + 1], lnb[:, l, t:t + 1], ALU.mult, ALU.add)\
                        .then_inc(R["ln_d"], 1)
                for ph, j in ahead:
                    split_lo(dve, ph, Step(0), j, None)
                if split:
                    n = {0: 2, 1: 3, 2: 4}[l]
                    dve.wait_ge(R["x_hi"], n)
                    tt(xl[:, :, :], x, xh[:, :, :].bitcast(F32), ALU.subtract).then_inc(R["x_lo"], 1)

            def ffn(layer):
                up, down = PHASES[f"up{layer}"], PHASES[f"down{layer}"]
                dve.wait_ge(R["ffn_state_in"], 16 * (layer + 1))
                for k, o in ((0, fsum), (1, ftmp)):
                    w = fcw[:, layer, k, :].unsqueeze(2).to_broadcast([P, 2 * FT, NB])
                    tt(o, fst[:, :, k, :], w, ALU.mult).then_inc(R["ffn_sum"], 1)
                dve.wait_ge(R["ffn_sum"], 3 * layer + 2)
                tt(fsum, fsum, ftmp, ALU.add).then_inc(R["ffn_sum"], 1)
                dve.wait_ge(R["ffn_sum"], 3 * layer + 3)

                def product(eng, ph, i, pb, q):
                    eng.wait_ge(R["conv_silu"], q + (conv_silu0[layer] + 1))
                    v = pt[:, 2 * q:2 * q + 2, :] if isinstance(q, int) else pt[:, bass.ds(q * 2, 2), :]
                    tt(v, stage[:, 0:2, :], stage[:, 2:4, :], ALU.mult).then_inc(R["ffn_tile"], 1)

                ev = taps(fcw[:, layer], fsum, fnew, tap0[layer], 4 * conv_silu0[layer],
                          lambda q, n: stage[:, n, :], 3, product)
                split_loop(dve, up, split_lo, None, ev, led=LOOK)
                dve.wait_ge(R["ffn_tile"], (layer + 1) * (FT // 2) + 1)
                clear_sum(2 * layer + 1)
                split_loop(dve, down, split_lo, pt, residual(2 * layer + 1))

            dve.wait_ge(R["rn_a"], H)
            dve.wait_ge(R["x_back"], 16)
            clear_sum(0)
            split_loop(dve, PHASES["out_ab"], split_lo, pt, residual(0))
            norm(0, True, lead[0])
            ffn(0)
            norm(1, True, lead[1])

            dve.wait_ge(R["sconv_in"], 16)
            wb = (lambda k: scw[:, k, :].unsqueeze(2).to_broadcast([P, CT, NB]))
            tt(ssum, sst[:, :, 0, :], wb(0), ALU.mult).then_inc(R["ssd_sum"], 1)
            for k in (1, 2):
                tt(stmp, sst[:, :, k, :], wb(k), ALU.mult).then_inc(R["ssd_sum"], 1)
                dve.wait_ge(R["ssd_sum"], 2 * k)
                tt(ssum, ssum, stmp, ALU.add).then_inc(R["ssd_sum"], 1)
                dve.wait_ge(R["ssd_sum"], 2 * k + 1)

            def xbc_tile(q, n):
                t = q * CN + n
                return pt[:, t, :] if isinstance(t, int) else pt[:, bass.ds(t, 1), :].rearrange("p a n -> p (a n)")

            ssd = PHASES["ssd"]
            ev = taps(scw, ssum, snew, tap0["ssd"], 4 * conv_silu0["ssd"], xbc_tile, 4,
                      lambda *a: None)
            split_loop(dve, ssd, split_lo, None, ev, 0, 6, led=LOOK)
            split_loop(dve, ssd, split_lo, None, no_evac, 6, 10)

            dve.wait_ge(used, PHASES["out_ssd"].chunk0)
            dve.wait_ge(R["x_out"], 16)
            dve.wait_ge(drained, 4 * PHASES["out_ssd"].panel0 + 4)
            r = dtraw[:, :]
            stt(dte[0:NH, :], r, -1.0, r, ALU.mult, ALU.min).then_inc(R["dt_c"], 1)
            dve.wait_ge(R["dt_a"], 3)
            stt(dtT[0:NH, :], r, 0.0, dte[0:NH, :], ALU.max, ALU.add).then_inc(R["dt_c"], 1)
            dve.wait_ge(R["dt_c"], 2)
            ts(dA[0:NH, :], dtT[0:NH, :], acol[0:NH, :], -1.0, ALU.mult, ALU.mult).then_inc(R["dt_c"], 1)
            dve.wait_ge(R["dt_c"], 3)
            dve.tensor_tensor_scan(cumT[0:NH, :], one_col[0:NH, :].to_broadcast([NH, SEQ]), dA[0:NH, 0:SEQ], 0.0,
                                   ALU.mult, ALU.add).then_inc(R["dt_c"], 1)
            dve.wait_ge(R["dt_a"], 5)
            tt(wendT[0:NH, :], wendT[0:NH, :], dtT[0:NH, 0:SEQ], ALU.mult).then_inc(R["dt_c"], 1)
            dve.wait_ge(R["sm_t"], 1)
            flat = (lambda v: v.rearrange("p c h -> p (c h)"))
            ts(flat(nctok), aux[0][:, 0:2 * NH], -1.0, None, ALU.mult).then_inc(R["dt_c"], 1)
            dve.tensor_copy(flat(dtok), aux[0][:, 2 * NH:4 * NH])
            dve.tensor_copy(flat(wend), aux[0][:, 4 * NH:6 * NH])
            dve.tensor_copy(dts[0:NB, :], aux[1][0:NB, 0:NH])
            dve.tensor_copy(cds[0:NB, :], aux[1][0:NB, NH:2 * NH]).then_inc(R["dt_c"], 1)
            dve.wait_ge(R["cd_p"], 1)
            dve.tensor_copy(cdbc.rearrange("p b h -> p (b h)"), aux[2][:, :]).then_inc(R["cd_ready"], 1)
            dve.wait_ge(R["dt_c"], 7)
            for q in range(G):
                dve.wait_ge(R["ss_t"], q + 1)
                tt(xds[0:NB, q * 512:q * 512 + 512].rearrange("p (h e) -> p h e", e=HD),
                   dts[0:NB, 8 * q:8 * q + 8].unsqueeze(2).to_broadcast([NB, 8, HD]),
                   acc[q % 4][0:NB, :].rearrange("p (h e) -> p h e", e=HD), ALU.mult).then_inc(R["ss_x"], 1)
            for b in range(NB):
                for g in range(G):
                    u = 2 * b + g // 4
                    dve.wait_ge(R["ss_o"], G * b + g + 1)
                    dve.wait_ge(R["ss_h"], u + 1)
                    v = hbuf[u % NHB][:, (g % 4) * 512:(g % 4) * 512 + 512]
                    stt(v, acc[g % 4][:, :], pt[:, BM + g, SEQ + b:SEQ + b + 1], v, ALU.mult, ALU.add)\
                        .then_inc(R["ss_n"], 1)
            dve.wait_ge(R["ss_y"], 2 * NB)
            xs_s = pt[:, XS:XS + XST, SEQ:T]
            tt(xs_s, xs_s, par_of("dskip").unsqueeze(2).to_broadcast([P, XST, NB]), ALU.mult).then_inc(R["ss_yd"], 1)
            dve.wait_ge(R["ss_yd"], 1)
            tt(xs_s, xs_s, aux[3][:, 0:XST * NB].rearrange("p (t b) -> p t b", b=NB), ALU.add).then_inc(R["ss_ya"], 1)

            dskip, normw = par_of("dskip"), par_of("normw")
            dve.wait_ge(R["mask_in"], 16)
            dve.wait_ge(R["z_in"], 16)

            def pair_out(n):
                dve.wait_ge(R["g_yh"], 2 * n + 2)
                v = pt[:, XS + n, 0:SEQ]
                stt(v, v, dskip[:, n:n + 1], aux[2 + n % 2][:, 0:SEQ], ALU.mult, ALU.add).then_inc(R["g_yd"], 1)

            def exponent(n):
                dve.wait_ge(R["g_bc"], n // 2 + 1)
                if n >= 2:
                    dve.wait_ge(R["g_w"], n - 1)
                bk, o, e = acc[2 + (n // 2) % 2], (n % 2) * 256, esb[n % 2]
                ts(e[:, 0:256], bk[:, o:o + 256], nctok[:, 0, n:n + 1], 0.0, ALU.add, ALU.min)
                ts(e[:, 256:384], bk[:, o + 128:o + 256], nctok[:, 1, n:n + 1], 0.0, ALU.add, ALU.min)\
                    .then_inc(R["g_arg"], 1)

            for g in range(G):
                dve.wait_ge(R["g_cb"], g + 1)
                tt(cbm[0], smask, aux[0][:, 0:384], ALU.mult).then_inc(R["g_cbm"], 1)
                for c in range(2):
                    dve.wait_ge(R["g_xt"], 2 * g + c + 1)
                    src = acc[c][:, :].rearrange("p (h e) -> p h e", e=HD)
                    for o, f in ((xdt[0], dtok), (xw[0], wend)):
                        ins = tt(o[:, c, :].rearrange("p (h e) -> p h e", e=HD),
                                 f[:, c, 8 * g:8 * g + 8].unsqueeze(2).to_broadcast([P, 8, HD]), src, ALU.mult)
                ins.then_inc(R["g_x"], 1)
                dve.wait_ge(R["g_cbm"], g + 1)
                exponent(8 * g)
                for k in range(8):
                    n = 8 * g + k
                    if k < 7:
                        exponent(n + 1)
                    dve.wait_ge(R["g_e"], n + 1)
                    if n >= 2:
                        dve.wait_ge(R["g_yh"], n - 1)
                    tt(wsb[n % 2], esb[n % 2], cbm[0], ALU.mult).then_inc(R["g_w"], 1)
                    if k % 2 == 1 and k >= 3:
                        pair_out(n // 2 - 1)
                pair_out(4 * g + 3)
                dve.wait_ge(R["z_in"], 16 * (g + 1))
                dve.wait_ge(R["g_yd"], 4 * g + 4)
                v = pt[:, XS + 4 * g:XS + 4 * g + 4, :]
                tt(v, v, zg, ALU.mult).then_inc(R["g_z"], 1)
                dve.wait_ge(R["g_ss"], g + 1)
                ts(gsum[:, g, :], aux[1][:, 0:T], 1.0 / 512, EPS, ALU.mult, ALU.add).then_inc(R["g_ssc"], 1)
            dve.wait_ge(R["g_sqrt"], 1)
            dve.reciprocal(gsum, gsum).then_inc(R["g_inv"], 1)
            dve.wait_ge(R["g_inv"], 1)
            for t in range(XST):
                v = pt[:, XS + t, :]
                stt(v, v, normw[:, t:t + 1], gsum[:, t // 4, :], ALU.mult, ALU.mult).then_inc(R["g_n"], 1)
            dve.wait_ge(R["g_n"], XST)
            dve.wait_ge(R["x_back"], 32)
            clear_sum(2)
            split_loop(dve, PHASES["out_ssd"], split_lo, pt[:, XS:XS + XST, :], residual(2))
            norm(2, True, lead[2])
            ffn(1)
            norm(3, False)

        @block.tensor
        def _(pe):
            mm = pe.matmul

            def turn(out, src):
                k = src.shape[0]
                return pe.transpose(out, src, ident[0:k, 0:k])

            pe.wait_ge(R["consts_in"], 48)
            pe.wait_ge(R["x_lo"], 1)
            products(pe, PHASES["ab"])

            pe.wait_ge(drained, 4 * PHASES["out_ab"].panel0 + 4)
            pe.wait_ge(R["att_in"], 16)
            for m in range(2 * H):
                if m >= 4:
                    pe.wait_ge(R["rot_m"], m - 3)
                mm(aux[m % 4][:, 0:T], rot, pt[:, QR + m, :], start=True, stop=True).then_inc(R["rot_p"], 1)

            def sb_scores(h):
                bk = banks[h % 2]
                k, q = pt[:, KA + h, :], pt[:, QA + h, :]
                if h >= 2:
                    pe.wait_ge(R["sbz_s"], h - 1)
                mm(bk[0][:, 0:256], k[:, 0:P], q[:, 0:SEQ], start=True, stop=True)
                mm(bk[0][:, 256:384], k[:, P:SEQ], q[:, P:SEQ], start=True, stop=True).then_inc(R["sbz"], 1)

            def sb_turn(h):
                bk, v = banks[h % 2], pt[:, VA + h, :]
                if h >= 2:
                    pe.wait_ge(R["sb_ycopy"], h - 1)
                turn(bk[2][:, 0:P], v[:, 0:P])
                turn(bk[2][:, P:SEQ], v[:, P:SEQ]).then_inc(R["sb_vt"], 1)

            def sb_sum(h):
                bk, lf = banks[h % 2], temps[h % 2][2]
                pe.wait_ge(R["sb_m"], h + 1)
                if h >= 2:
                    pe.wait_ge(R["sb_arg"], h - 1)
                mm(bk[1][:, 0:384], upper, lf, start=True, stop=False)
                mm(bk[1][:, P:SEQ], ones, lf[:, 256:384], start=False, stop=True).then_inc(R["sb_incl"], 1)

            def sb_out(h):
                bk, w, v = banks[h % 2], temps[h % 2][1], vtok[h % 2][:, 0, :]
                pe.wait_ge(R["sb_w"], h + 1)
                pe.wait_ge(R["sb_vs"], h + 1)
                y = bk[2][:, SEQ:2 * SEQ]
                mm(y, v[:, 0:P], w[:, 0:SEQ], start=True, stop=False)
                mm(y[:, P:SEQ], v[:, P:SEQ], w[:, 256:384], start=False, stop=True).then_inc(R["sb_y"], 1)

            def page_at(n):
                pe.wait_ge(R[f"page_in{n % NPB}"], 16 * (n // NPB + 1))
                return page[n % NPB]

            w = NB * H

            def page_scores(n):
                b, k = n // NPG, n % NPG
                pg = page_at(n)
                for h in range(H):
                    c = k * w + b * H + h
                    m = mm(aux[3][:, c:c + 1], pg[:, h, :], pt[:, QA + h, SEQ + b:SEQ + b + 1],
                           start=True, stop=True)
                m.then_inc(R["page_used"], 1)

            def page_values(n):
                b, k = n // NPG, n % NPG
                pg = page_at(NB * NPG + n)
                for h in range(H):
                    c = k * w + b * H + h
                    o = k * w + h * NB + b
                    m = mm(acc[3][:, o:o + 1], pg[:, h, :], temps[0][1][:, c:c + 1], start=True, stop=True)
                m.then_inc(R["page_used"], 1)

            pe.wait_ge(R["rot_done"], 2 * H)
            for t in range(H + 2):
                if t < H:
                    sb_scores(t)
                    page_scores(2 * t)
                if 1 <= t <= H:
                    sb_turn(t - 1)
                    sb_sum(t - 1)
                if t < H:
                    page_scores(2 * t + 1)
                if t >= 2:
                    sb_out(t - 2)

            def ret_scores(h):
                bk = banks[h % 2]
                k, q = pt[:, KR + h, :], pt[:, QR + h, :]
                if h >= 2:
                    pe.wait_ge(R["rt_stc"], h - 1)
                    pe.wait_ge(R["rt_k"], h - 1)
                mm(bk[0][:, 0:256], k[:, 0:P], q[:, 0:SEQ], start=True, stop=True)
                mm(bk[0][:, 256:384], k[:, P:SEQ], q[:, P:SEQ], start=True, stop=True).then_inc(R["rt_s"], 1)
                for c in range(2):
                    turn(bk[1][:, c * P:c * P + P], k[:, c * P:c * P + P])
                    for u in range(2):
                        m = turn(bk[2][:, c * 256 + u * P:c * 256 + u * P + P], pt[:, VR + 2 * h + u, c * P:c * P + P])
                m.then_inc(R["rt_t"], 1)

            def ret_out(h):
                bk, w, v, k = banks[h % 2], temps[h % 2][2], vtok[h % 2], ktw[h % 2]
                pe.wait_ge(R["rt_p"], h + 1)
                pe.wait_ge(R["rt_k"], h + 1)
                if h >= 1:
                    pe.wait_ge(R["rt_yc"], h)
                for u in range(2):
                    o = u * 256
                    mm(aux[3][:, o:o + 256], v[:, 0, u * P:u * P + P], w[:, 0:SEQ], start=True, stop=False)
                    m = mm(aux[3][:, o + P:o + 256], v[:, 1, u * P:u * P + P], w[:, 256:384], start=False, stop=True)
                m.then_inc(R["rt_y"], 1)
                mm(bk[0][:, 0:256], k[:, 0, :], v[:, 0, :], start=True, stop=False)
                mm(bk[0][:, 0:256], k[:, 1, :], v[:, 1, :], start=False, stop=True).then_inc(R["rt_st"], 1)

            pe.wait_ge(R["sb_ycopy"], H)
            ret_scores(0)
            lf = temps[0][2]
            pe.wait_ge(R["sb_lf"], H + 1)
            sums = acc[1][:, 0:2 * w]
            mm(sums, upper, lf[:, 0:2 * w], start=True, stop=False)
            mm(sums[:, 0:w], ones, lf[:, w:2 * w], start=False, stop=True).then_inc(R["sb_incl"], 1)
            pe.wait_ge(R["sb_arg"], H + 1)
            for t in range(1, H + 1):
                if t < H:
                    ret_scores(t)
                if t == 1:
                    pe.wait_ge(R["sb_w"], H + 1)
                page_values(2 * t - 2)
                ret_out(t - 1)
                page_values(2 * t - 1)
            pe.wait_ge(R["rt_yc"], H)
            pe.wait_ge(R["rt_stc"], H)
            pe.wait_ge(R["sb_ycopy"], H + 1)
            for h in range(H):
                turn(aux[h // 4][0:NB, (h % 4) * P:(h % 4) * P + P], pt[:, KR + h, SEQ:T])
            for t in range(2 * H):
                m = turn(acc[t // 4][0:NB, (t % 4) * P:(t % 4) * P + P], pt[:, VR + t, SEQ:T])
            m.then_inc(R["rs_t"], 1)

            def ret_outer(u):
                b = u // 2
                pe.wait_ge(R["rs_km"], b + 1)
                for k in range(4):
                    h = 4 * (u % 2) + k
                    if u >= 2 and k % 2 == 0:
                        pe.wait_ge(R["rs_new"], 4 * (u - 2) + k + 2)
                    m = mm(obank(h), ktm[b % 2][0:NB, h * P:h * P + P], vts[0:NB, h * 256:h * 256 + 256],
                           start=True, stop=True)
                    if k % 2:
                        m.then_inc(R["rs_o"], 1)

            def ret_read(u):
                b = u // 2
                pe.wait_ge(R["rs_new"], 4 * (u + 1))
                for k in range(4):
                    h = 4 * (u % 2) + k
                    for e in range(2):
                        c = (2 * h + e) * NB + b
                        m = mm(aux[2][:, c:c + 1], s0buf[u % NRB][:, k, e * P:e * P + P],
                               pt[:, QR + h, SEQ + b:SEQ + b + 1], start=True, stop=True)
                m.then_inc(R["rs_y"], 1)

            pe.wait_ge(R["sb_ycopy"], H + 1)
            ret_outer(0)
            for u in range(2 * NB):
                if u + 1 < 2 * NB:
                    ret_outer(u + 1)
                ret_read(u)
            for h in range(H):
                pe.wait_ge(R["rn_sq"], h + 1)
                for u in range(2):
                    m = mm(aux[0][0:H, 0:T], pick[:, 7 - h:15 - h], rsq[:, h % 2, u, :],
                           start=h == 0 and u == 0, stop=h == H - 1 and u == 1)
                m.then_inc(R["rn_sum"], 1)
            pe.wait_ge(R["rn_inv"], 1)
            for h in range(H):
                if h >= 4:
                    pe.wait_ge(R["rn_a"], h - 3)
                mm(acc[h % 4][:, 0:T], row_of(h, H), rinv[0:H, :], start=True, stop=True).then_inc(R["rn_bc"], 1)

            def norm(l):
                pe.wait_ge(R["ln_sum"], 17 * (l + 1))
                mm(aux[0][:, 0:T], ones, lsum[:, :], start=True, stop=True).then_inc(R["ln_mean"], 1)
                pe.wait_ge(R["ln_sqsum"], l + 1)
                mm(aux[1][:, 0:T], ones, lsum[:, :], start=True, stop=True).then_inc(R["ln_var"], 1)

            products(pe, PHASES["out_ab"])
            norm(0)
            pe.wait_ge(R["x_lo"], 2)
            products(pe, PHASES["up0"])
            products(pe, PHASES["down0"])
            norm(1)
            pe.wait_ge(R["x_lo"], 3)

            dt = PHASES["dt"]
            pe.wait_ge(lo_done, dt.chunk0 + 1)
            pe.wait_ge(drained, dt.panel0 * 4 + 1)
            for k in range(KT):
                w = slice(k * P, k * P + P)
                s, r = hi_slot(0, 1), raw_slot(0, 1)
                mm(acc[0][:, 0:T], hi[:, s, w], xh[:, k, :], start=k == 0, stop=False)
                mm(acc[0][:, 0:T], hi[:, s, w], xl[:, k, :], start=False, stop=False)
                m = mm(acc[0][:, 0:T], lo[:, r, w], xh[:, k, :], start=False, stop=k == KT - 1)
            m.then_inc(used, 1)
            products(pe, PHASES["ssd"])

            pe.wait_ge(R["dt_c"], 5)
            for c in range(2):
                s = slice(c * P, c * P + P)
                for k, v in enumerate((cumT, dtT, wendT)):
                    turn(aux[0][:, (2 * k + c) * NH:(2 * k + c) * NH + NH], v[0:NH, s])
            turn(aux[1][0:NB, 0:NH], dtT[0:NH, SEQ:T])
            turn(aux[1][0:NB, NH:2 * NH], cdT[0:NH, :]).then_inc(R["sm_t"], 1)
            pe.wait_ge(R["dt_c"], 7)
            for b in range(NB):
                m = mm(aux[2][:, b * NH:b * NH + NH], row_of(b, NB), cds[0:NB, :], start=True, stop=True)
            m.then_inc(R["cd_p"], 1)
            for q in range(G):
                if q >= 4:
                    pe.wait_ge(R["ss_x"], q - 3)
                for t in range(4):
                    m = turn(acc[q % 4][0:NB, t * P:t * P + P], pt[:, XS + 4 * q + t, SEQ:T])
                m.then_inc(R["ss_t"], 1)
            pe.wait_ge(R["ss_x"], G)

            def spread(n):
                b, g = n // G, n % G
                if n >= 4:
                    pe.wait_ge(R["ss_n"], n - 3)
                mm(acc[g % 4][:, :], row_of(b, NB), xds[0:NB, g * 512:g * 512 + 512], start=True, stop=True)\
                    .then_inc(R["ss_o"], 1)

            def read_state(n):
                b, g = n // G, n % G
                u = 2 * b + g // 4
                pe.wait_ge(R["ss_n"], n + 1)
                for t in range(4):
                    c = (4 * g + t) * NB + b
                    o = (g % 4) * 512 + t * P
                    m = mm(aux[3][:, c:c + 1], hbuf[u % NHB][:, o:o + P], pt[:, CM + g, SEQ + b:SEQ + b + 1],
                           start=True, stop=True)
                if g % 4 == 3:
                    m.then_inc(R["ss_y"], 1)

            for n in range(NB * G + 3):
                if n < NB * G:
                    spread(n)
                if n >= 3:
                    read_state(n - 3)

            pe.wait_ge(R["ss_ya"], 1)
            for g in range(G):
                bm, cm = pt[:, BM + g, :], pt[:, CM + g, :]
                if g >= 1:
                    pe.wait_ge(R["g_stc"], g)
                mm(aux[0][:, 0:256], bm[:, 0:P], cm[:, 0:SEQ], start=True, stop=True)
                mm(aux[0][:, 256:384], bm[:, P:SEQ], cm[:, P:SEQ], start=True, stop=True).then_inc(R["g_cb"], 1)
                if g >= 1:
                    pe.wait_ge(R["g_ssc"], g)
                for c in range(2):
                    m = turn(aux[1][:, c * P:c * P + P], bm[:, c * P:c * P + P])
                m.then_inc(R["g_bt"], 1)
                for c in range(2):
                    for t in range(4):
                        m = turn(acc[c][:, t * P:t * P + P], pt[:, XS + 4 * g + t, c * P:c * P + P])
                    m.then_inc(R["g_xt"], 1)

                def decays(q):
                    n = 4 * g + q
                    if n >= 2:
                        pe.wait_ge(R["g_arg"], 2 * (n - 1))
                    for k in range(2):
                        m = mm(acc[2 + n % 2][:, k * 256:k * 256 + 256], row_of(2 * n + k, NH), cumT[0:NH, :],
                               start=True, stop=True)
                    m.then_inc(R["g_bc"], 1)

                decays(0)
                for q in range(4):
                    if q < 3:
                        decays(q + 1)
                    n = 4 * g + q
                    if n >= 2:
                        pe.wait_ge(R["g_yd"], n - 1)
                    if q == 0:
                        pe.wait_ge(R["g_x"], g + 1)
                    for k in range(2):
                        h = 2 * n + k
                        pe.wait_ge(R["g_w"], h + 1)
                        o = (2 * q + k) * HD
                        y = aux[2 + n % 2][k * HD:k * HD + HD, :]
                        mm(y[:, 0:SEQ], xdt[0][:, 0, o:o + HD], wsb[h % 2][:, 0:SEQ], start=True, stop=False)
                        m = mm(y[:, P:SEQ], xdt[0][:, 1, o:o + HD], wsb[h % 2][:, 256:384], start=False, stop=True)
                        m.then_inc(R["g_yh"], 1)
                pe.wait_ge(R["g_btc"], g + 1)
                for t in range(4):
                    o = slice(t * P, t * P + P)
                    mm(aux[0][:, o], xw[0][:, 0, o], btok[0][:, 0, :], start=True, stop=False)
                    m = mm(aux[0][:, o], xw[0][:, 1, o], btok[0][:, 1, :], start=False, stop=True)
                m.then_inc(R["g_st"], 1)
                pe.wait_ge(R["g_sq"], g + 1)
                for t in range(4):
                    m = mm(aux[1][:, 0:T], ones, gsq[:, t, :], start=t == 0, stop=t == 3)
                m.then_inc(R["g_ss"], 1)

            products(pe, PHASES["out_ssd"])
            norm(2)
            pe.wait_ge(R["x_lo"], 4)
            products(pe, PHASES["up1"])
            products(pe, PHASES["down1"])
            norm(3)





def feature_major(a, axis=-1):
    a = np.moveaxis(np.asarray(a), axis, 0)
    return np.ascontiguousarray(np.moveaxis(a.reshape((-1, P) + a.shape[1:]), 1, 0))


def chunks(w, panels_of, kc):
    k, n = w.shape
    v = w.reshape(k // (CK * P), CK, P, n // (CN * P), CN * P)
    return v.transpose(3, 0, 2, 1, 4).reshape(-1, P, CW)


def kernel(**inputs):
    import concourse.bacc as bacc
    from concourse.bass_utils import run_bass_kernel_spmd

    g = {k: np.asarray(v) for k, v in inputs.items()}
    f32 = np.float32

    xp = np.concatenate([g["x_prompt"][0], g["x_sample"][:, 0]], 0)
    w_ab = g["w_in_ab"][0]
    cut = [0, 1024, 2048, 3072, 4096, 5120, 7168, 9216]
    qa, ka, va, qr, kr, vr, gr = (w_ab[:, a:b] for a, b in zip(cut, cut[1:]))
    w_ab = np.concatenate([qa, vr, ka, va, qr, kr, gr], 1)
    w_ssd = g["w_in_ssd"][0]
    w_z, w_xs, w_b, w_c, w_dt = (w_ssd[:, a:b] for a, b in ((0, 4096), (4096, 8192), (8192, 9216),
                                                            (9216, 10240), (10240, 10304)))
    dt_w = np.zeros((D, P), f32)
    dt_w[:, 0:NH] = w_dt
    pairs = np.arange(2 * FT).reshape(2, FT // 2, 2).transpose(1, 0, 2).reshape(-1)

    def by_pairs(a):
        v = a.reshape(a.shape[:-1] + (2 * FT, P))
        return v[..., pairs, :].reshape(a.shape)

    w = [chunks(w_ab, 18, 4), chunks(g["w_out_ab"][0], 4, 6)]
    for layer in range(DEPTH):
        if layer:
            w += [dt_w.reshape(KT, P, P).transpose(1, 0, 2).reshape(1, P, CW),
                  chunks(np.concatenate([w_b, w_c, w_xs, w_z], 1), 20, 4), chunks(g["w_out_ssd"][0], 4, 8)]
        w += [chunks(by_pairs(g["w_up"][layer]), 22, 4), chunks(g["w_down"][layer], 4, 11)]
    w = np.concatenate(w, 0)

    param = np.zeros((P, PARAM_W), f32)

    def put(name, a, rows=P):
        param[0:rows, PARAM[name][0]:PARAM[name][1]] = a.reshape(rows, -1)

    ln_g = np.stack([g["ln1_g"][0], g["ln2_g"][0], g["ln1_g"][1], g["ln2_g"][1]])
    ln_b = np.stack([g["ln1_b"][0], g["ln2_b"][0], g["ln1_b"][1], g["ln2_b"][1]])
    put("lng", ln_g.reshape(4, KT, P).transpose(2, 0, 1))
    put("lnb", ln_b.reshape(4, KT, P).transpose(2, 0, 1))
    put("sbias", np.broadcast_to(g["sb_bias"][0][None], (P, H)))
    put("fcw", by_pairs(g["conv_w_ffn"]).reshape(DEPTH, 3, 2 * FT, P).transpose(3, 0, 1, 2))
    put("fcb", by_pairs(g["conv_b_ffn"]).reshape(DEPTH, 2 * FT, P).transpose(2, 0, 1))

    def bcx(a):
        return np.concatenate([a[..., SSM_IN:], a[..., :SSM_IN]], -1)

    put("scw", bcx(g["conv_w_ssd"][0]).reshape(4, CT, P).transpose(2, 0, 1))
    put("scb", bcx(g["conv_b_ssd"][0]).reshape(CT, P).T)
    put("dskip", np.repeat(g["d_skip"][0], HD).reshape(XST, P).T)
    put("normw", g["norm_w_ssd"][0].reshape(XST, P).T)
    put("dtb", g["dt_bias"][0], NH)
    put("alog", g["a_log"][0], NH)

    arrays = {
        "x": xp.T.reshape(KT, P, T).transpose(1, 0, 2).reshape(P, KT * T),
        "w": w, "const": constants(), "param": param,
        "pages": g["page_table"].reshape(1, -1),
        "ck": g["cache_k"][0].transpose(0, 3, 2, 1),
        "cv": g["cache_v"][0],
        "ret0": g["state_ret"][0].transpose(0, 2, 1, 3).reshape(NB, P, H * 256),
        "ssm0": g["state_ssm"][0].transpose(0, 3, 1, 2).reshape(NB, P, SSM_IN),
        "sst": bcx(g["state_ssm_conv"][0]).reshape(NB, 3, CT, P).transpose(3, 2, 1, 0),
        "fst": by_pairs(g["state_ffn_conv"]).reshape(DEPTH, NB, 2, 2 * FT, P).transpose(0, 4, 3, 2, 1),
    }
    arrays = {k: np.ascontiguousarray(v) for k, v in arrays.items()}

    nc = bacc.Bacc("TRN2", target_bir_lowering=False, num_devices=1)
    d = {k: nc.dram_tensor(f"in_{k}", v.shape, mybir.dt.from_np(v.dtype), kind="ExternalInput").ap()
         for k, v in arrays.items()}
    for k, shape in OUT_SHAPES.items():
        d[k] = nc.dram_tensor(f"out_{k}", shape, F32, kind="ExternalOutput").ap()
    d["gate"] = nc.dram_tensor("gate", (P, XST, T), F32, kind="Internal").ap()
    d["xsave"] = nc.dram_tensor("xsave", (P, KT * T), F32, kind="Internal").ap()
    d["y"] = d["y"].rearrange("p t n -> p (t n)")
    build(nc, d)
    r = run_bass_kernel_spmd(nc, [{f"in_{k}": v for k, v in arrays.items()}], core_ids=[0]).results[0]
    o = {k: r[f"out_{k}"].reshape(s) for k, s in OUT_SHAPES.items()}

    def tokens(a):
        return a.transpose(2, 1, 0).reshape(a.shape[2], -1)

    y = tokens(o["y"])
    k, v = tokens(o["kv"][:, 0:H]), tokens(o["kv"][:, H:])
    back = np.argsort(pairs)

    def channels(a, undo):
        return np.moveaxis(a[:, undo], (1, 0), (-2, -1)).reshape(a.shape[2:] + (-1,))

    xbc = np.concatenate([np.arange(2 * G, CT), np.arange(2 * G)])
    sc, so = channels(o["sconv"], xbc), channels(o["sconv_old"], xbc)
    fc = np.stack([channels(o["fconv"][l], back) for l in range(DEPTH)])
    fo = np.stack([channels(o["fconv_old"][l], back) for l in range(DEPTH)])
    out = (
        y[None, 0:SEQ], y[SEQ:, None],
        k[None, None, 0:SEQ].reshape(1, 1, SEQ, H, P), v[0:SEQ].reshape(1, 1, SEQ, H, P),
        k[SEQ:].reshape(1, NB, 1, H, P), v[SEQ:].reshape(1, NB, 1, H, P),
        o["retp"].transpose(1, 0, 2)[None, None],
        o["rets"].reshape(NB, P, H, 256).transpose(0, 2, 1, 3)[None],
        o["ssmp"].transpose(1, 0, 2).reshape(1, 1, NH, HD, P),
        o["ssms"].reshape(NB, P, NH, HD).transpose(0, 2, 3, 1)[None],
        sc[None, None, 0:3],
        np.stack([so[0], so[1], sc[3:]], 1)[None],
        fc[:, None, 0:2],
        np.stack([fo, fc[:, 2:]], 2),
    )
    return tuple(np.ascontiguousarray(a) for a in out)
```

```python
from contextlib import ExitStack
import math

import numpy as np
import concourse.bass as bass
from concourse import mybir

F32 = mybir.dt.float32
F32R = mybir.dt.float32r
I32 = mybir.dt.int32
ALU = mybir.AluOpType
ACT = mybir.ActivationFunctionType
AX = mybir.AxisListType

P = 128
D = 2048
SEQ = 256
NB = 8
T = SEQ + NB
KT = D // P
H = 8
DEPTH = 2
PAST = 256
PAGE = 128
NPG = PAST // PAGE
NPHYS = 20
FF = 11 * D // 4
FT = FF // P
SSM_IN = 2 * D
XST = SSM_IN // P
G = 8
CT = XST + 2 * G
NH = 64
HD = 64
ALPHA = float((2 * DEPTH) ** 0.25)
EPS = 1e-5
SCALE = float(128 ** -0.5)
GAMMA = [1.0 - 2.0 ** (-5.0 - h) for h in range(H)]

QA, VR, KA, VA, QR, KR = 0, 8, 24, 32, 40, 48
AB_TILES = 56
BM, CM, XS = 0, 8, 16

CK = 4
CN = 4
CW = CK * CN * P
NRAW = 6
NHI = 4
XB = KT // CK
LOOK = 2


def raw_slot(j, body):
    return NRAW - 1 if body == 1 else (0, 1, 2, 3, 0, 1, 4, 5)[j] if body == 8 else j % NRAW


def hi_slot(j, body):
    return NHI - 1 if body == 1 else j % NHI


class Step:

    def __init__(self, base, reg=None):
        self.base, self.reg = base, reg

    def at(self, times, plus):
        fixed = self.base * times + plus
        return fixed if self.reg is None else self.reg * times + fixed

    def next(self):
        return Step(self.base + 1, self.reg)


class Phase:

    def __init__(self, name, iters, panels, kc, ring):
        self.name, self.iters, self.panels, self.kc, self.ring = name, iters, panels, kc, ring
        self.body = panels * kc

    def place(self, before):
        self.chunk0, self.panel0, self.acc0 = before


def plan():
    phases = [
        Phase("ab", 9, 2, 4, False), Phase("out_ab", 2, 2, 6, True),
        Phase("up0", 11, 2, 4, False), Phase("down0", 4, 1, 11, True),
        Phase("dt", 1, 1, 1, False), Phase("ssd", 10, 2, 4, False), Phase("out_ssd", 4, 1, 8, True),
        Phase("up1", 11, 2, 4, False), Phase("down1", 4, 1, 11, True),
    ]
    c = p = a = 0
    raw, hi = [], []
    for ph in phases:
        ph.place((c, p, a))
        c += ph.iters * ph.body
        p += ph.iters * ph.panels
        a += 0 if ph.name == "dt" else 3 * ph.iters * ph.panels
        for _ in range(ph.iters):
            raw += [raw_slot(j, ph.body) for j in range(ph.body)]
            hi += [hi_slot(j, ph.body) for j in range(ph.body)]
    uses = []
    count = [0] * NRAW
    for s in raw:
        count[s] += 1
        uses.append(count[s])

    def previous(slots):
        last, out = {}, []
        for n, s in enumerate(slots):
            out.append(last.get(s, -1))
            last[s] = n
        return out

    return {ph.name: ph for ph in phases}, phases, c, uses, previous(raw), previous(hi)


PHASES, ORDER, CHUNKS, USES, RAW_PREV, HI_PREV = plan()

CONST = {}


def const_layout():
    at = 0
    for name, width in (("ident", P), ("ones", P), ("upper", P), ("rot", P), ("mask", 384), ("cap", 384),
                        ("cosq", T), ("sinq", T), ("cosk", T), ("sink", T), ("decay", H * 384),
                        ("tend", 2 * H), ("sel", 2 * P + NH + NB), ("pick", 15)):
        CONST[name] = (at, at + width)
        at += width
    return at


CONST_W = const_layout()


def constants():
    c = np.zeros((P, CONST_W), np.float32)

    def put(name, a):
        c[:, CONST[name][0]:CONST[name][1]] = a

    j = np.arange(P)
    put("ident", np.eye(P))
    put("ones", np.ones((P, P)))
    put("upper", (j[:, None] >= j[None, :]))
    rot = np.zeros((P, P))
    for m in range(64):
        rot[m + 64, m] = -1.0
        rot[m, m + 64] = 1.0
    put("rot", rot)
    key = np.concatenate([np.tile(j[:, None], (1, 256)), np.tile(j[:, None] + 128, (1, 128))], 1)
    query = np.concatenate([np.arange(256), np.arange(128, 256)])[None, :]
    put("mask", key < query)
    part = np.where(j[:, None] <= j[None, :], 0.0, -1e30)
    by_head = j[:, None] % NH == np.arange(NH)[None, :]
    by_sample = (j[:, None] < 64) & (j[:, None] % 32 == np.arange(NB)[None, :])
    put("sel", np.concatenate([part, np.eye(P), by_head, by_sample], 1))
    put("pick", np.tile(np.arange(15) == 7, (P, 1)))
    put("cap", np.where(key < query, 0.0, -1e30))
    half = 64
    inv = (np.float32(10000.0) ** (-np.linspace(0.0, 1.0, half, dtype=np.float32))).astype(np.float32)
    pos = np.concatenate([np.arange(SEQ), np.full(NB, PAST)]).astype(np.float32)
    ang = (pos[None, :] * inv[:, None]).astype(np.float32)
    cos, sin = np.cos(ang, dtype=np.float32), np.sin(ang, dtype=np.float32)
    cos, sin = np.concatenate([cos, cos]), np.concatenate([sin, sin])
    put("cosq", cos)
    put("sinq", sin)
    put("cosk", cos * np.float32(SCALE))
    put("sink", sin * np.float32(SCALE))
    gap = (query - key).astype(np.float64)
    put("decay", np.concatenate([np.where(gap >= 0, g ** np.maximum(gap, 0), 0.0) for g in GAMMA], 1))
    put("tend", np.stack([g ** (255.0 - (ch * 128 + j)) for g in GAMMA for ch in range(2)], 1))
    return c


PARAM = {}


def param_layout():
    at = 0
    for name, width in (("lng", 4 * KT), ("lnb", 4 * KT), ("sbias", H), ("fcw", DEPTH * 3 * 2 * FT),
                        ("fcb", DEPTH * 2 * FT), ("scw", 4 * CT), ("scb", CT), ("dskip", XST),
                        ("normw", XST), ("dtb", 1), ("alog", 1)):
        PARAM[name] = (at, at + width)
        at += width
    return at


PARAM_W = param_layout()
OUT_SHAPES = {
    "y": (P, KT, T), "kv": (P, 2 * H, T), "retp": (P, H, 256), "rets": (NB, P, H * 256),
    "ssmp": (P, XST, P), "ssms": (NB, P, SSM_IN),
    "sconv": (P, CT, 11), "sconv_old": (P, CT, 2, NB), "fconv": (DEPTH, P, 2 * FT, 10),
    "fconv_old": (DEPTH, P, 2 * FT, NB),
}


SIGNALS = (
    "att_in", "cd_p", "cd_ready", "consts_in", "conv_base", "conv_silu", "conv_tap", "cum_hi", "cum_lo",
    "dt_a", "dt_c", "ffn_out", "ffn_state_in", "ffn_sum", "ffn_tile", "g_bc", "g_bt", "g_btc", "g_cb", "g_cbm",
    "g_e", "g_inv", "g_n", "g_out", "g_rb", "g_sq", "g_sqrt", "g_ss", "g_st", "g_stc", "g_w", "g_x", "g_xt",
    "g_yd", "g_yh", "g_z", "gate_in", "gate_out", "kv_out", "ln_a", "ln_cen", "ln_mean", "ln_norm", "ln_rstd",
    "ln_sq", "ln_sqrt", "ln_sum", "ln_var", "page_in0", "page_in1", "page_in2", "page_used", "pages_in",
    "rn_a", "rn_b", "rn_bc", "rn_inv", "rn_sq", "rn_sqrt", "rn_sum", "rot_c", "rot_done", "rot_m", "rot_p",
    "rs_in0", "rs_in1", "rs_in2", "rs_in3", "rs_in4", "rs_km", "rs_new", "rs_o", "rs_out0", "rs_out1",
    "rs_out2", "rs_out3", "rs_out4", "rs_t", "rs_tc", "rs_y", "rs_yc", "rt_k", "rt_out", "rt_p", "rt_s",
    "rt_st", "rt_stc", "rt_t", "rt_v", "rt_y", "rt_yc", "samples_out", "sb_L", "sb_arg", "sb_cap", "sb_e",
    "sb_incl", "sb_lf", "sb_m", "sb_na", "sb_part", "sb_vs", "sb_vt", "sb_w", "sb_y", "sb_ycopy", "sbz",
    "sbz_s", "sconv_in", "sconv_out", "sel_in", "sel_r", "sm_t", "small_set", "ss_h", "ss_in0", "ss_in1",
    "ss_in2", "ss_n", "ss_o", "ss_out0", "ss_out1", "ss_out2", "ss_t", "ss_x", "ss_xh", "ss_xl", "ss_y",
    "ss_ya", "ss_yd", "ssd_sum", "x_back", "x_hi", "x_in", "x_lo", "x_out", "xd_zero", "y_out", "z_in",
)


def build(nc, d):
    ctx = ExitStack()

    def sb(name, shape, dt=F32):
        return ctx.enter_context(nc.sbuf_tensor(name, shape, dt))

    def sem(name):
        return ctx.enter_context(nc.semaphore(name))

    with ctx:
        NHB = 3
        NRB = 5
        with nc.sbuf_tensor("lo", [P, NRAW, CW], F32R) as lo:
            pass
        raw = sb("raw", [P, NRAW, CW])
        with nc.sbuf_tensor("work", [P, 3 * KT * T], F32) as work:
            pass
        with nc.sbuf_tensor("workr", [P, 3 * KT * T], F32R) as workr:
            pass
        x_ = sb("x", [P, KT * T])
        xh = sb("xh", [P, KT, T], F32R)
        xl = sb("xl", [P, KT, T], F32R)
        pj = sb("pj", [P, AB_TILES * T])
        hi = sb("hi", [P, NHI, CW], F32R)
        cons = sb("cons", [P, 2 * P])
        pick = sb("pick", [P, 15])
        par = sb("par", [P, PARAM_W])
        with nc.sbuf_tensor("selr", [P, 2 * P + NH + NB], F32R) as selr:
            pass
        stage = sb("stage", [P, CN, T])
        small = sb("small", [P, 8])
        dtraw = sb("dtraw", [NH, T])
        lsum = sb("lsum", [P, T])
        pages_sb = sb("pages", [1, NB * NPG], I32)
        x = x_[:, :].rearrange("p (t n) -> p t n", n=T)
        pt = pj[:, :].rearrange("p (t n) -> p t n", n=T)
        ident, ones = cons[:, 0:P], cons[:, P:2 * P]
        eps_col, one_col = small[:, 0:1], small[:, 1:2]

        def par_of(name):
            return par[:, PARAM[name][0]:PARAM[name][1]]

        lng = par_of("lng").rearrange("p (l t) -> p l t", t=KT)
        lnb = par_of("lnb").rearrange("p (l t) -> p l t", t=KT)
        fcw = par_of("fcw").rearrange("p (l w t) -> p l w t", l=DEPTH, w=3)
        fcb = par_of("fcb").rearrange("p (l t) -> p l t", l=DEPTH)
        scw = par_of("scw").rearrange("p (w t) -> p w t", w=4)
        scb = par_of("scb")

        def carve(tensor, at, *shape):
            n = int(np.prod(shape))
            v = tensor[:, at:at + n]
            if len(shape) == 2:
                v = v.rearrange("p (a b) -> p a b", a=shape[0])
            elif len(shape) == 3:
                v = v.rearrange("p (a b c) -> p a b c", a=shape[0], b=shape[1])
            return v, at + n

        fst, at = carve(pj, FT * T, 2 * FT, 2, NB)
        fsum, at = carve(pj, at, 2 * FT, NB)
        fnew, at = carve(pj, at, 2 * FT, 10)
        sst, at = carve(pj, CT * T, CT, 3, NB)
        ssum, at = carve(pj, at, CT, NB)
        snew, at = carve(pj, at, CT, 11)
        ftmp = stage[:, :, :].rearrange("p a b -> p (a b)")[:, 0:2 * FT * NB].rearrange("p (a b) -> p a b", b=NB)
        stmp = stage[:, :, :].rearrange("p a b -> p (a b)")[:, 0:CT * NB].rearrange("p (a b) -> p a b", b=NB)

        acc = [ctx.enter_context(nc.psum_tensor(f"acc{n}", [P, 512], F32)) for n in range(4)]
        aux = [ctx.enter_context(nc.psum_tensor(f"aux{n}", [P, 512], F32)) for n in range(4)]
        banks = [aux, acc]

        at = 0
        upper, at = carve(work, at, P)
        rot, at = carve(work, at, P)
        mask, at = carve(work, at, 384)
        cap, at = carve(work, at, 384)
        trig, at = carve(work, at, 4, T)
        decay, at = carve(work, at, H, 384)
        tend, at = carve(work, at, H, 2)
        c0, c1 = CONST["upper"][0], CONST["tend"][1]
        assert at == c1 - c0, (at, c1 - c0)
        work_consts = work[:, 0:at]
        att0 = at
        temps = []
        for _ in range(2):
            zs, at = carve(work, at, 384)
            e_, at = carve(work, at, 384)
            lf, at = carve(work, at, 384)
            temps.append((zs, e_, lf))
        vtok = []
        ktw = []
        for _ in range(2):
            v, at = carve(work, at, 2, 256)
            vtok.append(v)
            v, at = carve(work, at, 2, P)
            ktw.append(v)
        NPB = 3
        pg0 = at
        page = []
        for _ in range(NPB):
            v, at = carve(work, at, H, P)
            page.append(v)
        retp, _ = carve(pj, KA * T, H, 256)
        assert at <= 3 * KT * T, (at, 3 * KT * T)
        at = att0
        s0buf = []
        for _ in range(NRB):
            v, at = carve(work, at, H // 2, 256)
            s0buf.append(v)
        vts, at = carve(work, at, 2048)
        assert at <= 3 * KT * T
        kts, _ = carve(work, c1 - c0 - H * 2 - H * 384, 1024)
        ktm = [carve(work, c1 - c0 - H * 2 - H * 384 + 1024 * (1 + n), 1024)[0] for n in range(2)]
        silg = pt[:, KA:KA + 2 * H, :]
        rinv, at = carve(work, KT * T, T)
        rsq, at = carve(work, at, 2, 2, T)

        at = 0
        cumT, at = carve(work, at, SEQ)
        dtT, at = carve(work, at, T)
        cumr, _ = carve(workr, at, SEQ)
        dte, at = carve(work, at, T)
        cdT, at = carve(work, at, NB)
        dA, at = carve(work, at, T)
        wendT, at = carve(work, at, SEQ)
        nctok, at = carve(work, at, 2, NH)
        dtok, at = carve(work, at, 2, NH)
        wend, at = carve(work, at, 2, NH)
        dts, at = carve(work, at, NH)
        cds, at = carve(work, at, NH)
        cdbc, at = carve(work, at, NB, NH)
        acol, at = carve(work, at, 1)
        ssm0 = at
        stage_ = stage[:, :, :].rearrange("p a b -> p (a b)")
        sel = stage_[:, 0:2 * P + NH + NB]
        block_cap, identr = selr[:, 0:P], selr[:, P:2 * P]
        by_head, by_sample = selr[:, 2 * P:2 * P + NH], selr[:, 2 * P + NH:2 * P + NH + NB]
        cbm0, at = carve(work, at, 384)
        btok0, at = carve(work, at, 2, P)
        xdt0, at = carve(work, at, 2, 512)
        xw0, at = carve(work, at, 2, 512)
        cbm = [cbm0, carve(stage_, 384, 384)[0]]
        btok = [btok0, carve(stage_, 768, 2, P)[0]]
        xdt = [xdt0, carve(pj, CT * T, 2, 512)[0]]
        xw = [xw0, carve(pj, CT * T + 1024, 2, 512)[0]]
        NE, NW = 4, 3
        esb = []
        for _ in range(NE):
            v, at = carve(work, at, 384)
            esb.append(v)
        wsb = []
        for _ in range(NW):
            v, at = carve(work, at, 384)
            wsb.append(v)
        hst, at = carve(work, at, 4, P)
        zg, at = carve(work, at, 4, T)
        gsq, at = carve(work, at, 4, T)
        ginv, at = carve(work, at, T)
        assert at <= 3 * KT * T, at
        at = ssm0
        xdr, at = carve(workr, at, SSM_IN)
        xtmp = [carve(pj, CT * T + 512 * n, 512)[0] for n in range(2)]
        hbuf = []
        for _ in range(NHB):
            v, at = carve(work, at, SSM_IN // 2)
            hbuf.append(v)
        assert at <= 3 * KT * T, at

        lsq = pt[:, 0:KT, :]
        lrt = pt[:, KT, :]
        conv_silu0 = {0: 0, "ssd": FT // 2, 1: FT // 2 + CT // CN}
        tap0 = {0: 0, "ssd": 2 * FT, 1: 2 * FT + 2 * CT}

        lead = [[(PHASES["up0"], 0), (PHASES["up0"], 1)], [(PHASES["dt"], 0), (PHASES["ssd"], 0), (PHASES["ssd"], 1)],
                [(PHASES["up1"], 0), (PHASES["up1"], 1)]]

        def obank(h):
            return acc[h // 2][:, (h % 2) * 256:(h % 2) * 256 + 256]

        def row_of(n, rows):
            return ident[0:rows, n:n + 1].to_broadcast([rows, P])

        landed = [sem(f"landed{s}") for s in range(NRAW)]
        hi_done = sem("hi_done")
        lo_done = sem("lo_done")
        used = sem("used")
        acc_done = sem("acc_done")
        drained = sem("drained")
        R = {n: sem(n) for n in SIGNALS}
        block = ctx.enter_context(nc.Block())

        def chunk_of(ph, i, j):
            return i.at(ph.body, ph.chunk0 + j)

        def load_chunk(eng, ph, i, j):
            n = ph.chunk0 + i.base * ph.body + j
            if RAW_PREV[n] >= 0:
                eng.wait_ge(used, i.at(ph.body, RAW_PREV[n] + 1 - i.base * ph.body))
            c, s = chunk_of(ph, i, j), raw_slot(j, ph.body)
            src = d["w"][c] if isinstance(c, int) else d["w"][bass.ds(c, 1)].rearrange("a p f -> (a p) f")
            eng.dma_start(raw[:, s, :], src).then_inc(landed[s], 16)

        def fill(ph, i, j):
            n = ph.chunk0 + j
            per = USES[n + ph.body] - USES[n] if ph.iters > 1 else 0
            return i.at(16 * per, 16 * USES[n])

        def hi_wait(ph, i, j):
            if i.reg is None:
                c = chunk_of(ph, i, j)
                back = c - HI_PREV[c] if HI_PREV[c] >= 0 else None
            else:
                back = min(n - HI_PREV[n] for n in (ph.chunk0 + k * ph.body + j for k in range(ph.iters))
                           if HI_PREV[n] >= 0)
            if back is None:
                return None
            if i.reg is not None:
                back = min(back, ph.chunk0 + i.base * ph.body + j)
            return i.at(ph.body, ph.chunk0 + j + 1 - back)

        def split_hi(act, ph, i, j, src):
            r = raw_slot(j, ph.body)
            act.wait_ge(landed[r], fill(ph, i, j))
            w = hi_wait(ph, i, j)
            if w is not None:
                act.wait_ge(used, w)
            if ph.ring:
                kc, s = j % ph.kc, j % 4
                act.activation(xh[:, CK * s:CK * s + CK, :], src[:, CK * kc:CK * kc + CK, :], ACT.Copy)
            act.activation(hi[:, hi_slot(j, ph.body), :], raw[:, r, :], ACT.Copy).then_inc(hi_done, 1)

        def split_lo(dve, ph, i, j, src):
            dve.wait_ge(hi_done, i.at(ph.body, ph.chunk0 + j + 1))
            if ph.ring:
                kc, s = j % ph.kc, j % 4
                dve.tensor_tensor(xl[:, CK * s:CK * s + CK, :], src[:, CK * kc:CK * kc + CK, :],
                                  xh[:, CK * s:CK * s + CK, :].bitcast(F32), ALU.subtract)
            r = raw_slot(j, ph.body)
            dve.tensor_tensor(lo[:, r, :], raw[:, r, :], hi[:, hi_slot(j, ph.body), :].bitcast(F32),
                              ALU.subtract).then_inc(lo_done, 1)

        def split_loop(eng, ph, split, src, evac, first=0, end=None, led=0, follow=None):
            end = ph.iters if end is None else end
            if first == 0:
                for j in range(led, min(LOOK, ph.body * ph.iters)):
                    split(eng, ph, Step(0), j, src)

            def body(i, last):
                since = Step(i.base - first, i.reg)
                for j in range(ph.body):
                    n = j + LOOK
                    if n < ph.body:
                        split(eng, ph, i, n, src)
                    elif not last:
                        split(eng, ph, i.next(), n - ph.body, src)
                    elif follow is not None:
                        follow(n - ph.body)
                    if j % ph.kc == ph.kc - 1:
                        evac(eng, ph, i, j // ph.kc, since.at(ph.panels, j // ph.kc))

            stop = end - 1 if end == ph.iters else end
            if stop - first > 1:
                with eng.Fori(0, stop - first) as r:
                    body(Step(first, r), False)
            elif stop > first:
                body(Step(first), False)
            if end == ph.iters:
                body(Step(end - 1), True)

        def wait_acc(eng, ph, i, pb, n):
            if n < 3:
                eng.wait_ge(acc_done, i.at(3 * ph.panels, ph.acc0 + 3 * pb + n + 1))
            else:
                eng.wait_ge(used, i.at(ph.body, ph.chunk0 + pb * ph.kc + ph.kc))

        def products(pe, ph, split=None):
            def body(i):
                for j in range(ph.body):
                    pb, kc = j // ph.kc, j % ph.kc
                    pe.wait_ge(lo_done, i.at(ph.body, ph.chunk0 + j + 1))
                    s, r = hi_slot(j, ph.body), raw_slot(j, ph.body)
                    if pb == 0 and split is not None:
                        pe.wait_ge(R["x_lo"], XB * split + kc + 1)
                    for n in range(CN):
                        if kc == 0:
                            pe.wait_ge(drained, i.at(4 * ph.panels, 4 * (ph.panel0 + pb) + n + 1))
                        for k in range(CK):
                            a = (j % 4 if ph.ring else kc) * CK + k
                            w = slice((k * CN + n) * P, (k * CN + n + 1) * P)
                            out = acc[n][:, 0:T]
                            pe.matmul(out, hi[:, s, w], xh[:, a, :], start=kc == 0 and k == 0, stop=False)
                            pe.matmul(out, hi[:, s, w], xl[:, a, :], start=False, stop=False)
                            m = pe.matmul(out, lo[:, r, w], xh[:, a, :], start=False,
                                          stop=kc == ph.kc - 1 and k == CK - 1)
                        if n < 3 and kc == ph.kc - 1:
                            m.then_inc(acc_done, 1)
                    m.then_inc(used, 1)

            with pe.Fori(0, ph.iters) as r:
                body(Step(0, r))

        @block.sync
        def _(sp):
            sp.dma_start(x_[:, :], d["x"]).then_inc(R["x_in"], 16)
            for ph in ORDER:
                for j in range(ph.body):
                    load_chunk(sp, ph, Step(0), j)
                if ph.iters > 1:
                    with sp.Fori(0, ph.iters - 1) as r:
                        for j in range(ph.body):
                            load_chunk(sp, ph, Step(1, r), j)

        @block.gpsimd
        def _(pool):
            pool.dma_start(cons[:, :], d["const"][:, 0:2 * P]).then_inc(R["consts_in"], 16)
            pool.dma_start(par[:, :], d["param"]).then_inc(R["consts_in"], 16)
            pool.dma_start(pick[:, :], d["const"][:, CONST["pick"][0]:CONST["pick"][1]]).then_inc(R["consts_in"], 16)
            pool.dma_start(pages_sb[:, :], d["pages"]).then_inc(R["pages_in"], 16)

            for n in range(4):
                pool.wait_ge(drained, 4 * (PHASES["ab"].panel0 + 14 + n) + 8)
                pool.dma_start(d["gate"][:, 4 * n:4 * n + 4, :], stage[:, :, :]).then_inc(R["gate_out"], 16)

            pool.wait_ge(used, PHASES["out_ab"].chunk0)
            pool.wait_ge(R["x_lo"], XB)
            pool.dma_start(work_consts, d["const"][:, c0:c1]).then_inc(R["att_in"], 16)
            pool.wait_ge(drained, 4 * PHASES["out_ab"].panel0 + 4)
            pool.dma_start(d["kv"], pt[:, KA:KA + 2 * H, :]).then_inc(R["kv_out"], 16)
            pool.wait_ge(R["pages_in"], 16)
            n = 0
            for cache in ("ck", "cv"):
                for b in range(NB):
                    for k in range(NPG):
                        v = pool.value_load(pages_sb[0:1, b * NPG + k:b * NPG + k + 1], min_val=0, max_val=NPHYS - 1)
                        if n >= NPB:
                            pool.wait_ge(R["page_used"], n - NPB + 1)
                        pool.dma_start(page[n % NPB], d[cache][bass.ds(v, 1)].rearrange("a p h f -> (a p) h f"))\
                            .then_inc(R[f"page_in{n % NPB}"], 16)
                        n += 1
            pool.wait_ge(R["rt_stc"], H)
            pool.dma_start(d["retp"], retp).then_inc(R["rt_out"], 16)
            pool.wait_ge(R["rt_out"], 16)

            units = 2 * NB

            def ret_half(array, u):
                return array[u // 2].rearrange("p (h e) -> p h e", h=H)[:, (u % 2) * 4:(u % 2) * 4 + 4, :]

            def ret_load(u):
                if u >= NRB:
                    pool.wait_ge(R["rs_y"], u - NRB + 1)
                    pool.wait_ge(R[f"rs_out{u % NRB}"], 16 * (u // NRB))
                pool.dma_start(s0buf[u % NRB], ret_half(d["ret0"], u)).then_inc(R[f"rs_in{u % NRB}"], 16)

            pool.wait_ge(R["sb_ycopy"], H + 1)
            pool.wait_ge(R["rt_yc"], H)
            pool.wait_ge(R["page_used"], 2 * NB * NPG)
            pool.wait_ge(R["kv_out"], 16)
            pool.wait_ge(R["gate_out"], 16 * 4)
            for u in range(NRB - 1):
                ret_load(u)
            pool.dma_start(silg, d["gate"][:, 0:2 * H, :]).then_inc(R["gate_in"], 16)
            for u in range(units):
                if u + NRB - 1 < units:
                    ret_load(u + NRB - 1)
                pool.wait_ge(R["rs_new"], 4 * (u + 1))
                pool.dma_start(ret_half(d["rets"], u), s0buf[u % NRB]).then_inc(R[f"rs_out{u % NRB}"], 16)
            pool.wait_ge(R["rs_y"], units)
            pool.dma_start(x_[:, :], d["x"]).then_inc(R["x_back"], 16)
            for n in range(NRB):
                pool.wait_ge(R[f"rs_out{n}"], 16 * ((units - n + NRB - 1) // NRB))

            def ffn(layer):
                pool.wait_ge(used, PHASES[f"up{layer}"].chunk0)
                if layer == 0:
                    pool.wait_ge(R["kv_out"], 16)
                else:
                    pool.wait_ge(R["sconv_out"], 32)
                pool.dma_start(fst, d["fst"][layer]).then_inc(R["ffn_state_in"], 16)
                up = PHASES[f"up{layer}"]
                pool.wait_ge(drained, 4 * (up.panel0 + up.iters * up.panels) + 4)
                pool.wait_ge(R["ffn_state_in"], 16 * (layer + 1))
                pool.dma_start(d["fconv"][layer], fnew).then_inc(R["ffn_out"], 16)
                pool.dma_start(d["fconv_old"][layer], fst[:, :, 1, :]).then_inc(R["ffn_out"], 16)

            ffn(0)
            pool.wait_ge(R["ffn_out"], 32)
            pool.wait_ge(used, PHASES["dt"].chunk0)
            pool.dma_start(sst, d["sst"]).then_inc(R["sconv_in"], 16)
            pool.wait_ge(R["ln_a"], 2 * KT)
            pool.dma_start(d["xsave"], x_[:, :]).then_inc(R["x_out"], 16)
            for n in range(8):
                pool.wait_ge(drained, 4 * (PHASES["ssd"].panel0 + 12 + n) + 8)
                pool.wait_ge(R["gate_in"], 16)
                pool.dma_start(d["gate"][:, 4 * n:4 * n + 4, :], stage[:, :, :]).then_inc(R["gate_out"], 16)
            pool.wait_ge(R["sconv_in"], 16)
            pool.dma_start(d["sconv"], snew).then_inc(R["sconv_out"], 16)
            pool.dma_start(d["sconv_old"], sst[:, :, 1:3, :]).then_inc(R["sconv_out"], 16)
            pool.wait_ge(used, PHASES["out_ssd"].chunk0)
            pool.wait_ge(R["x_out"], 16)
            pool.wait_ge(R["gate_out"], 16 * 12)
            pool.dma_start(sel, d["const"][:, CONST["sel"][0]:CONST["sel"][1]]).then_inc(R["sel_in"], 16)
            pool.memset(xdr[0:32, :].bitcast(F32), 0.0).then_inc(R["xd_zero"], 1)

            def state_load(u):
                b, half = u // 2, u % 2
                if u >= NHB:
                    pool.wait_ge(R["ss_y"], u - NHB + 1)
                    pool.wait_ge(R[f"ss_out{u % NHB}"], 16 * (u // NHB))
                pool.dma_start(hbuf[u % NHB], d["ssm0"][b][:, half * 2048:half * 2048 + 2048])\
                    .then_inc(R[f"ss_in{u % NHB}"], 16)

            units = 2 * NB
            state_load(0)
            state_load(1)
            for u in range(units):
                b, half = u // 2, u % 2
                if u + 2 < units:
                    state_load(u + 2)
                pool.wait_ge(R["ss_n"], 4 * (u + 1))
                pool.dma_start(d["ssms"][b][:, half * 2048:half * 2048 + 2048], hbuf[u % NHB])\
                    .then_inc(R[f"ss_out{u % NHB}"], 16)
            for s in range(NHB):
                pool.wait_ge(R[f"ss_out{s}"], 16 * ((units - s + NHB - 1) // NHB))
            pool.wait_ge(R["ss_y"], 2 * NB)
            pool.memset(small[0:1, 7:8], 1.0).then_inc(R["samples_out"], 1)
            pool.wait_ge(R["gate_out"], 16 * 12)
            for g in range(G):
                if g >= 1:
                    pool.wait_ge(R["g_z"], g)
                pool.dma_start(zg, d["gate"][:, 4 * g:4 * g + 4, :]).then_inc(R["z_in"], 16)
                pool.wait_ge(R["g_stc"], g + 1)
                pool.dma_start(d["ssmp"][:, 4 * g:4 * g + 4, :], hst).then_inc(R["g_out"], 16)
            pool.wait_ge(R["g_n"], XST)
            pool.wait_ge(R["g_out"], 16 * G)
            pool.dma_start(x_[:, :], d["xsave"]).then_inc(R["x_back"], 16)
            ffn(1)
            for q in range(XB):
                pool.wait_ge(R["ln_a"], 3 * KT + CK * (q + 1))
                part = slice(CK * T * q, CK * T * (q + 1))
                pool.dma_start(d["y"][:, part], x_[:, part]).then_inc(R["y_out"], 16)
            pool.wait_ge(R["y_out"], 16 * XB)
            pool.wait_ge(R["ffn_out"], 64)
            pool.wait_ge(R["rt_out"], 16)
            pool.wait_ge(R["kv_out"], 16)

        @block.scalar
        def _(act):
            a = act.activation

            def apart(eng):
                eng.wait_ge(R["consts_in"], 48)

            def copy_tiles(eng, ph, i, pb, q):
                for n in range(CN):
                    wait_acc(eng, ph, i, pb, n)
                    apart(eng)
                    t = q * CN + n
                    dst = pt[:, t, :] if isinstance(t, int) else pt[:, bass.ds(t, 1), :].rearrange("p a n -> p (a n)")
                    a(dst, acc[n][:, 0:T], ACT.Copy).then_inc(drained, 1)

            def gate_tiles(base):
                def evac(eng, ph, i, pb, q):
                    if base or q:
                        eng.wait_ge(R["gate_out"], q * 16 + base * 16)
                    for n in range(CN):
                        wait_acc(eng, ph, i, pb, n)
                        a(stage[:, n, :], acc[n][:, 0:T], ACT.Silu).then_inc(drained, 1)
                return evac

            def conv_base(w, bias, dst, silu):
                def evac(eng, ph, i, pb, q):
                    for n in range(CN):
                        wait_acc(eng, ph, i, pb, n)
                        apart(eng)
                        ch = q * CN + n
                        col = (lambda v: v[:, ch:ch + 1] if isinstance(ch, int) else v[:, bass.ds(ch, 1)])
                        a(dst(q, n), acc[n][:, 0:T], ACT.Identity, bias=col(bias), scale=col(w))\
                            .then_inc(R["conv_base"], 1)
                    eng.wait_ge(drained, i.at(4 * ph.panels, 4 * (ph.panel0 + pb) + 8))
                    a(small[:, 2:3], small[:, 1:2], ACT.Silu)
                    silu(q)
                return evac

            act.wait_ge(R["x_in"], 16)
            for k in range(0, KT, CK):
                a(xh[:, k:k + CK, :], x[:, k:k + CK, :], ACT.Copy).then_inc(R["x_hi"], 1)
            act.wait_ge(R["small_set"], 2)

            ab = PHASES["ab"]
            split_loop(act, ab, split_hi, None, copy_tiles, 0, 7)
            split_loop(act, ab, split_hi, None, gate_tiles(0), 7, 9)

            act.wait_ge(R["att_in"], 16)

            def sb_z(h):
                bk, (zs, e, lf) = banks[h % 2], temps[h % 2]
                act.wait_ge(R["sbz"], h + 1)
                if h >= 2:
                    act.wait_ge(R["sb_arg"], h - 1)
                a(zs, bk[0][:, 0:384], ACT.Identity, bias=par_of("sbias")[:, h:h + 1], scale=SCALE)\
                    .then_inc(R["sbz_s"], 1)

            def sb_values(h):
                bk = banks[h % 2]
                act.wait_ge(R["sb_vt"], h + 1)
                if h >= 2:
                    act.wait_ge(R["sb_y"], h - 1)
                a(vtok[h % 2][:, 0, :], bk[2][:, 0:256], ACT.Copy).then_inc(R["sb_vs"], 1)

            def sb_softplus(h, n=384):
                e = temps[h % 2][1][:, 0:n]
                act.wait_ge(R["sb_na"], h + 1)
                a(e, e, ACT.Exp).then_inc(R["sb_e"], 1)
                act.wait_ge(R["sb_e"], h + 1)
                a(e, e, ACT.Ln, bias=one_col).then_inc(R["sb_L"], 1)

            def sb_weight(h, n=384):
                e = temps[h % 2][1][:, 0:n]
                act.wait_ge(R["sb_cap"], h + 1)
                a(e, e, ACT.Exp).then_inc(R["sb_w"], 1)

            def sb_out(h):
                act.wait_ge(R["sb_y"], h + 1)
                a(pt[:, QA + h, 0:SEQ], banks[h % 2][2][:, SEQ:2 * SEQ], ACT.Copy).then_inc(R["sb_ycopy"], 1)

            for t in range(H + 2):
                if t < H:
                    sb_z(t)
                    sb_softplus(t)
                if 1 <= t <= H:
                    sb_values(t - 1)
                    sb_weight(t - 1)
                if t >= 2:
                    sb_out(t - 2)
            sb_softplus(H, 2 * NB * H)
            sb_weight(H, 2 * NB * H)

            for t in range(H + 1):
                if t < H:
                    h, bk = t, banks[t % 2]
                    act.wait_ge(R["rt_t"], h + 1)
                    if h >= 2:
                        act.wait_ge(R["rt_st"], h - 1)
                    a(vtok[h % 2].rearrange("p c e -> p (c e)"), bk[2][:, :], ACT.Copy).then_inc(R["rt_v"], 1)
                    for c in range(2):
                        ins = a(ktw[h % 2][:, c, :], bk[1][:, c * P:c * P + P], ACT.Identity,
                                scale=tend[:, h, c:c + 1])
                    ins.then_inc(R["rt_k"], 1)
                if t >= 1:
                    h = t - 1
                    act.wait_ge(R["rt_y"], h + 1)
                    a(pt[:, VR + 2 * h:VR + 2 * h + 2, 0:SEQ], aux[3][:, :].rearrange("p (u n) -> p u n", u=2),
                      ACT.Copy).then_inc(R["rt_yc"], 1)
            act.wait_ge(R["rs_t"], 1)
            act.wait_ge(R["rt_out"], 16)
            act.wait_ge(R["rt_p"], H)
            for q in range(4):
                a(vts[0:NB, q * 512:q * 512 + 512], acc[q][0:NB, :], ACT.Copy)
            for q in range(2):
                ins = a(kts[0:NB, q * 512:q * 512 + 512], aux[q][0:NB, :], ACT.Copy)
            ins.then_inc(R["rs_tc"], 1)
            act.wait_ge(R["rs_yc"], 1)
            act.wait_ge(R["rt_yc"], H)
            rest = 16 * ((2 * NB + NRB - 1) // NRB)
            act.wait_ge(R["rs_out0"], rest)
            for h in range(H):
                if h >= 2:
                    act.wait_ge(R["rn_sum"], h - 1)
                a(rsq[:, h % 2], pt[:, VR + 2 * h:VR + 2 * h + 2, :], ACT.Square).then_inc(R["rn_sq"], 1)
            act.wait_ge(R["rn_sum"], H)
            a(rinv[0:H, :], aux[0][0:H, 0:T], ACT.Sqrt, bias=eps_col[0:H, :], scale=1.0 / 256)\
                .then_inc(R["rn_sqrt"], 1)

            def norm(l, split, ahead=()):
                for ph, j in ahead:
                    split_hi(act, ph, Step(0), j, None)
                for k in range(0, KT, CK):
                    act.wait_ge(R["ln_cen"], XB * l + k // CK + 1)
                    a(lsq[:, k:k + CK, :], x[:, k:k + CK, :], ACT.Square).then_inc(R["ln_sq"], 1)
                act.wait_ge(R["ln_var"], l + 1)
                a(lrt, aux[1][:, 0:T], ACT.Sqrt, bias=eps_col, scale=1.0 / D).then_inc(R["ln_sqrt"], 1)
                for q in range(XB):
                    act.wait_ge(R["ln_norm"], XB * l + q + 1)
                    for t in range(CK * q, CK * q + CK):
                        a(x[:, t, :], x[:, t, :], ACT.Identity, bias=lnb[:, l, t:t + 1]).then_inc(R["ln_a"], 1)
                    if split:
                        act.wait_ge(R["ln_a"], KT * l + CK * (q + 1))
                        a(xh[:, CK * q:CK * q + CK, :], x[:, CK * q:CK * q + CK, :], ACT.Copy)\
                            .then_inc(R["x_hi"], 1)

            def no_evac(eng, ph, i, pb, q):
                pass

            def ffn(layer):
                up, down = PHASES[f"up{layer}"], PHASES[f"down{layer}"]

                def silu(q):
                    a(stage[:, 0:2, :], stage[:, 0:2, :], ACT.Silu).then_inc(R["conv_silu"], 1)

                base = conv_base(fcw[:, layer, 2, :], fcb[:, layer, :], lambda q, n: stage[:, n, :], silu)

                def evac(eng, ph, i, pb, q):
                    eng.wait_ge(R["ffn_tile"], q + (layer * (FT // 2) + 1))
                    base(eng, ph, i, pb, q)

                act.wait_ge(R["ffn_sum"], 3 * (layer + 1))

                def to_down(j):
                    act.wait_ge(R["ffn_tile"], layer * (FT // 2) + 1 + 2 * LOOK)
                    split_hi(act, down, Step(0), j, pt)

                split_loop(act, up, split_hi, None, evac, led=LOOK, follow=to_down)
                act.wait_ge(R["ffn_tile"], (layer + 1) * (FT // 2) + 1)
                split_loop(act, down, split_hi, pt, no_evac, led=LOOK)

            act.wait_ge(R["rn_a"], H)
            act.wait_ge(R["sb_ycopy"], H + 1)
            for n in range(NRB):
                act.wait_ge(R[f"rs_out{n}"], 16 * ((2 * NB - n + NRB - 1) // NRB))
            split_loop(act, PHASES["out_ab"], split_hi, pt, no_evac)
            norm(0, True, lead[0])
            ffn(0)
            norm(1, True, lead[1])

            act.wait_ge(used, PHASES["dt"].chunk0 + 1)
            a(dtraw[:, :], acc[0][0:NH, 0:T], ACT.Identity, bias=par_of("dtb")[0:NH, :]).then_inc(drained, 4)

            def xbc_tile(q, n):
                t = q * CN + n
                return pt[:, t, :] if isinstance(t, int) else pt[:, bass.ds(t, 1), :].rearrange("p a n -> p (a n)")

            def xbc_silu(q):
                v = pt[:, q * CN:q * CN + CN, :] if isinstance(q, int) else pt[:, bass.ds(q * CN, CN), :]
                a(v, v, ACT.Silu).then_inc(R["conv_silu"], 1)

            act.wait_ge(R["ssd_sum"], 5)
            split_loop(act, PHASES["ssd"], split_hi, None, conv_base(scw[:, 3, :], scb, xbc_tile, xbc_silu), 0, 6,
                       led=LOOK)
            split_loop(act, PHASES["ssd"], split_hi, None, gate_tiles(4), 6, 10)

            act.wait_ge(R["dt_c"], 1)
            a(dte[0:NH, :], dte[0:NH, :], ACT.Exp).then_inc(R["dt_a"], 1)
            act.wait_ge(R["dt_a"], 1)
            a(dte[0:NH, :], dte[0:NH, :], ACT.Ln, bias=one_col[0:NH, :]).then_inc(R["dt_a"], 1)
            a(acol[0:NH, :], par_of("alog")[0:NH, :], ACT.Exp).then_inc(R["dt_a"], 1)
            act.wait_ge(R["dt_c"], 4)
            a(wendT[0:NH, :], cumT[0:NH, :], ACT.Exp, bias=cumT[0:NH, SEQ - 1:SEQ], scale=-1.0).then_inc(R["dt_a"], 1)
            a(cdT[0:NH, :], dA[0:NH, SEQ:T], ACT.Exp).then_inc(R["dt_a"], 1)
            a(cumr[0:NH, :], cumT[0:NH, :], ACT.Copy).then_inc(R["cum_hi"], 1)
            act.wait_ge(R["sel_in"], 16)
            a(selr[:, :], sel, ACT.Copy).then_inc(R["sel_r"], 1)
            for q in range(G):
                act.wait_ge(R["ss_x"], q + 1)
                if q == 0:
                    act.wait_ge(R["xd_zero"], 1)
                a(xdr[0:NB, q * 512:q * 512 + 512], xtmp[q % 2][0:NB, :], ACT.Copy).then_inc(R["ss_xh"], 1)

            def group_bc(g):
                act.wait_ge(R["g_bt"], g + 1)
                if g >= 2:
                    act.wait_ge(R["g_st"], g - 1)
                a(btok[g % 2], acc[0][:, 0:256].rearrange("p (c s) -> p c s", c=2), ACT.Copy).then_inc(R["g_btc"], 1)
                act.wait_ge(R["g_cb"], g + 1)
                if g >= 2:
                    act.wait_ge(R["g_w"], 8 * (g - 1))
                a(cbm[g % 2], aux[0][:, 0:384], ACT.Copy).then_inc(R["g_cbm"], 1)

            def head_decay(n):
                bk, e = acc[1 + n % 3], esb[n % NE]
                act.wait_ge(R["g_bc"], n + 1)
                if n >= NE:
                    act.wait_ge(R["g_w"], n - NE + 1)
                a(e[:, 0:256], bk[:, 0:256], ACT.Exp, bias=nctok[:, 0, n:n + 1])
                a(e[:, 256:384], bk[:, 256:384], ACT.Exp, bias=nctok[:, 1, n:n + 1]).then_inc(R["g_e"], 1)

            def group_squares(g):
                act.wait_ge(R["g_z"], g + 1)
                if g >= 1:
                    act.wait_ge(R["g_ss"], g)
                a(gsq, pt[:, XS + 4 * g:XS + 4 * g + 4, :], ACT.Square).then_inc(R["g_sq"], 1)

            def group_state(g):
                act.wait_ge(R["g_st"], g + 1)
                if g >= 1:
                    act.wait_ge(R["g_out"], 16 * g)
                a(hst, aux[0][:, :].rearrange("p (t s) -> p t s", t=4), ACT.Copy).then_inc(R["g_stc"], 1)

            act.wait_ge(R["samples_out"], 1)
            act.wait_ge(R["ss_ya"], 1)
            group_bc(0)
            for g in range(G):
                for k in range(8):
                    head_decay(8 * g + k)
                    if k == 3 and g >= 1:
                        group_squares(g - 1)
                    if k == 4 and g >= 1:
                        group_state(g - 1)
                    if k == 5 and g + 1 < G:
                        group_bc(g + 1)
            group_state(G - 1)
            group_squares(G - 1)
            act.wait_ge(R["g_ss"], G)
            a(ginv[0:G, :], aux[1][0:G, 0:T], ACT.Sqrt, bias=eps_col[0:G, :], scale=1.0 / 512)\
                .then_inc(R["g_sqrt"], 1)
            act.wait_ge(R["g_n"], XST)
            act.wait_ge(R["g_out"], 16 * G)
            split_loop(act, PHASES["out_ssd"], split_hi, pt[:, XS:XS + XST, :], no_evac)
            norm(2, True, lead[2])
            ffn(1)
            norm(3, False)

        @block.vector
        def _(dve):
            tt, ts, stt = dve.tensor_tensor, dve.tensor_scalar, dve.scalar_tensor_tensor

            def no_evac(eng, ph, i, pb, q):
                pass

            def x_low(n, q):
                dve.wait_ge(R["x_hi"], XB * n + q + 1)
                k = slice(CK * q, CK * q + CK)
                tt(xl[:, k, :], x[:, k, :], xh[:, k, :].bitcast(F32), ALU.subtract).then_inc(R["x_lo"], 1)

            def residual(l):
                def evac(eng, ph, i, pb, q):
                    for n in range(CN):
                        wait_acc(eng, ph, i, pb, n)
                        t = q * CN + n
                        v = x[:, t, :] if isinstance(t, int) else x[:, bass.ds(t, 1), :].rearrange("p a n -> p (a n)")
                        stt(v, v, ALPHA, acc[n][:, 0:T], ALU.mult, ALU.add).then_inc(drained, 1)
                    for n in range(CN):
                        eng.wait_ge(drained, i.at(4 * ph.panels, 4 * (ph.panel0 + pb) + 4 + n + 1))
                        eng.wait_ge(R["ln_sum"], q * CN + (17 * l + n + 1))
                        t = q * CN + n
                        v = x[:, t, :] if isinstance(t, int) else x[:, bass.ds(t, 1), :].rearrange("p a n -> p (a n)")
                        tt(lsum[:, :], lsum[:, :], v, ALU.add).then_inc(R["ln_sum"], 1)
                return evac

            def clear_sum(l):
                if l:
                    dve.wait_ge(R["ln_var"], l)
                dve.memset(lsum[:, :], 0.0).then_inc(R["ln_sum"], 1)

            def taps(w, sums, new, tap0, conv0, dst, width, after):
                def evac(eng, ph, i, pb, q):
                    for n in range(CN):
                        ch = q * CN + n
                        one = (lambda v: v[:, ch:ch + 1] if isinstance(ch, int) else v[:, bass.ds(ch, 1)])
                        row = (lambda v: v[:, ch, :] if isinstance(ch, int)
                               else v[:, bass.ds(ch, 1), :].rearrange("p a n -> p (a n)"))
                        eng.wait_ge(R["conv_base"], q * CN + (conv0 + n + 1))
                        y, h = dst(q, n), acc[n]
                        tap = tap0 + n * (width - 2)
                        dve.tensor_copy(row(new), h[:, T - NB - (width - 1):T])
                        tt(y[:, SEQ:T], y[:, SEQ:T], row(sums), ALU.add)
                        for k in range(1, width):
                            if k > 1:
                                eng.wait_ge(R["conv_tap"], q * (CN * (width - 2)) + (tap + k - 1))
                            ins = stt(y[:, k:SEQ], h[:, 0:SEQ - k], one(w[:, width - 1 - k, :]), y[:, k:SEQ],
                                      ALU.mult, ALU.add)
                            ins.then_inc(R["conv_tap"] if k < width - 1 else drained, 1)
                    after(eng, ph, i, pb, q)
                return evac

            dve.memset(small[:, 7:8], 1.0).then_inc(R["ffn_tile"], 1)
            dve.memset(small[:, 0:1], EPS).then_inc(R["small_set"], 1)
            dve.memset(small[:, 1:7], 1.0).then_inc(R["small_set"], 1)
            for n in range(4):
                dve.memset(acc[n][:, :], 0.0).then_inc(drained, 1)
            for q in range(KT // CK):
                x_low(0, q)
            split_loop(dve, PHASES["ab"], split_lo, None, no_evac)

            dve.wait_ge(R["att_in"], 16)
            dve.wait_ge(drained, 4 * PHASES["out_ab"].panel0 + 4)
            for m in range(2 * H):
                tile = pt[:, QR + m, :]
                cos, sin = (trig[:, 0, :], trig[:, 1, :]) if m < H else (trig[:, 2, :], trig[:, 3, :])
                t = temps[m % 2][0][:, 0:T]
                dve.wait_ge(R["rot_p"], m + 1)
                tt(t, sin, aux[m % 4][:, 0:T], ALU.mult).then_inc(R["rot_m"], 1)
                tt(tile, tile, cos, ALU.mult).then_inc(R["rot_c"], 1)
                dve.wait_ge(R["rot_m"], m + 1)
                dve.wait_ge(R["rot_c"], m + 1)
                tt(tile, tile, t, ALU.add).then_inc(R["rot_done"], 1)
            dve.wait_ge(R["rot_done"], 2 * H)

            def sb_neg(h, n=384):
                zs, e, _ = temps[h % 2]
                dve.wait_ge(R["sbz_s"], h + 1)
                if h >= 2:
                    dve.wait_ge(R["sb_y"], h - 1)
                stt(e[:, 0:n], zs[:, 0:n], -1.0, zs[:, 0:n], ALU.mult, ALU.min).then_inc(R["sb_na"], 1)

            def sb_fail(h, n=384):
                zs, e, lf = (v[:, 0:n] for v in temps[h % 2])
                dve.wait_ge(R["sb_L"], h + 1)
                stt(lf, zs, 0.0, e, ALU.max, ALU.add).then_inc(R["sb_lf"], 1)
                if h < H:
                    dve.wait_ge(R["sb_lf"], h + 1)
                    tt(lf, lf, mask, ALU.mult).then_inc(R["sb_m"], 1)

            def sb_arg(h, n=384):
                zs, e, _ = (v[:, 0:n] for v in temps[h % 2])
                dve.wait_ge(R["sb_incl"], h + 1)
                tt(e, zs, banks[h % 2 if h < H else 1][1][:, 0:n], ALU.subtract).then_inc(R["sb_arg"], 1)
                dve.wait_ge(R["sb_arg"], h + 1)
                if h < H:
                    tt(e, e, cap, ALU.min).then_inc(R["sb_cap"], 1)
                else:
                    ts(e, e, 0.0, None, ALU.min).then_inc(R["sb_cap"], 1)

            for t in range(H + 1):
                if t < H:
                    sb_neg(t)
                if t >= 1:
                    sb_arg(t - 1)
                if t < H:
                    sb_fail(t)
            dve.wait_ge(R["page_used"], NB * NPG)
            zs = temps[0][0][:, 0:2 * NB * H]
            v3 = (lambda v: v.rearrange("p (a h) -> p a h", h=H))
            stt(v3(zs), v3(aux[3][:, 0:2 * NB * H]), SCALE,
                par_of("sbias").unsqueeze(1).to_broadcast([P, 2 * NB, H]), ALU.mult, ALU.add).then_inc(R["sbz_s"], 1)
            sb_neg(H, 2 * NB * H)
            sb_fail(H, 2 * NB * H)
            sb_arg(H, 2 * NB * H)
            for t in range(H + 1):
                if t < H:
                    h = t
                    dve.wait_ge(R["rt_s"], h + 1)
                    if h >= 2:
                        dve.wait_ge(R["rt_y"], h - 1)
                    tt(temps[h % 2][2], decay[:, h, :], banks[h % 2][0][:, 0:384], ALU.mult).then_inc(R["rt_p"], 1)
                if t >= 1:
                    h = t - 1
                    dve.wait_ge(R["rt_st"], h + 1)
                    if h == 0:
                        dve.wait_ge(R["kv_out"], 16)
                    dve.tensor_copy(retp[:, h, :], banks[h % 2][0][:, 0:256]).then_inc(R["rt_stc"], 1)

            dve.wait_ge(R["page_used"], 2 * NB * NPG)
            part = temps[1][0][:, 0:NB * H]
            dve.tensor_copy(part, acc[3][:, NB * H:2 * NB * H]).then_inc(R["sb_part"], 1)
            dve.wait_ge(R["sb_part"], 1)
            tt(pt[:, QA:QA + H, SEQ:T], part.rearrange("p (h b) -> p h b", b=NB),
               acc[3][:, 0:NB * H].rearrange("p (h b) -> p h b", b=NB), ALU.add).then_inc(R["sb_ycopy"], 1)

            def key_of(b):
                if b >= 2:
                    dve.wait_ge(R["rs_o"], 4 * (b - 1))
                ts(ktm[b % 2][0:NB, :], kts[0:NB, :], ident[0:NB, b:b + 1], None, ALU.mult).then_inc(R["rs_km"], 1)

            dve.wait_ge(R["rs_tc"], 1)
            key_of(0)
            key_of(1)
            for u in range(2 * NB):
                dve.wait_ge(R[f"rs_in{u % NRB}"], 16 * (u // NRB + 1))
                for k in range(4):
                    h = 4 * (u % 2) + k
                    dve.wait_ge(R["rs_o"], 2 * u + k // 2 + 1)
                    v = s0buf[u % NRB][:, k, :]
                    stt(v, v, float(GAMMA[h]), obank(h), ALU.mult, ALU.add).then_inc(R["rs_new"], 1)
                if u % 2 and u // 2 + 2 < NB:
                    key_of(u // 2 + 2)
            dve.wait_ge(R["rs_y"], 2 * NB)
            dve.tensor_copy(pt[:, VR:VR + 2 * H, SEQ:T], aux[2][:, 0:2 * H * NB].rearrange("p (t b) -> p t b", b=NB))\
                .then_inc(R["rs_yc"], 1)
            dve.wait_ge(R["gate_in"], 16)
            dve.wait_ge(R["rn_sq"], H)
            v = pt[:, VR:VR + 2 * H, :]
            tt(v, v, silg, ALU.mult).then_inc(R["rn_b"], 1)
            dve.wait_ge(R["rn_sqrt"], 1)
            dve.reciprocal(rinv[0:H, :], rinv[0:H, :]).then_inc(R["rn_inv"], 1)
            dve.wait_ge(R["rn_b"], 1)
            for h in range(H):
                dve.wait_ge(R["rn_bc"], h + 1)
                v = pt[:, VR + 2 * h:VR + 2 * h + 2, :]
                tt(v, v, acc[h % 4][:, 0:T].unsqueeze(1).to_broadcast([P, 2, T]), ALU.mult).then_inc(R["rn_a"], 1)

            def norm(l, split, ahead=()):
                dve.wait_ge(R["ln_mean"], l + 1)
                for k in range(0, KT, CK):
                    v = x[:, k:k + CK, :]
                    stt(v, aux[0][:, 0:T].unsqueeze(1).to_broadcast([P, CK, T]), -1.0 / D, v, ALU.mult, ALU.add)\
                        .then_inc(R["ln_cen"], 1)
                for ph, j in ahead:
                    split_lo(dve, ph, Step(0), j, None)
                dve.wait_ge(R["ln_sqrt"], l + 1)
                dve.reciprocal(lrt, lrt).then_inc(R["ln_rstd"], 1)
                dve.wait_ge(R["ln_rstd"], l + 1)
                dve.wait_ge(R["ln_cen"], XB * (l + 1))
                for q in range(XB + 1):
                    if q < XB:
                        for t in range(CK * q, CK * q + CK):
                            ins = stt(x[:, t, :], x[:, t, :], lng[:, l, t:t + 1], lrt, ALU.mult, ALU.mult)
                        ins.then_inc(R["ln_norm"], 1)
                    if q and split:
                        x_low(l + 1, q - 1)

            def ffn(layer):
                up, down = PHASES[f"up{layer}"], PHASES[f"down{layer}"]
                dve.wait_ge(R["ffn_state_in"], 16 * (layer + 1))
                for k, o in ((0, fsum), (1, ftmp)):
                    w = fcw[:, layer, k, :].unsqueeze(2).to_broadcast([P, 2 * FT, NB])
                    tt(o, fst[:, :, k, :], w, ALU.mult).then_inc(R["ffn_sum"], 1)
                dve.wait_ge(R["ffn_sum"], 3 * layer + 2)
                tt(fsum, fsum, ftmp, ALU.add).then_inc(R["ffn_sum"], 1)
                dve.wait_ge(R["ffn_sum"], 3 * layer + 3)

                def product(eng, ph, i, pb, q):
                    eng.wait_ge(R["conv_silu"], q + (conv_silu0[layer] + 1))
                    v = pt[:, 2 * q:2 * q + 2, :] if isinstance(q, int) else pt[:, bass.ds(q * 2, 2), :]
                    tt(v, stage[:, 0:2, :], stage[:, 2:4, :], ALU.mult).then_inc(R["ffn_tile"], 1)

                ev = taps(fcw[:, layer], fsum, fnew, tap0[layer], 4 * conv_silu0[layer],
                          lambda q, n: stage[:, n, :], 3, product)

                def to_down(j):
                    dve.wait_ge(R["ffn_tile"], layer * (FT // 2) + 1 + 2 * LOOK)
                    split_lo(dve, down, Step(0), j, pt)

                split_loop(dve, up, split_lo, None, ev, led=LOOK, follow=to_down)
                dve.wait_ge(R["ffn_tile"], (layer + 1) * (FT // 2) + 1)
                clear_sum(2 * layer + 1)
                split_loop(dve, down, split_lo, pt, residual(2 * layer + 1), led=LOOK)

            dve.wait_ge(R["rn_a"], H)
            dve.wait_ge(R["x_back"], 16)
            clear_sum(0)
            split_loop(dve, PHASES["out_ab"], split_lo, pt, residual(0))
            norm(0, True, lead[0])
            ffn(0)
            norm(1, True, lead[1])

            dve.wait_ge(R["sconv_in"], 16)
            wb = (lambda k: scw[:, k, :].unsqueeze(2).to_broadcast([P, CT, NB]))
            tt(ssum, sst[:, :, 0, :], wb(0), ALU.mult).then_inc(R["ssd_sum"], 1)
            for k in (1, 2):
                tt(stmp, sst[:, :, k, :], wb(k), ALU.mult).then_inc(R["ssd_sum"], 1)
                dve.wait_ge(R["ssd_sum"], 2 * k)
                tt(ssum, ssum, stmp, ALU.add).then_inc(R["ssd_sum"], 1)
                dve.wait_ge(R["ssd_sum"], 2 * k + 1)

            def xbc_tile(q, n):
                t = q * CN + n
                return pt[:, t, :] if isinstance(t, int) else pt[:, bass.ds(t, 1), :].rearrange("p a n -> p (a n)")

            ssd = PHASES["ssd"]
            ev = taps(scw, ssum, snew, tap0["ssd"], 4 * conv_silu0["ssd"], xbc_tile, 4,
                      lambda *a: None)
            split_loop(dve, ssd, split_lo, None, ev, 0, 6, led=LOOK)
            split_loop(dve, ssd, split_lo, None, no_evac, 6, 10)

            dve.wait_ge(used, PHASES["out_ssd"].chunk0)
            dve.wait_ge(R["x_out"], 16)
            dve.wait_ge(drained, 4 * PHASES["out_ssd"].panel0 + 4)
            r = dtraw[:, :]
            stt(dte[0:NH, :], r, -1.0, r, ALU.mult, ALU.min).then_inc(R["dt_c"], 1)
            dve.wait_ge(R["dt_a"], 3)
            stt(dtT[0:NH, :], r, 0.0, dte[0:NH, :], ALU.max, ALU.add).then_inc(R["dt_c"], 1)
            dve.wait_ge(R["dt_c"], 2)
            ts(dA[0:NH, :], dtT[0:NH, :], acol[0:NH, :], -1.0, ALU.mult, ALU.mult).then_inc(R["dt_c"], 1)
            dve.wait_ge(R["dt_c"], 3)
            dve.tensor_tensor_scan(cumT[0:NH, :], one_col[0:NH, :].to_broadcast([NH, SEQ]), dA[0:NH, 0:SEQ], 0.0,
                                   ALU.mult, ALU.add).then_inc(R["dt_c"], 1)
            dve.wait_ge(R["dt_a"], 5)
            tt(wendT[0:NH, :], wendT[0:NH, :], dtT[0:NH, 0:SEQ], ALU.mult).then_inc(R["dt_c"], 1)
            dve.wait_ge(R["cum_hi"], 1)
            tt(cumr[NH:2 * NH, :], cumT[0:NH, :], cumr[0:NH, :].bitcast(F32), ALU.subtract).then_inc(R["cum_lo"], 1)
            dve.wait_ge(R["sm_t"], 1)
            flat = (lambda v: v.rearrange("p c h -> p (c h)"))
            ts(flat(nctok), aux[0][:, 0:2 * NH], -1.0, None, ALU.mult).then_inc(R["dt_c"], 1)
            dve.tensor_copy(flat(dtok), aux[0][:, 2 * NH:4 * NH])
            dve.tensor_copy(flat(wend), aux[0][:, 4 * NH:6 * NH])
            dve.tensor_copy(dts[0:NB, :], aux[1][0:NB, 0:NH])
            dve.tensor_copy(cds[0:NB, :], aux[1][0:NB, NH:2 * NH]).then_inc(R["dt_c"], 1)
            dve.wait_ge(R["cd_p"], 1)
            dve.tensor_copy(cdbc.rearrange("p b h -> p (b h)"), aux[2][:, :]).then_inc(R["cd_ready"], 1)
            dve.wait_ge(R["dt_c"], 7)
            dve.wait_ge(R["sconv_out"], 32)
            dve.wait_ge(R["xd_zero"], 1)

            def low_part(q):
                dve.wait_ge(R["ss_xh"], q + 1)
                o = slice(q * 512, q * 512 + 512)
                tt(xdr[32:32 + NB, o], xtmp[q % 2][0:NB, :], xdr[0:NB, o].bitcast(F32), ALU.subtract)\
                    .then_inc(R["ss_xl"], 1)

            for q in range(G + 1):
                if q < G:
                    dve.wait_ge(R["ss_t"], q + 1)
                    if q >= 2:
                        dve.wait_ge(R["ss_xl"], q - 1)
                    tt(xtmp[q % 2][0:NB, :].rearrange("p (h e) -> p h e", e=HD),
                       dts[0:NB, 8 * q:8 * q + 8].unsqueeze(2).to_broadcast([NB, 8, HD]),
                       acc[q % 4][0:NB, :].rearrange("p (h e) -> p h e", e=HD), ALU.mult).then_inc(R["ss_x"], 1)
                if q >= 1:
                    low_part(q - 1)

            def decay_state(u):
                b, half = u // 2, u % 2
                dve.wait_ge(R[f"ss_in{u % NHB}"], 16 * (u // NHB + 1))
                hv = hbuf[u % NHB].rearrange("p (h q) -> p h q", q=HD)
                f = cdbc[:, b, 32 * half:32 * half + 32].unsqueeze(2).to_broadcast([P, 32, HD])
                tt(hv, hv, f, ALU.mult).then_inc(R["ss_h"], 1)

            dve.wait_ge(R["cd_ready"], 1)
            for b in range(NB):
                for g in range(G):
                    u = 2 * b + g // 4
                    if g % 4 == 0:
                        decay_state(u)
                    dve.wait_ge(R["ss_o"], G * b + g + 1)
                    dve.wait_ge(R["ss_h"], u + 1)
                    v = hbuf[u % NHB][:, (g % 4) * 512:(g % 4) * 512 + 512]
                    stt(v, acc[g % 4][:, :], pt[:, BM + g, SEQ + b:SEQ + b + 1], v, ALU.mult, ALU.add)\
                        .then_inc(R["ss_n"], 1)
            dve.wait_ge(R["ss_y"], 2 * NB)
            xs_s = pt[:, XS:XS + XST, SEQ:T]
            tt(xs_s, xs_s, par_of("dskip").unsqueeze(2).to_broadcast([P, XST, NB]), ALU.mult).then_inc(R["ss_yd"], 1)
            dve.wait_ge(R["ss_yd"], 1)
            tt(xs_s, xs_s, aux[3][:, 0:XST * NB].rearrange("p (t b) -> p t b", b=NB), ALU.add).then_inc(R["ss_ya"], 1)

            dskip, normw = par_of("dskip"), par_of("normw")
            dve.wait_ge(R["samples_out"], 1)

            def inputs(g, c):
                dve.wait_ge(R["g_xt"], 2 * g + c + 1)
                if g >= 2:
                    dve.wait_ge(R["g_yh"], 8 * (g - 1))
                    dve.wait_ge(R["g_st"], g - 1)
                src = acc[0][:, :].rearrange("p (h e) -> p h e", e=HD)
                for o, f in ((xdt[g % 2], dtok), (xw[g % 2], wend)):
                    ins = tt(o[:, c, :].rearrange("p (h e) -> p h e", e=HD),
                             f[:, c, 8 * g:8 * g + 8].unsqueeze(2).to_broadcast([P, 8, HD]), src, ALU.mult)
                ins.then_inc(R["g_x"], 1)

            def weights(n):
                dve.wait_ge(R["g_e"], n + 1)
                dve.wait_ge(R["g_cbm"], n // 8 + 1)
                if n >= NW:
                    dve.wait_ge(R["g_yh"], n - NW + 1)
                tt(wsb[n % NW], esb[n % NE], cbm[(n // 8) % 2], ALU.mult).then_inc(R["g_w"], 1)

            def pair_out(n):
                dve.wait_ge(R["g_yh"], 2 * n + 2)
                v = pt[:, XS + n, 0:SEQ]
                stt(v, v, dskip[:, n:n + 1], aux[2 + n % 2][:, 0:SEQ], ALU.mult, ALU.add).then_inc(R["g_yd"], 1)

            def gate(g):
                dve.wait_ge(R["z_in"], 16 * (g + 1))
                dve.wait_ge(R["g_yd"], 4 * g + 4)
                v = pt[:, XS + 4 * g:XS + 4 * g + 4, :]
                tt(v, v, zg, ALU.mult).then_inc(R["g_z"], 1)

            inputs(0, 0)
            inputs(0, 1)
            for g in range(G):
                for k in range(8):
                    n = 8 * g + k
                    weights(n)
                    if k % 2 and n >= 3:
                        pair_out(n // 2 - 1)
                    if k == 1 and g >= 1:
                        gate(g - 1)
                    if k == 6 and g + 1 < G:
                        inputs(g + 1, 0)
                    if k == 7 and g + 1 < G:
                        inputs(g + 1, 1)
            pair_out(4 * G - 1)
            gate(G - 1)
            dve.wait_ge(R["g_sqrt"], 1)
            dve.reciprocal(ginv[0:G, :], ginv[0:G, :]).then_inc(R["g_inv"], 1)
            for t in range(XST):
                dve.wait_ge(R["g_rb"], t // 4 + 1)
                v = pt[:, XS + t, :]
                stt(v, v, normw[:, t:t + 1], acc[(t // 4) % 4][:, 0:T], ALU.mult, ALU.mult).then_inc(R["g_n"], 1)
            dve.wait_ge(R["g_n"], XST)
            dve.wait_ge(R["x_back"], 32)
            clear_sum(2)
            split_loop(dve, PHASES["out_ssd"], split_lo, pt[:, XS:XS + XST, :], residual(2))
            norm(2, True, lead[2])
            ffn(1)
            norm(3, False)

        @block.tensor
        def _(pe):
            mm = pe.matmul

            def turn(out, src):
                k = src.shape[0]
                return pe.transpose(out, src, ident[0:k, 0:k])

            products(pe, PHASES["ab"], 0)
            pe.wait_ge(R["consts_in"], 48)

            pe.wait_ge(drained, 4 * PHASES["out_ab"].panel0 + 4)
            pe.wait_ge(R["att_in"], 16)
            for m in range(2 * H):
                if m >= 4:
                    pe.wait_ge(R["rot_m"], m - 3)
                mm(aux[m % 4][:, 0:T], rot, pt[:, QR + m, :], start=True, stop=True).then_inc(R["rot_p"], 1)

            def sb_scores(h):
                bk = banks[h % 2]
                k, q = pt[:, KA + h, :], pt[:, QA + h, :]
                if h >= 2:
                    pe.wait_ge(R["sbz_s"], h - 1)
                mm(bk[0][:, 0:256], k[:, 0:P], q[:, 0:SEQ], start=True, stop=True)
                mm(bk[0][:, 256:384], k[:, P:SEQ], q[:, P:SEQ], start=True, stop=True).then_inc(R["sbz"], 1)

            def sb_turn(h):
                bk, v = banks[h % 2], pt[:, VA + h, :]
                if h >= 2:
                    pe.wait_ge(R["sb_ycopy"], h - 1)
                turn(bk[2][:, 0:P], v[:, 0:P])
                turn(bk[2][:, P:SEQ], v[:, P:SEQ]).then_inc(R["sb_vt"], 1)

            def sb_sum(h):
                bk, lf = banks[h % 2], temps[h % 2][2]
                pe.wait_ge(R["sb_m"], h + 1)
                if h >= 2:
                    pe.wait_ge(R["sb_arg"], h - 1)
                mm(bk[1][:, 0:384], upper, lf, start=True, stop=False)
                mm(bk[1][:, P:SEQ], ones, lf[:, 256:384], start=False, stop=True).then_inc(R["sb_incl"], 1)

            def sb_out(h):
                bk, w, v = banks[h % 2], temps[h % 2][1], vtok[h % 2][:, 0, :]
                pe.wait_ge(R["sb_w"], h + 1)
                pe.wait_ge(R["sb_vs"], h + 1)
                y = bk[2][:, SEQ:2 * SEQ]
                mm(y, v[:, 0:P], w[:, 0:SEQ], start=True, stop=False)
                mm(y[:, P:SEQ], v[:, P:SEQ], w[:, 256:384], start=False, stop=True).then_inc(R["sb_y"], 1)

            def page_at(n):
                pe.wait_ge(R[f"page_in{n % NPB}"], 16 * (n // NPB + 1))
                return page[n % NPB]

            w = NB * H

            def page_scores(n):
                b, k = n // NPG, n % NPG
                pg = page_at(n)
                for h in range(H):
                    c = k * w + b * H + h
                    m = mm(aux[3][:, c:c + 1], pg[:, h, :], pt[:, QA + h, SEQ + b:SEQ + b + 1],
                           start=True, stop=True)
                m.then_inc(R["page_used"], 1)

            def page_values(n):
                b, k = n // NPG, n % NPG
                pg = page_at(NB * NPG + n)
                for h in range(H):
                    c = k * w + b * H + h
                    o = k * w + h * NB + b
                    m = mm(acc[3][:, o:o + 1], pg[:, h, :], temps[0][1][:, c:c + 1], start=True, stop=True)
                m.then_inc(R["page_used"], 1)

            pe.wait_ge(R["rot_done"], 2 * H)
            for t in range(H + 2):
                if t < H:
                    sb_scores(t)
                    page_scores(2 * t)
                if 1 <= t <= H:
                    sb_turn(t - 1)
                    sb_sum(t - 1)
                if t < H:
                    page_scores(2 * t + 1)
                if t >= 2:
                    sb_out(t - 2)

            def ret_scores(h):
                bk = banks[h % 2]
                k, q = pt[:, KR + h, :], pt[:, QR + h, :]
                if h >= 2:
                    pe.wait_ge(R["rt_stc"], h - 1)
                    pe.wait_ge(R["rt_k"], h - 1)
                mm(bk[0][:, 0:256], k[:, 0:P], q[:, 0:SEQ], start=True, stop=True)
                mm(bk[0][:, 256:384], k[:, P:SEQ], q[:, P:SEQ], start=True, stop=True).then_inc(R["rt_s"], 1)
                for c in range(2):
                    turn(bk[1][:, c * P:c * P + P], k[:, c * P:c * P + P])
                    for u in range(2):
                        m = turn(bk[2][:, c * 256 + u * P:c * 256 + u * P + P], pt[:, VR + 2 * h + u, c * P:c * P + P])
                m.then_inc(R["rt_t"], 1)

            def ret_out(h):
                bk, w, v, k = banks[h % 2], temps[h % 2][2], vtok[h % 2], ktw[h % 2]
                pe.wait_ge(R["rt_p"], h + 1)
                pe.wait_ge(R["rt_k"], h + 1)
                if h >= 1:
                    pe.wait_ge(R["rt_yc"], h)
                for u in range(2):
                    o = u * 256
                    mm(aux[3][:, o:o + 256], v[:, 0, u * P:u * P + P], w[:, 0:SEQ], start=True, stop=False)
                    m = mm(aux[3][:, o + P:o + 256], v[:, 1, u * P:u * P + P], w[:, 256:384], start=False, stop=True)
                m.then_inc(R["rt_y"], 1)
                mm(bk[0][:, 0:256], k[:, 0, :], v[:, 0, :], start=True, stop=False)
                mm(bk[0][:, 0:256], k[:, 1, :], v[:, 1, :], start=False, stop=True).then_inc(R["rt_st"], 1)

            pe.wait_ge(R["sb_ycopy"], H)
            ret_scores(0)
            lf = temps[0][2]
            pe.wait_ge(R["sb_lf"], H + 1)
            sums = acc[1][:, 0:2 * w]
            mm(sums, upper, lf[:, 0:2 * w], start=True, stop=False)
            mm(sums[:, 0:w], ones, lf[:, w:2 * w], start=False, stop=True).then_inc(R["sb_incl"], 1)
            pe.wait_ge(R["sb_arg"], H + 1)
            for t in range(1, H + 1):
                if t < H:
                    ret_scores(t)
                if t == 1:
                    pe.wait_ge(R["sb_w"], H + 1)
                page_values(2 * t - 2)
                ret_out(t - 1)
                page_values(2 * t - 1)
            pe.wait_ge(R["rt_yc"], H)
            pe.wait_ge(R["rt_stc"], H)
            pe.wait_ge(R["sb_ycopy"], H + 1)
            for h in range(H):
                turn(aux[h // 4][0:NB, (h % 4) * P:(h % 4) * P + P], pt[:, KR + h, SEQ:T])
            for t in range(2 * H):
                m = turn(acc[t // 4][0:NB, (t % 4) * P:(t % 4) * P + P], pt[:, VR + t, SEQ:T])
            m.then_inc(R["rs_t"], 1)

            def ret_outer(u):
                b = u // 2
                pe.wait_ge(R["rs_km"], b + 1)
                for k in range(4):
                    h = 4 * (u % 2) + k
                    if u >= 2 and k % 2 == 0:
                        pe.wait_ge(R["rs_new"], 4 * (u - 2) + k + 2)
                    m = mm(obank(h), ktm[b % 2][0:NB, h * P:h * P + P], vts[0:NB, h * 256:h * 256 + 256],
                           start=True, stop=True)
                    if k % 2:
                        m.then_inc(R["rs_o"], 1)

            def ret_read(u):
                b = u // 2
                pe.wait_ge(R["rs_new"], 4 * (u + 1))
                for k in range(4):
                    h = 4 * (u % 2) + k
                    for e in range(2):
                        c = (2 * h + e) * NB + b
                        m = mm(aux[2][:, c:c + 1], s0buf[u % NRB][:, k, e * P:e * P + P],
                               pt[:, QR + h, SEQ + b:SEQ + b + 1], start=True, stop=True)
                m.then_inc(R["rs_y"], 1)

            pe.wait_ge(R["sb_ycopy"], H + 1)
            ret_outer(0)
            for u in range(2 * NB):
                if u + 1 < 2 * NB:
                    ret_outer(u + 1)
                ret_read(u)
            for h in range(H):
                pe.wait_ge(R["rn_sq"], h + 1)
                for u in range(2):
                    m = mm(aux[0][0:H, 0:T], pick[:, 7 - h:15 - h], rsq[:, h % 2, u, :],
                           start=h == 0 and u == 0, stop=h == H - 1 and u == 1)
                m.then_inc(R["rn_sum"], 1)
            pe.wait_ge(R["rn_inv"], 1)
            for h in range(H):
                if h >= 4:
                    pe.wait_ge(R["rn_a"], h - 3)
                mm(acc[h % 4][:, 0:T], row_of(h, H), rinv[0:H, :], start=True, stop=True).then_inc(R["rn_bc"], 1)

            def norm(l):
                pe.wait_ge(R["ln_sum"], 17 * (l + 1))
                mm(aux[0][:, 0:T], ones, lsum[:, :], start=True, stop=True).then_inc(R["ln_mean"], 1)
                for t in range(KT):
                    if t % CK == 0:
                        pe.wait_ge(R["ln_sq"], XB * l + t // CK + 1)
                    m = mm(aux[1][:, 0:T], ones, lsq[:, t, :], start=t == 0, stop=t == KT - 1)
                m.then_inc(R["ln_var"], 1)

            products(pe, PHASES["out_ab"])
            norm(0)
            products(pe, PHASES["up0"], 1)
            products(pe, PHASES["down0"])
            norm(1)

            dt = PHASES["dt"]
            pe.wait_ge(lo_done, dt.chunk0 + 1)
            pe.wait_ge(drained, dt.panel0 * 4 + 1)
            for k in range(KT):
                if k % CK == 0:
                    pe.wait_ge(R["x_lo"], XB * 2 + k // CK + 1)
                w = slice(k * P, k * P + P)
                s, r = hi_slot(0, 1), raw_slot(0, 1)
                mm(acc[0][:, 0:T], hi[:, s, w], xh[:, k, :], start=k == 0, stop=False)
                mm(acc[0][:, 0:T], hi[:, s, w], xl[:, k, :], start=False, stop=False)
                m = mm(acc[0][:, 0:T], lo[:, r, w], xh[:, k, :], start=False, stop=k == KT - 1)
            m.then_inc(used, 1)
            products(pe, PHASES["ssd"])

            pe.wait_ge(R["dt_c"], 5)
            for c in range(2):
                s = slice(c * P, c * P + P)
                for k, v in enumerate((cumT, dtT, wendT)):
                    turn(aux[0][:, (2 * k + c) * NH:(2 * k + c) * NH + NH], v[0:NH, s])
            turn(aux[1][0:NB, 0:NH], dtT[0:NH, SEQ:T])
            turn(aux[1][0:NB, NH:2 * NH], cdT[0:NH, :]).then_inc(R["sm_t"], 1)
            pe.wait_ge(R["dt_c"], 7)
            for b in range(NB):
                m = mm(aux[2][:, b * NH:b * NH + NH], row_of(b, NB), cds[0:NB, :], start=True, stop=True)
            m.then_inc(R["cd_p"], 1)
            for q in range(G):
                if q >= 4:
                    pe.wait_ge(R["ss_x"], q - 3)
                for t in range(4):
                    m = turn(acc[q % 4][0:NB, t * P:t * P + P], pt[:, XS + 4 * q + t, SEQ:T])
                m.then_inc(R["ss_t"], 1)
            pe.wait_ge(R["ss_xl"], G)
            pe.wait_ge(R["sel_r"], 1)

            def spread(n):
                b, g = n // G, n % G
                if n >= 4:
                    pe.wait_ge(R["ss_n"], n - 3)
                mm(acc[g % 4][:, :], by_sample[0:40, b:b + 1].to_broadcast([40, P]),
                   xdr[0:40, g * 512:g * 512 + 512], start=True, stop=True)\
                    .then_inc(R["ss_o"], 1)

            def read_state(n):
                b, g = n // G, n % G
                u = 2 * b + g // 4
                pe.wait_ge(R["ss_n"], n + 1)
                for t in range(4):
                    c = (4 * g + t) * NB + b
                    o = (g % 4) * 512 + t * P
                    m = mm(aux[3][:, c:c + 1], hbuf[u % NHB][:, o:o + P], pt[:, CM + g, SEQ + b:SEQ + b + 1],
                           start=True, stop=True)
                if g % 4 == 3:
                    m.then_inc(R["ss_y"], 1)

            for n in range(NB * G + 3):
                if n < NB * G:
                    spread(n)
                if n >= 3:
                    read_state(n - 3)

            pe.wait_ge(R["ss_ya"], 1)
            pe.wait_ge(R["cum_lo"], 1)

            def group_cb(g):
                bm, cm = pt[:, BM + g, :], pt[:, CM + g, :]
                if g == 1:
                    pe.wait_ge(R["g_cbm"], 1)
                if g >= 2:
                    pe.wait_ge(R["g_stc"], g - 1)
                mm(aux[0][:, 0:256], bm[:, 0:P], cm[:, 0:SEQ], start=True, stop=True)
                mm(aux[0][:, 256:384], bm[:, P:SEQ], cm[:, P:SEQ], start=True, stop=True).then_inc(R["g_cb"], 1)

            def group_b(g):
                if g >= 1:
                    pe.wait_ge(R["g_x"], 2 * g)
                for c in range(2):
                    m = turn(acc[0][:, c * P:c * P + P], pt[:, BM + g, c * P:c * P + P])
                m.then_inc(R["g_bt"], 1)

            def group_x(g, c):
                pe.wait_ge(R["g_btc"], g + 1)
                if c:
                    pe.wait_ge(R["g_x"], 2 * g + 1)
                for t in range(4):
                    m = turn(acc[0][:, t * P:t * P + P], pt[:, XS + 4 * g + t, c * P:c * P + P])
                m.then_inc(R["g_xt"], 1)

            def decays(n):
                bk, s = acc[1 + n % 3], by_head[:, n:n + 1].to_broadcast([P, P])
                if n >= 3:
                    pe.wait_ge(R["g_e"], n - 2)
                mm(bk[:, 0:256], s, cumr[:, :], start=True, stop=False)
                mm(bk[:, 0:P], identr, block_cap, start=False, stop=True)
                mm(bk[:, 256:384], s, cumr[:, P:SEQ], start=True, stop=False)
                mm(bk[:, 256:384], identr, block_cap, start=False, stop=True).then_inc(R["g_bc"], 1)

            def head_out(n):
                g, p, k = n // 8, n // 2, n % 2
                if p >= 2 and k == 0:
                    pe.wait_ge(R["g_yd"], p - 1)
                if n % 8 == 0:
                    pe.wait_ge(R["g_x"], 2 * g + 2)
                pe.wait_ge(R["g_w"], n + 1)
                o, w = (n % 8) * HD, wsb[n % NW]
                y = aux[2 + p % 2][k * HD:k * HD + HD, :]
                mm(y[:, 0:SEQ], xdt[g % 2][:, 0, o:o + HD], w[:, 0:SEQ], start=True, stop=False)
                mm(y[:, P:SEQ], xdt[g % 2][:, 1, o:o + HD], w[:, 256:384], start=False, stop=True)\
                    .then_inc(R["g_yh"], 1)

            def group_state(g):
                pe.wait_ge(R["g_cbm"], min(g + 2, G))
                for t in range(4):
                    o = slice(t * P, t * P + P)
                    mm(aux[0][:, o], xw[g % 2][:, 0, o], btok[g % 2][:, 0, :], start=True, stop=False)
                    m = mm(aux[0][:, o], xw[g % 2][:, 1, o], btok[g % 2][:, 1, :], start=False, stop=True)
                m.then_inc(R["g_st"], 1)

            def group_sum(g):
                pe.wait_ge(R["g_sq"], g + 1)
                for t in range(4):
                    m = mm(aux[1][0:G, 0:T], pick[:, 7 - g:15 - g], gsq[:, t, :],
                           start=g == 0 and t == 0, stop=g == G - 1 and t == 3)
                m.then_inc(R["g_ss"], 1)

            group_b(0)
            group_cb(0)
            group_x(0, 0)
            group_x(0, 1)
            for n in range(3):
                decays(n)
            for g in range(G):
                for k in range(8):
                    n = 8 * g + k
                    if n + 3 < NH:
                        decays(n + 3)
                    head_out(n)
                    if k == 1 and g >= 1:
                        group_state(g - 1)
                    if k == 2 and g + 1 < G:
                        group_b(g + 1)
                        group_cb(g + 1)
                    if k == 3 and g >= 1:
                        group_sum(g - 1)
                    if k == 3 and g + 1 < G:
                        group_x(g + 1, 0)
                    if k == 5 and g + 1 < G:
                        group_x(g + 1, 1)
            pe.wait_ge(R["g_stc"], G - 1)
            group_state(G - 1)
            group_sum(G - 1)
            pe.wait_ge(R["g_inv"], 1)
            for g in range(G):
                if g >= 4:
                    pe.wait_ge(R["g_n"], 4 * (g - 3))
                mm(acc[g % 4][:, 0:T], row_of(g, G), ginv[0:G, :], start=True, stop=True).then_inc(R["g_rb"], 1)

            products(pe, PHASES["out_ssd"])
            norm(2)
            products(pe, PHASES["up1"], 3)
            products(pe, PHASES["down1"])
            norm(3)





def feature_major(a, axis=-1):
    a = np.moveaxis(np.asarray(a), axis, 0)
    return np.ascontiguousarray(np.moveaxis(a.reshape((-1, P) + a.shape[1:]), 1, 0))


def chunks(w, panels_of, kc):
    k, n = w.shape
    v = w.reshape(k // (CK * P), CK, P, n // (CN * P), CN * P)
    return v.transpose(3, 0, 2, 1, 4).reshape(-1, P, CW)


def kernel(**inputs):
    import concourse.bacc as bacc
    from concourse.bass_utils import run_bass_kernel_spmd

    g = {k: np.asarray(v) for k, v in inputs.items()}
    f32 = np.float32

    xp = np.concatenate([g["x_prompt"][0], g["x_sample"][:, 0]], 0)
    w_ab = g["w_in_ab"][0]
    cut = [0, 1024, 2048, 3072, 4096, 5120, 7168, 9216]
    qa, ka, va, qr, kr, vr, gr = (w_ab[:, a:b] for a, b in zip(cut, cut[1:]))
    w_ab = np.concatenate([qa, vr, ka, va, qr, kr, gr], 1)
    w_ssd = g["w_in_ssd"][0]
    w_z, w_xs, w_b, w_c, w_dt = (w_ssd[:, a:b] for a, b in ((0, 4096), (4096, 8192), (8192, 9216),
                                                            (9216, 10240), (10240, 10304)))
    dt_w = np.zeros((D, P), f32)
    dt_w[:, 0:NH] = w_dt
    pairs = np.arange(2 * FT).reshape(2, FT // 2, 2).transpose(1, 0, 2).reshape(-1)

    def by_pairs(a):
        v = a.reshape(a.shape[:-1] + (2 * FT, P))
        return v[..., pairs, :].reshape(a.shape)

    w = [chunks(w_ab, 18, 4), chunks(g["w_out_ab"][0], 4, 6)]
    for layer in range(DEPTH):
        if layer:
            w += [dt_w.reshape(KT, P, P).transpose(1, 0, 2).reshape(1, P, CW),
                  chunks(np.concatenate([w_b, w_c, w_xs, w_z], 1), 20, 4), chunks(g["w_out_ssd"][0], 4, 8)]
        w += [chunks(by_pairs(g["w_up"][layer]), 22, 4), chunks(g["w_down"][layer], 4, 11)]
    w = np.concatenate(w, 0)

    param = np.zeros((P, PARAM_W), f32)

    def put(name, a, rows=P):
        param[0:rows, PARAM[name][0]:PARAM[name][1]] = a.reshape(rows, -1)

    ln_g = np.stack([g["ln1_g"][0], g["ln2_g"][0], g["ln1_g"][1], g["ln2_g"][1]])
    ln_b = np.stack([g["ln1_b"][0], g["ln2_b"][0], g["ln1_b"][1], g["ln2_b"][1]])
    put("lng", ln_g.reshape(4, KT, P).transpose(2, 0, 1))
    put("lnb", ln_b.reshape(4, KT, P).transpose(2, 0, 1))
    put("sbias", np.broadcast_to(g["sb_bias"][0][None], (P, H)))
    put("fcw", by_pairs(g["conv_w_ffn"]).reshape(DEPTH, 3, 2 * FT, P).transpose(3, 0, 1, 2))
    put("fcb", by_pairs(g["conv_b_ffn"]).reshape(DEPTH, 2 * FT, P).transpose(2, 0, 1))

    def bcx(a):
        return np.concatenate([a[..., SSM_IN:], a[..., :SSM_IN]], -1)

    put("scw", bcx(g["conv_w_ssd"][0]).reshape(4, CT, P).transpose(2, 0, 1))
    put("scb", bcx(g["conv_b_ssd"][0]).reshape(CT, P).T)
    put("dskip", np.repeat(g["d_skip"][0], HD).reshape(XST, P).T)
    put("normw", g["norm_w_ssd"][0].reshape(XST, P).T)
    put("dtb", g["dt_bias"][0], NH)
    put("alog", g["a_log"][0], NH)

    arrays = {
        "x": xp.T.reshape(KT, P, T).transpose(1, 0, 2).reshape(P, KT * T),
        "w": w, "const": constants(), "param": param,
        "pages": g["page_table"].reshape(1, -1),
        "ck": g["cache_k"][0].transpose(0, 3, 2, 1),
        "cv": g["cache_v"][0],
        "ret0": g["state_ret"][0].transpose(0, 2, 1, 3).reshape(NB, P, H * 256),
        "ssm0": g["state_ssm"][0].transpose(0, 3, 1, 2).reshape(NB, P, SSM_IN),
        "sst": bcx(g["state_ssm_conv"][0]).reshape(NB, 3, CT, P).transpose(3, 2, 1, 0),
        "fst": by_pairs(g["state_ffn_conv"]).reshape(DEPTH, NB, 2, 2 * FT, P).transpose(0, 4, 3, 2, 1),
    }
    arrays = {k: np.ascontiguousarray(v) for k, v in arrays.items()}

    nc = bacc.Bacc("TRN2", target_bir_lowering=False, num_devices=1)
    d = {k: nc.dram_tensor(f"in_{k}", v.shape, mybir.dt.from_np(v.dtype), kind="ExternalInput").ap()
         for k, v in arrays.items()}
    for k, shape in OUT_SHAPES.items():
        d[k] = nc.dram_tensor(f"out_{k}", shape, F32, kind="ExternalOutput").ap()
    d["gate"] = nc.dram_tensor("gate", (P, XST, T), F32, kind="Internal").ap()
    d["xsave"] = nc.dram_tensor("xsave", (P, KT * T), F32, kind="Internal").ap()
    d["y"] = d["y"].rearrange("p t n -> p (t n)")
    build(nc, d)
    r = run_bass_kernel_spmd(nc, [{f"in_{k}": v for k, v in arrays.items()}], core_ids=[0]).results[0]
    o = {k: r[f"out_{k}"].reshape(s) for k, s in OUT_SHAPES.items()}

    def tokens(a):
        return a.transpose(2, 1, 0).reshape(a.shape[2], -1)

    y = tokens(o["y"])
    k, v = tokens(o["kv"][:, 0:H]), tokens(o["kv"][:, H:])
    back = np.argsort(pairs)

    def channels(a, undo):
        return np.moveaxis(a[:, undo], (1, 0), (-2, -1)).reshape(a.shape[2:] + (-1,))

    xbc = np.concatenate([np.arange(2 * G, CT), np.arange(2 * G)])
    sc, so = channels(o["sconv"], xbc), channels(o["sconv_old"], xbc)
    fc = np.stack([channels(o["fconv"][l], back) for l in range(DEPTH)])
    fo = np.stack([channels(o["fconv_old"][l], back) for l in range(DEPTH)])
    out = (
        y[None, 0:SEQ], y[SEQ:, None],
        k[None, None, 0:SEQ].reshape(1, 1, SEQ, H, P), v[0:SEQ].reshape(1, 1, SEQ, H, P),
        k[SEQ:].reshape(1, NB, 1, H, P), v[SEQ:].reshape(1, NB, 1, H, P),
        o["retp"].transpose(1, 0, 2)[None, None],
        o["rets"].reshape(NB, P, H, 256).transpose(0, 2, 1, 3)[None],
        o["ssmp"].transpose(1, 0, 2).reshape(1, 1, NH, HD, P),
        o["ssms"].reshape(NB, P, NH, HD).transpose(0, 2, 3, 1)[None],
        sc[None, None, 0:3],
        np.stack([so[0], so[1], sc[3:]], 1)[None],
        fc[:, None, 0:2],
        np.stack([fo, fc[:, 2:]], 2),
    )
    return tuple(np.ascontiguousarray(a) for a in out)
```
